# Optimizing a Trainium2 kernel written in Bass

```python
import math
import jax
import jax.numpy as jnp
from jax import lax
import numpy as np

D_MODEL = 1024
BATCH = 1
SEQ = 512
DEPTH = 1

GRID_W = 64
CTX_LEN = 256
N_MOD = 6
NORM_EPS = 1e-6
FOURIER_GROUPS = 4
FOURIER_GROUP_DIM = 64
FOURIER_WIDTH = FOURIER_GROUPS * FOURIER_GROUP_DIM
DIFF_HEADS = 6
DIFF_HEAD_DIM = 64
DIFF_VALUE_DIM = 2 * DIFF_HEAD_DIM
DIFF_QK_WIDTH = DIFF_HEADS * 2 * DIFF_HEAD_DIM
DIFF_V_WIDTH = DIFF_HEADS * DIFF_VALUE_DIM
IN_WIDTH = FOURIER_WIDTH + 2 * DIFF_QK_WIDTH + DIFF_V_WIDTH
MIX_WIDTH = FOURIER_WIDTH + DIFF_V_WIDTH
QUERY_BLOCK = 128
ROPE_BASE = 10000.0
ROPE_AXIS_DIM = DIFF_HEAD_DIM // 2
N_EXPERTS = 64
TOP_K = 8
N_EXPERT_GROUPS = 8
TOP_K_GROUPS = 4
D_EXPERT = 256
ROUTED_SCALE = 2.5
EXPERT_BLOCK = 128

kernel_name = "hybrid_fourier_diffattn_moe_dit"

def rms_norm(x, g):
    xf = x.astype(jnp.float32)
    y = xf * lax.rsqrt(jnp.mean(xf * xf, axis=-1, keepdims=True) + NORM_EPS)
    return (y * g.astype(jnp.float32)).astype(x.dtype)

def modulate(h, shift, scale):
    return h * (1 + scale) + shift

def ada_params(cond, w_mod, b_mod):
    m = jax.nn.silu(cond) @ w_mod + b_mod
    return m.reshape(cond.shape[:-1] + (N_MOD, D_MODEL))

def axial_rope_tables(n_tokens):
    rows = n_tokens // GRID_W
    row = jnp.broadcast_to(jnp.arange(rows)[:, None], (rows, GRID_W)).reshape(-1)
    col = jnp.broadcast_to(jnp.arange(GRID_W)[None, :], (rows, GRID_W)).reshape(-1)
    inv_freq = ROPE_BASE ** (-jnp.arange(0, ROPE_AXIS_DIM, 2, dtype=jnp.float32) / ROPE_AXIS_DIM)
    pos = jnp.stack([row, col], axis=-1).astype(jnp.float32)
    ang = pos[:, :, None] * inv_freq
    return jnp.cos(ang), jnp.sin(ang)

def apply_axial_rope(t, cos, sin):
    xf = t.astype(jnp.float32).reshape(t.shape[:-1] + (2, 2, ROPE_AXIS_DIM // 2))
    x1 = xf[..., 0, :]
    x2 = xf[..., 1, :]
    cb = cos[None, :, None, None]
    sb = sin[None, :, None, None]
    out = jnp.stack([x1 * cb - x2 * sb, x2 * cb + x1 * sb], axis=-2)
    return out.reshape(t.shape).astype(t.dtype)

def split_groups(p):
    b, n, _ = p.shape
    o1 = FOURIER_WIDTH
    o2 = o1 + DIFF_QK_WIDTH
    o3 = o2 + DIFF_QK_WIDTH
    f = p[..., :o1]
    q = p[..., o1:o2].reshape(b, n, DIFF_HEADS, 2, DIFF_HEAD_DIM)
    k = p[..., o2:o3].reshape(b, n, DIFF_HEADS, 2, DIFF_HEAD_DIM)
    v = p[..., o3:].reshape(b, n, DIFF_HEADS, DIFF_VALUE_DIM)
    return f, q, k, v

def fourier_mix(f, w_fourier):
    b, n, _ = f.shape
    fg = f.astype(jnp.float32).reshape(b, n, FOURIER_GROUPS, FOURIER_GROUP_DIM)
    spec = jnp.fft.fft2(fg, axes=(1, 3), norm="ortho").real.astype(f.dtype)
    out = jnp.einsum("bngc,gcd->bngd", spec, w_fourier)
    return out.reshape(b, n, FOURIER_WIDTH)

def diff_attn_block(q, k, v, lam):
    s = jnp.einsum("bqhmd,bkhmd->bhmqk", q, k).astype(jnp.float32) * (DIFF_HEAD_DIM ** -0.5)
    p = jax.nn.softmax(s, axis=-1)
    a = p[:, :, 0] - lam * p[:, :, 1]
    return jnp.einsum("bhqk,bkhe->bqhe", a.astype(v.dtype), v)

def latent_diff_attention(qx, kx, vx, kc, vc, lam):
    b, n = qx.shape[:2]
    n_blocks = n // QUERY_BLOCK
    k_all = jnp.concatenate([kc, kx], axis=1)
    v_all = jnp.concatenate([vc, vx], axis=1)
    qb = qx.reshape(b, n_blocks, QUERY_BLOCK, DIFF_HEADS, 2, DIFF_HEAD_DIM).transpose(1, 0, 2, 3, 4, 5)
    o = lax.map(lambda q_blk: diff_attn_block(q_blk, k_all, v_all, lam), qb)
    return o.transpose(1, 0, 2, 3, 4).reshape(b, n, DIFF_HEADS, DIFF_VALUE_DIM)

def diff_subln(o, g, lam_init):
    b, n = o.shape[:2]
    return (rms_norm(o, g) * (1.0 - lam_init)).reshape(b, n, DIFF_V_WIDTH)

def swiglu(h, w_gate, w_up, w_down):
    return (jax.nn.silu(h @ w_gate) * (h @ w_up)) @ w_down

def moe_ffn(h, w_router, router_bias, w_gate, w_up, w_down, ws_gate, ws_up, ws_down):
    b, n, d = h.shape
    ht = h.reshape(b * n, d)
    n_tok = b * n
    scores = jax.nn.sigmoid((ht @ w_router).astype(jnp.float32))
    sel = scores + router_bias.astype(jnp.float32)
    grouped = sel.reshape(n_tok, N_EXPERT_GROUPS, N_EXPERTS // N_EXPERT_GROUPS)
    group_score = lax.top_k(grouped, 2)[0].sum(-1)
    gidx = lax.top_k(group_score, TOP_K_GROUPS)[1]
    group_mask = jnp.any(gidx[..., None] == jnp.arange(N_EXPERT_GROUPS), axis=-2)
    expert_mask = jnp.repeat(group_mask, N_EXPERTS // N_EXPERT_GROUPS, axis=-1)
    _, idx = lax.top_k(jnp.where(expert_mask, sel, -jnp.inf), TOP_K)
    wts = jnp.take_along_axis(scores, idx, axis=-1)
    wts = wts / (wts.sum(-1, keepdims=True) + 1e-20) * ROUTED_SCALE
    n_assign = n_tok * TOP_K
    n_blocks = -(-n_assign // EXPERT_BLOCK) + N_EXPERTS
    n_slots = n_blocks * EXPERT_BLOCK
    flat_e = idx.reshape(-1)
    flat_w = wts.reshape(-1).astype(h.dtype)
    flat_tok = jnp.arange(n_assign, dtype=jnp.int32) // TOP_K
    order = jnp.argsort(flat_e)
    e_sorted = flat_e[order]
    counts = jnp.zeros((N_EXPERTS,), jnp.int32).at[flat_e].add(1)
    start = jnp.cumsum(counts) - counts
    padded = (counts + EXPERT_BLOCK - 1) // EXPERT_BLOCK * EXPERT_BLOCK
    pad_end = jnp.cumsum(padded)
    pad_start = pad_end - padded
    dest = pad_start[e_sorted] + (jnp.arange(n_assign, dtype=jnp.int32) - start[e_sorted])
    slot_tok = jnp.full((n_slots,), n_tok, jnp.int32).at[dest].set(flat_tok[order])
    slot_w = jnp.zeros((n_slots,), h.dtype).at[dest].set(flat_w[order])
    block_expert = jnp.minimum(
        jnp.searchsorted(pad_end, jnp.arange(n_blocks, dtype=jnp.int32) * EXPERT_BLOCK, side="right"),
        N_EXPERTS - 1)
    h_pad = jnp.concatenate([ht, jnp.zeros((1, d), h.dtype)], axis=0)

    def expert_block(args):
        tok, w, e = args
        xb = h_pad[tok]
        return swiglu(xb, w_gate[e], w_up[e], w_down[e]) * w[:, None]

    y = lax.map(expert_block, (slot_tok.reshape(n_blocks, EXPERT_BLOCK),
                               slot_w.reshape(n_blocks, EXPERT_BLOCK), block_expert))
    routed = jnp.zeros((n_tok + 1, d), h.dtype).at[slot_tok].add(y.reshape(n_slots, d))[:n_tok]
    shared = swiglu(ht, ws_gate, ws_up, ws_down)
    return (routed + shared).reshape(b, n, d)

def setup_inputs(seed: int = 0) -> dict:
    key = jax.random.key(seed)
    ks = jax.random.split(key, 26)

    def nrm(k, shape, scale):
        return jax.random.normal(k, shape, jnp.float32) * scale

    def gain(k, shape):
        return 1.0 + 0.1 * jax.random.normal(k, shape, jnp.float32)

    d = D_MODEL
    return {
        "x": nrm(ks[0], (BATCH, SEQ, d), 1.0),
        "c": nrm(ks[1], (BATCH, d), 1.0),
        "ctx": nrm(ks[2], (BATCH, CTX_LEN, d), 1.0),
        "c_ctx": nrm(ks[3], (d,), 1.0),
        "w_mod": nrm(ks[4], (DEPTH, d, N_MOD * d), d ** -0.5),
        "b_mod": nrm(ks[5], (DEPTH, N_MOD * d), 0.02),
        "g_attn_pre": gain(ks[6], (DEPTH, d)),
        "g_attn_post": gain(ks[7], (DEPTH, d)),
        "w_in": nrm(ks[8], (DEPTH, d, IN_WIDTH), d ** -0.5),
        "w_fourier": nrm(ks[9], (DEPTH, FOURIER_GROUPS, FOURIER_GROUP_DIM, FOURIER_GROUP_DIM), FOURIER_GROUP_DIM ** -0.5),
        "lambda_q1": nrm(ks[10], (DEPTH, DIFF_HEAD_DIM), 0.1),
        "lambda_k1": nrm(ks[11], (DEPTH, DIFF_HEAD_DIM), 0.1),
        "lambda_q2": nrm(ks[12], (DEPTH, DIFF_HEAD_DIM), 0.1),
        "lambda_k2": nrm(ks[13], (DEPTH, DIFF_HEAD_DIM), 0.1),
        "g_subln": gain(ks[14], (DEPTH, DIFF_VALUE_DIM)),
        "w_out": nrm(ks[15], (DEPTH, MIX_WIDTH, d), MIX_WIDTH ** -0.5),
        "g_ffn_pre": gain(ks[16], (DEPTH, d)),
        "g_ffn_post": gain(ks[17], (DEPTH, d)),
        "w_router": nrm(ks[18], (DEPTH, d, N_EXPERTS), d ** -0.5),
        "router_bias": nrm(ks[19], (DEPTH, N_EXPERTS), 0.01),
        "w_gate": nrm(ks[20], (DEPTH, N_EXPERTS, d, D_EXPERT), d ** -0.5),
        "w_up": nrm(ks[21], (DEPTH, N_EXPERTS, d, D_EXPERT), d ** -0.5),
        "w_down": nrm(ks[22], (DEPTH, N_EXPERTS, D_EXPERT, d), D_EXPERT ** -0.5),
        "ws_gate": nrm(ks[23], (DEPTH, d, D_EXPERT), d ** -0.5),
        "ws_up": nrm(ks[24], (DEPTH, d, D_EXPERT), d ** -0.5),
        "ws_down": nrm(ks[25], (DEPTH, D_EXPERT, d), D_EXPERT ** -0.5),
    }

def reference(x, c, ctx, c_ctx, w_mod, b_mod, g_attn_pre, g_attn_post, w_in, w_fourier,
              lambda_q1, lambda_k1, lambda_q2, lambda_k2, g_subln, w_out, g_ffn_pre, g_ffn_post,
              w_router, router_bias, w_gate, w_up, w_down, ws_gate, ws_up, ws_down):
    n_lat = x.shape[1]
    cos, sin = axial_rope_tables(n_lat)
    for l in range(DEPTH):
        last = l == DEPTH - 1
        lam_init = 0.8 - 0.6 * math.exp(-0.3 * l)
        lam = (jnp.exp(jnp.sum(lambda_q1[l].astype(jnp.float32) * lambda_k1[l].astype(jnp.float32)))
               - jnp.exp(jnp.sum(lambda_q2[l].astype(jnp.float32) * lambda_k2[l].astype(jnp.float32)))
               + lam_init)
        mx = ada_params(c, w_mod[l], b_mod[l])[:, None]
        mc = ada_params(c_ctx, w_mod[l], b_mod[l])

        hx = modulate(rms_norm(x, g_attn_pre[l]), mx[..., 0, :], mx[..., 1, :])
        hc = modulate(rms_norm(ctx, g_attn_pre[l]), mc[..., 0, :], mc[..., 1, :])
        fx, qx, kx, vx = split_groups(hx @ w_in[l])
        fc, qc, kc, vc = split_groups(hc @ w_in[l])
        qx = apply_axial_rope(qx, cos, sin)
        kx = apply_axial_rope(kx, cos, sin)
        ox = latent_diff_attention(qx, kx, vx, kc, vc, lam)
        yx = jnp.concatenate([fourier_mix(fx, w_fourier[l]), diff_subln(ox, g_subln[l], lam_init)], axis=-1) @ w_out[l]
        x = x + mx[..., 2, :] * rms_norm(yx, g_attn_post[l])
        if not last:
            oc = diff_attn_block(qc, kc, vc, lam)
            yc = jnp.concatenate([fourier_mix(fc, w_fourier[l]), diff_subln(oc, g_subln[l], lam_init)], axis=-1) @ w_out[l]
            ctx = ctx + mc[..., 2, :] * rms_norm(yc, g_attn_post[l])

        moe_args = (w_router[l], router_bias[l], w_gate[l], w_up[l], w_down[l], ws_gate[l], ws_up[l], ws_down[l])
        hx = modulate(rms_norm(x, g_ffn_pre[l]), mx[..., 3, :], mx[..., 4, :])
        x = x + mx[..., 5, :] * rms_norm(moe_ffn(hx, *moe_args), g_ffn_post[l])
        if not last:
            hc = modulate(rms_norm(ctx, g_ffn_pre[l]), mc[..., 3, :], mc[..., 4, :])
            ctx = ctx + mc[..., 5, :] * rms_norm(moe_ffn(hc, *moe_args), g_ffn_post[l])
    return x


_drawn_inputs = setup_inputs


def setup_inputs(seed=0):
    import zlib

    import numpy as np

    out = dict(_drawn_inputs(seed))
    spreads = {}
    factors = {}
    for name, (base, spread) in spreads.items():
        noise = np.random.default_rng([zlib.crc32(name.encode()), seed]).standard_normal(out[name].shape)
        drawn = base * np.exp(spread * noise) if base else spread * noise
        out[name] = jnp.asarray(drawn.astype(out[name].dtype))
    for name, factor in factors.items():
        out[name] = (out[name] * factor).astype(out[name].dtype)
    return out
```

```python
import math
from contextlib import ExitStack

import concourse.bass as bass
from concourse import mybir

F32 = mybir.dt.float32
I32 = mybir.dt.int32
U32 = mybir.dt.uint32
ALU = mybir.AluOpType
ACT = mybir.ActivationFunctionType
AX = mybir.AxisListType.X

P = 128
D = 1024
KC = D // P
NLAT, NCTX = 512, 256
NT = NLAT // P
NCT = NCTX // P
NTOK = NLAT + NCTX
FW = 256
HEADS, HD = 6, 64
VD = 2 * HD
QKW = HEADS * VD
NE, TOPK, NGRP, TOPG = 64, 8, 8, 4
GE = NE // NGRP
DE = 256
MIXC = (FW + QKW) // P
EPS = 1e-6
LAM0 = 0.8 - 0.6 * math.exp(-0.3 * 0)
ROUTED_SCALE = 2.5
UNITS = HEADS * NT
U = 4
MAXOV = NLAT * TOPK // P
TURNS = (NE + MAXOV) // U
NB = NE + MAXOV + U
SKIP = 100000.0
GU_W = KC * DE
WBUF = 3 * GU_W
FRONT = 8 * 512
NFRONT = 5

C_ID, C_TRI, C_IOTA, C_LT, C_V, C_CC, C_SC = 0, 128, 256, 384, 448, 480, 608
C_MAP = 736
C_ALL = 738


def at(index, size):
    return slice(index, index + size) if isinstance(index, int) else bass.ds(index, size)


def need(eng, sem, value):
    if not (isinstance(value, int) and value <= 0):
        eng.wait_ge(sem, value)


def build(nc, A):
    ctx = ExitStack()
    sb = lambda name, shape, dt=F32: ctx.enter_context(nc.sbuf_tensor(name, shape, dt))
    sem = lambda name: ctx.enter_context(nc.semaphore(name))
    with ctx:
        xres = sb("xres", [P, NT, D])
        ring = sb("ring", [P, NFRONT * FRONT])
        hreg = sb("hreg", [P, KC * NTOK])
        qreg = sb("qreg", [P, 12288])
        sreg = sb("sreg", [P, 3072])
        freg = sb("freg", [P, 2560])
        grow = sb("grow", [P, 2, D])
        const = sb("const", [P, C_ALL])
        ones = sb("ones", [P, P])
        stat = sb("stat", [P, 4, 16])
        colc = sb("colc", [P, 2, KC])
        silc = sb("silc", [P, KC, 2])
        bmod = sb("bmod", [P, 6, KC])
        gain = sb("gain", [P, 4, KC])
        modc = sb("modc", [P, 6, KC, 2])
        scl1 = sb("scl1", [P, KC, 2])
        rowc = sb("rowc", [P, 4, KC])
        lam = sb("lam", [P, 8])
        gsub = sb("gsub", [P, 2])
        nrm = sb("nrm", [P, 3, 24])
        mhalf = sb("mhalf", [P, 1])
        wrt = sb("wrt", [P, KC, NE])
        rbias = sb("rbias", [P, NE])
        slots = sb("slots", [P, NB, 3], I32)
        ids = sb("ids", [P, U, 3], I32)
        steer = sb("steer", [1, NB + 4], I32)
        ps = ctx.enter_context(nc.psum_tensor("ps", [P, 8, 512], F32))
        psf = ps[:].rearrange("p b n -> p (b n)")
        h2_dram = nc.dram_tensor("h2_rows", [NLAT, D], F32, kind="Internal").ap()
        y_dram = nc.dram_tensor("y_rows", [NLAT * TOPK, D], F32, kind="Internal").ap()

        hT = hreg[:].rearrange("p (c n) -> p c n", c=KC)
        mixT = hreg[:, 0:MIXC * NLAT]
        mixTv = mixT.rearrange("p (c n) -> p c n", c=MIXC)
        fg = hreg[:, 4096:6144].rearrange("p (t j s n) -> p t j s n", t=NT, j=2, s=2)
        hT2 = hreg[:, 0:KC * NLAT].rearrange("p (c n) -> p c n", c=KC)
        xg = hreg[:, 4096:6144].rearrange("p (s n) -> p s n", s=2)
        xn = qreg[:, 0:6144].rearrange("p (t n) -> p t n", t=NCT + NT)
        qT = qreg[:, 0:3072]
        kT = qreg[:, 3072:7680]
        vt = qreg[:, 7680:12288].rearrange("p (t n) -> p t n", t=NCT + NT)
        tmp1 = qreg[:, 0:1024]
        h2 = qreg[:, 1024:3072].rearrange("p (s n) -> p s n", s=2)
        shy = qreg[:, 6144:10240].rearrange("p (t n) -> p t n", t=NT)
        rt = qreg[:, 10240:12288]
        prob = sreg[:].rearrange("p (s m n) -> p s m n", s=2, m=2)
        xctx = sreg[:, 0:2048].rearrange("p (t n) -> p t n", t=NCT)
        ropeA = sreg[:, 0:1024].rearrange("p (s n) -> p s n", s=2)
        ropeB = sreg[:, 1024:2048].rearrange("p (s n) -> p s n", s=2)
        srow = sreg[:, 0:2048].rearrange("p (s n) -> p s n", s=2)
        xgT = sreg[:, 0:2048].rearrange("p (s c n) -> p s c n", s=2, c=KC)
        hmid = sreg[:, 2048:2560].rearrange("p (s n) -> p s n", s=2)
        hmT = sreg[:, 2560:3072].rearrange("p (s c n) -> p s c n", s=2, c=2)
        lamv = sreg[:, 2048:2304].rearrange("p (i d) -> p i d", i=4)
        wbd = sreg[:, 2304:2560].rearrange("p (j n) -> p j n", j=2)
        bd = sreg[:, 2560:3072].rearrange("p (j s n) -> p j s n", j=2, s=2)
        ropet = freg[:, 1024:1536].rearrange("p (t s d) -> p t s d", t=NT, s=2)
        qz = freg[:, 0:512].rearrange("p (s m n) -> p s m n", s=2, m=2)
        onrm = freg[:, 512:768].rearrange("p (s n) -> p s n", s=2)
        junk = freg[:, 768:896]
        FT = freg[:, 0:1024].rearrange("p (j n) -> p j n", j=2)
        aT = freg[:, 1024:2560].rearrange("p (s n) -> p s n", s=2)
        sq = freg[:, 1024:2048]
        yb = freg[:, 0:2048].rearrange("p (s n) -> p s n", s=2)
        gsil = freg[:, 2048:2560].rearrange("p (s n) -> p s n", s=2)

        ident = const[:, C_ID:C_ID + P]
        tri = const[:, C_TRI:C_TRI + P]
        iota = const[:, C_IOTA:C_IOTA + P]

        small_in = sem("small_in")
        wbd_zero, wbd_in = sem("wbd_zero"), sem("wbd_in")
        x_in = [sem(f"x_in{t}") for t in range(NCT + NT)]
        item_in = [sem(f"item_in{s}") for s in range(NFRONT)]
        dve_step, pool_step = sem("dve_step"), sem("pool_step")
        setup = sem("setup")
        silc_ready, lam_sum, lam_exp = sem("silc_ready"), sem("lam_sum"), sem("lam_exp")
        squares, rms_ready, xn_ready = sem("squares"), sem("rms_ready"), sem("xn_ready")
        bd_done, bd_ready = sem("bd_done"), sem("bd_ready")
        mod_done, mod_ready = sem("mod_done"), sem("mod_ready")
        tlat_done, tctx_done = sem("tlat_done"), sem("tctx_done")
        hlat_ready, hctx_ready = sem("hlat_ready"), sem("hctx_ready")
        proj_done, roped, rope_sum, copied = sem("proj_done"), sem("roped"), sem("rope_sum"), sem("copied")
        turn_done, turn_out = sem("turn_done"), sem("turn_out")
        g_done, g_ready, fmix_done, fmix_ready = sem("g_done"), sem("g_ready"), sem("fmix_done"), sem("fmix_ready")
        q_staged = sem("q_staged")
        s_done = [sem("s_done0"), sem("s_done1")]
        nmax = [sem("nmax0"), sem("nmax1")]
        exped = [sem("exped0"), sem("exped1")]
        combined, at_done = sem("combined"), sem("at_done")
        at_out = [sem("at_out_act"), sem("at_out_dve")]
        pv_done, o_square, o_rms, o_normed = sem("pv_done"), sem("o_square"), sem("o_rms"), sem("o_normed")
        ot_done, ot_out = sem("ot_done"), sem("ot_out")
        rowc_ready, row_done = sem("rowc_ready"), sem("row_done")
        row_out = [sem("row_out_act"), sem("row_out_dve")]
        pool_tick = sem("pool_tick")
        wo_done, y_square, y_rms, y_scaled, x1_ready = (sem(n) for n in ("wo_done", "y_square", "y_rms", "y_scaled", "x1_ready"))
        x1_square, x1_rms, h_scaled, h2_ready = (sem(n) for n in ("x1_square", "x1_rms", "h_scaled", "h2_ready"))
        h2_stored = [sem("h2_stored0"), sem("h2_stored1")]
        h2t_done, h2t_act, h2t_dve = sem("h2t_done"), sem("h2t_act"), sem("h2t_dve")
        logits_done, scores_ready, mask_ready, pos_done = sem("logits_done"), sem("scores_ready"), sem("mask_ready"), sem("pos_done")
        hot_ready, hot_used, slots_ready, steer_ready = sem("hot_ready"), sem("hot_used"), sem("slots_ready"), sem("steer_ready")
        sgu_done, s_gate, s_up, s_mid, smt_done, smt_out, sy_done, sy_out = (
            sem(n) for n in ("sgu_done", "s_gate", "s_up", "s_mid", "smt_done", "smt_out", "sy_done", "sy_out"))
        w_in = [sem(f"w_in{s}") for s in range(U)]
        ids_ready = sem("ids_ready")
        xg_in = [sem("xg_in0"), sem("xg_in1")]
        gu_done, gate_ready, mid_ready = sem("gu_done"), sem("gate_ready"), sem("mid_ready")
        mt_done, mt_out = sem("mt_done"), sem("mt_out")
        xt_done, xt_act, xt_dve = sem("xt_done"), sem("xt_act"), sem("xt_dve")
        dn_done, y_act, y_dve = sem("dn_done"), sem("y_act"), sem("y_dve")
        y_out = [sem("y_out0"), sem("y_out1")]
        moe_done = sem("moe_done")
        r_in = [sem(f"r_in{s}") for s in range(2)]
        r_sum, r_square, r_rms, r_scaled, r_fin, stored = (sem(n) for n in ("r_sum", "r_square", "r_rms", "r_scaled", "r_fin", "stored"))

        CHUNK_TILES = [range(2, 6), range(2, 6), range(6), range(6), range(6)]
        proj_units = [(c, t) for c in range(5) for t in CHUNK_TILES[c]]
        chunk_end = [max(i for i, (c, _) in enumerate(proj_units) if c == k) + 1 for k in range(5)]
        mod_items = lambda m: [(f"mod{m}{h}", mod_done, m + 1) for h in range(2)]
        items = mod_items(0) + mod_items(1) + [(f"win{c}", proj_done, chunk_end[c]) for c in range(5)]
        items += [("dft", fmix_done, 2)]
        for m in range(2, 6):
            items += mod_items(m)
        items += [("wo0", wo_done, NT), ("wo1", wo_done, NT), ("shgu", sgu_done, NT), ("shd", sy_done, NT)]
        place = {name: i for i, (name, _, _) in enumerate(items)}

        def item(name):
            s = place[name] % NFRONT
            return ring[:, s * FRONT:(s + 1) * FRONT]

        def item_landed(eng, name):
            i = place[name]
            eng.wait_ge(item_in[i % NFRONT], 16 * (i // NFRONT + 1))

        def source(name):
            if name.startswith("mod"):
                m, h = int(name[3]), int(name[4])
                w = A["w_mod"][0].rearrange("(p c) n -> p c n", c=KC)
                return [(item(name).rearrange("p (c n) -> p c n", c=4), w[:, 4 * h:4 * h + 4, m * D:(m + 1) * D])]
            if name.startswith("win"):
                c = int(name[3])
                w = A["w_in"][0].rearrange("(p c) n -> p c n", c=KC)
                return [(item(name).rearrange("p (c n) -> p c n", c=KC), w[:, :, c * 512:(c + 1) * 512])]
            if name == "dft":
                return [(item(name), A["dft"])]
            if name.startswith("wo"):
                n = int(name[2])
                w = A["w_out"][0].rearrange("(c p) n -> p c n", p=P)
                return [(item(name).rearrange("p (c n) -> p c n", c=MIXC), w[:, :, n * 512:(n + 1) * 512])]
            if name == "shgu":
                v = item(name).rearrange("p (s n) -> p s n", s=2)
                return [(v[:, 0], A["ws_gate"][0].rearrange("(p c) n -> p (c n)", c=KC)),
                        (v[:, 1], A["ws_up"][0].rearrange("(p c) n -> p (c n)", c=KC))]
            return [(item(name)[:, 0:GU_W], A["ws_down"][0].rearrange("(p c) n -> p (c n)", c=2))]

        def landed_shared(eng):
            i = place["shgu"]
            eng.wait_ge(item_in[i % NFRONT], 16 * (i // NFRONT + 2))

        def wbuf(s):
            k = (1, 2, 0)[s] if s < 3 else None
            flat = ring[:, k * WBUF:(k + 1) * WBUF] if s < 3 else qreg[:, 0:WBUF]
            return flat

        def gate_up(s):
            return wbuf(s)[:, 0:2 * GU_W].rearrange("p (w c n) -> p w c n", w=2, c=KC)

        def down(s):
            return wbuf(s)[:, 2 * GU_W:].rearrange("p (c n) -> p c n", c=2)

        def done_scatters(g, u):
            k = (u - 3) // 2 + 1 if (u - 1) % 2 == 0 else (u - 4) // 2 + 1
            return g * (16 * U // 2) + 16 * k

        def hot(t):
            base = (t % 2) * (TOPK * P + TOPK * 2 * NB)
            ph = qreg[:, base:base + TOPK * P].rearrange("p (k n) -> p k n", k=TOPK)
            bvw = qreg[:, base + TOPK * P:base + TOPK * P + TOPK * 2 * NB].rearrange("p (k n) -> p k n", k=TOPK)
            return ph, bvw

        def proj_plan():
            pe_turns, act_steps, dve_steps, pool_steps = [], [], [], []
            n_rope = n_copy = n_turn = 0
            unit_free = []
            for i, (c, t) in enumerate(proj_units):
                bank, tok = i % 4, t * P
                rope = t >= NCT and c < 4
                width = (512, 512, 512, 256, 0)[c]
                slot = n_turn % 2
                if rope:
                    n_rope += 1
                    unit_free.append((roped, n_rope))

                    def dve_step_(e, i=i, c=c, t=t, bank=bank, width=width, slot=slot, n=n_turn):
                        e.wait_ge(proj_done, i + 1)
                        if n >= 2:
                            e.wait_ge(turn_done, n - 1)
                        lo = FW if c == 0 else 0
                        g = (width - lo) // HD
                        src = ps[:, bank, lo:width]
                        a, b = ropeA[:, slot, lo:width], ropeB[:, slot, lo:width]
                        cs = ropet[:, t - NCT, 0].unsqueeze(1).broadcast_to([P, g, HD])
                        sn = ropet[:, t - NCT, 1].rearrange("p (a h i) -> p a h i", a=2, h=2)
                        e.tensor_tensor(a.rearrange("p (g d) -> p g d", d=HD), src.rearrange("p (g d) -> p g d", d=HD),
                                        cs, ALU.mult)
                        sv = src.rearrange("p (g a h i) -> p g a h i", a=2, h=2, i=16)
                        bv = b.rearrange("p (g a h i) -> p g a h i", a=2, h=2, i=16)
                        if c == 0:
                            e.tensor_copy(ropeA[:, slot, 0:FW], ps[:, bank, 0:FW])
                        if c == 3:
                            e.tensor_copy(vt[:, t, 0:256], ps[:, bank, 256:512])
                        for x in range(2):
                            snx = sn[:, x].unsqueeze(1).broadcast_to([P, g, 2, 16])
                            for half in range(2):
                                snh = sn[:, x, half].unsqueeze(1).broadcast_to([P, g, 16])
                                last = e.tensor_tensor(bv[:, :, x, half], sv[:, :, x, 1 - half], snh, ALU.mult)
                        last.then_inc(roped, 1)

                    dve_steps.append(dve_step_)

                    def pool_step_(e, c=c, width=width, slot=slot, n=n_rope):
                        e.wait_ge(roped, n)
                        lo = FW if c == 0 else 0
                        a, b = ropeA[:, slot, lo:width], ropeB[:, slot, lo:width]
                        e.tensor_tensor(a, a, b, ALU.add).then_inc(rope_sum, 1)

                    pool_steps.append(pool_step_)
                    staged = (rope_sum, n_rope)
                else:
                    n_copy += 1
                    unit_free.append((copied, n_copy))

                    def copy_step(e, i=i, c=c, t=t, bank=bank, width=width, slot=slot, n=n_turn):
                        e.wait_ge(proj_done, i + 1)
                        if width and n >= 2:
                            e.wait_ge(turn_done, n - 1)
                        if width:
                            last = e.activation(ropeA[:, slot, 0:width], ps[:, bank, 0:width], ACT.Copy)
                        if width < 512:
                            v0 = 0 if c == 3 else 256
                            last = e.activation(vt[:, t, v0:v0 + 512 - width], ps[:, bank, width:512], ACT.Copy)
                        last.then_inc(copied, 1)

                    act_steps.append(copy_step)
                    staged = (copied, n_copy)
                if width:
                    n_turn += 1
                    pe_turns.append((i, slot, width // P, staged))

                    def turn_out_step(e, c=c, t=t, width=width, n=n_turn):
                        e.wait_ge(turn_done, n)
                        bank = 4 + (n - 1) % 2
                        v = ps[:, bank].rearrange("p (h n) -> p h n", h=4)
                        tl = (t - NCT) * P
                        qv = qT.rearrange("p (h n) -> p h n", h=HEADS)
                        kv = kT.rearrange("p (h n) -> p h n", h=HEADS)
                        if c == 0:
                            e.activation(FT[:, :, tl:tl + P], v[:, 0:2], ACT.Copy)
                            last = e.activation(qv[:, 0:2, tl:tl + P], v[:, 2:4], ACT.Copy, scale=HD ** -0.5)
                        elif c == 1:
                            last = e.activation(qv[:, 2:6, tl:tl + P], v, ACT.Copy, scale=HD ** -0.5)
                        elif c == 2:
                            last = e.activation(kv[:, 0:4, t * P:(t + 1) * P], v, ACT.Copy)
                        else:
                            last = e.activation(kv[:, 4:6, t * P:(t + 1) * P], v[:, 0:2], ACT.Copy)
                        last.then_inc(turn_out, 1)

                    act_steps.append(turn_out_step)
                else:
                    pe_turns.append(None)
            return {"pe": pe_turns, "act": act_steps, "dve": dve_steps, "pool": pool_steps, "free": unit_free}

        plan_proj = proj_plan()

        NSMALL = 16
        block = ctx.enter_context(nc.Block())

        @block.sync
        def _(sp):
            xl = A["x"][0].rearrange("(t p) n -> t p n", p=P)
            xc = A["ctx"][0].rearrange("(t p) n -> t p n", p=P)
            for t in range(NCT):
                sp.dma_start(xctx[:, t], xc[t]).then_inc(x_in[t], 16)
            for t in range(NT):
                sp.dma_start(xres[:, t], xl[t]).then_inc(x_in[NCT + t], 16)
            for i, (name, _, _) in enumerate(items):
                if i >= NFRONT:
                    _, used, count = items[i - NFRONT]
                    sp.wait_ge(used, count)
                for dst, src in source(name):
                    sp.dma_start(dst, src).then_inc(item_in[i % NFRONT], 16)
                if name == "shd":
                    break
            for t in range(NT):
                sp.wait_ge(h2_ready, t + 1)
                sp.dma_start(h2_dram[t * P:(t + 1) * P, :], h2[:, t % 2]).then_inc(h2_stored[t % 2], 16)

            def load_expert(s, e):
                v = gate_up(s)
                sp.dma_start(v[:, 0], A["w_gate"][0, e].rearrange("(p c) n -> p c n", c=KC)).then_inc(w_in[s], 16)
                sp.dma_start(v[:, 1], A["w_up"][0, e].rearrange("(p c) n -> p c n", c=KC)).then_inc(w_in[s], 16)
                sp.dma_start(down(s), A["w_down"][0, e].rearrange("(p c) n -> p c n", c=2)).then_inc(w_in[s], 16)

            load_expert(0, 0)
            load_expert(1, 1)
            sp.wait_ge(sgu_done, NT)
            sp.wait_ge(sy_done, NT)
            load_expert(2, 2)
            sp.wait_ge(hot_used, NT)
            sp.wait_ge(steer_ready, 1)
            load_expert(3, 3)
            turns = sp.value_load(steer[0:1, NB:NB + 1], min_val=1, max_val=TURNS)
            with sp.Fori(1, TURNS) as g:
                with sp.If(g < turns):
                    for u in range(U):
                        sp.wait_ge(dn_done, g * U + (u - U + 1))
                        e = sp.value_load(steer[0:1, at(g * U + u, 1)], min_val=0, max_val=NE - 1)
                        v = gate_up(u)
                        for k, name in enumerate(("w_gate", "w_up")):
                            w = A[name][0].rearrange("e (p c) n -> p e (c n)", c=KC)
                            sp.dma_start(v[:, k].rearrange("p c n -> p (c n)").unsqueeze(1),
                                         w[:, bass.ds(e, 1)]).then_inc(w_in[u], 16)
                        w = A["w_down"][0].rearrange("e (p c) n -> p e (c n)", c=2)
                        sp.dma_start(wbuf(u)[:, 2 * GU_W:].unsqueeze(1), w[:, bass.ds(e, 1)]).then_inc(w_in[u], 16)
            sp.wait_ge(moe_done, 1)
            yv = y_dram.rearrange("(t p k) n -> t p (k n)", p=P, k=TOPK)
            for t in range(NT):
                if t >= 2:
                    sp.wait_ge(r_sum, t - 1)
                sp.dma_start(ring[:, (t % 2) * 8192:(t % 2) * 8192 + 8192], yv[t]).then_inc(r_in[t % 2], 16)
            for t in range(NT):
                sp.wait_ge(r_fin, t + 1)
                sp.dma_start(A["out"][0, t * P:(t + 1) * P, :], shy[:, t]).then_inc(stored, 16)
            sp.wait_ge(stored, 16 * NT)
            for s in h2_stored:
                sp.wait_ge(s, 16 * NT // 2)

        @block.scalar
        def _(act):
            col = lambda a: a.rearrange("(p c) -> p c", c=KC)
            loads = [(const[:], A["consts"]), (colc[:, 0], col(A["c"][0])), (colc[:, 1], col(A["c_ctx"])),
                     (bmod[:], A["b_mod"][0].rearrange("(m p c) -> p m c", m=6, c=KC)),
                     (gain[:, 0], col(A["g_attn_pre"][0])), (gain[:, 1], col(A["g_attn_post"][0])),
                     (gain[:, 2], col(A["g_ffn_pre"][0])), (gain[:, 3], col(A["g_ffn_post"][0])),
                     (ropet, A["rope"].rearrange("(t p) s n -> p t s n", p=P)),
                     (gsub[:, 0:1], A["g_subln"][0].rearrange("(p c) -> p c", c=1)),
                     (wrt[:], A["w_router"][0].rearrange("(p c) n -> p c n", c=KC)),
                     (rbias[:], A["router_bias"][0].partition_broadcast(P))]
            loads += [(lamv[:, i], A[n][0].partition_broadcast(P))
                      for i, n in enumerate(("lambda_q1", "lambda_k1", "lambda_q2", "lambda_k2"))]
            assert len(loads) == NSMALL
            for dst, src in loads:
                act.dma_start(dst, src).then_inc(small_in, 16)
            act.wait_ge(wbd_zero, 1)
            for g in range(4):
                r = slice(64 * (g % 2), 64 * (g % 2) + 64)
                act.dma_start(wbd[r, g // 2, r], A["w_fourier"][0, g]).then_inc(wbd_in, 16)
            act.wait_ge(small_in, 16 * NSMALL)
            act.activation(silc[:].rearrange("p c s -> p s c"), colc[:], ACT.Silu).then_inc(silc_ready, 1)
            for t in range(NCT + NT):
                act.wait_ge(x_in[t], 16)
                src = xctx[:, t] if t < NCT else xres[:, t - NCT]
                act.activation(xn[:, t], src, ACT.Square, accum_out=nrm[:, 0, t:t + 1]).then_inc(squares, 1)
            act.wait_ge(lam_sum, 1)
            act.activation(lam[:, 2:4], lam[:, 0:2], ACT.Exp).then_inc(lam_exp, 1)
            act.wait_ge(mod_ready, 3)
            for c in range(KC):
                act.wait_ge(tctx_done, c + 1)
                act.activation(hT[:, c, 0:NCTX], ps[:, 2 + c % 2, 0:NCTX], ACT.Identity,
                               bias=modc[:, 0, c, 1:2], scale=scl1[:, c, 1:2]).then_inc(hctx_ready, 1)
            for step in plan_proj["act"]:
                step(act)
            for t in range(0, NT, 2):
                act.wait_ge(g_done, t + 1)
                act.activation(fg[:, t].rearrange("p j s n -> p (j s n)"), ps[:, t], ACT.Copy).then_inc(g_ready, 1)
            act.wait_ge(fmix_done, 2)
            for j in range(2):
                act.activation(mixTv[:, j], ps[:, 4 + j], ACT.Copy).then_inc(fmix_ready, 1)

            def exps(n, h, qt):
                for m in range(2):
                    act.wait_ge(nmax[m], n + 1)
                    act.activation(prob[:, qt % 2, m], psf[:, 1024 * m:1024 * m + NTOK], ACT.Exp,
                                   bias=stat[:, qt, m:m + 1], accum_out=stat[:, qt, 2 + m:3 + m]).then_inc(exped[m], 1)

            def at_evac(n, qt):
                act.wait_ge(at_done, n + 1)
                act.activation(aT[:, qt % 2, 0:512], ps[:, 4], ACT.Copy).then_inc(at_out[0], 1)

            def square(n, qt):
                act.wait_ge(pv_done, n + 1)
                act.wait_ge(combined, n + 1)
                act.activation(junk, ps[:, 6, 0:VD], ACT.Square, scale=stat[:, qt, 4:5],
                               accum_out=stat[:, qt, 7:8]).then_inc(o_square, 1)

            def ot_evac(n, h, qt):
                act.wait_ge(ot_done, n + 1)
                act.activation(mixT[:, at((2 + h) * NLAT + qt * P, P)], ps[:, 7, 0:P], ACT.Copy,
                               scale=gsub[:, 1:2]).then_inc(ot_out, 1)

            def act_unit(h, u):
                n = h * NT + u
                first = isinstance(h, int) and h == 0
                exps(n, h, u)
                if not first or u >= 1:
                    at_evac(n - 1, (u - 1) % 4)
                if not first or u >= 2:
                    square(n - 2, (u - 2) % 4)
                if not first or u >= 3:
                    ot_evac(n - 3, h - (1 if u < 3 else 0), (u - 3) % 4)

            act.wait_ge(setup, 1)
            for u in range(NT):
                act_unit(0, u)
            with act.Fori(1, HEADS) as h:
                for u in range(NT):
                    act_unit(h, u)
            square(UNITS - 2, 2)
            ot_evac(UNITS - 3, HEADS - 1, 1)
            at_evac(UNITS - 1, 3)
            square(UNITS - 1, 3)
            ot_evac(UNITS - 2, HEADS - 1, 2)
            ot_evac(UNITS - 1, HEADS - 1, 3)

            for i in range(0, 8, 2):
                act.wait_ge(row_done, i + 1)
                row_dst = (grow[:, 0], srow[:, 0], srow[:, 1], grow[:, 1])[i // 2]
                act.activation(row_dst.rearrange("p (j c) -> p c j", c=KC)[:, 0:4],
                               ps[:, 4].rearrange("p (c j) -> p c j", c=4), ACT.Copy).then_inc(row_out[0], 1)

            def h2t_evac(t):
                act.wait_ge(h2t_done, t + 1)
                act.activation(hT2[:, 0:4, t * P:(t + 1) * P], ps[:, 4].rearrange("p (c n) -> p c n", c=4), ACT.Copy)\
                    .then_inc(h2t_act, 1)

            for t in range(NT):
                act.wait_ge(wo_done, t + 1)
                b = 2 * (t % 2)
                act.activation(sq, psf[:, b * 512:b * 512 + D], ACT.Square, accum_out=nrm[:, 0, 6 + t:7 + t])\
                   .then_inc(y_square, 1)
                act.wait_ge(x1_ready, t + 1)
                act.wait_ge(y_square, t + 1)
                act.activation(sq, xres[:, t], ACT.Square, accum_out=nrm[:, 0, 10 + t:11 + t]).then_inc(x1_square, 1)
                act.wait_ge(x1_square, t + 1)
                if t >= 2:
                    h2t_evac(t - 2)
            h2t_evac(NT - 2)
            h2t_evac(NT - 1)
            act.wait_ge(logits_done, 1)
            act.activation(rt[:, 0:256], ps[:, 7, 0:256], ACT.Sigmoid).then_inc(scores_ready, 1)

            def shared_gate(t):
                act.wait_ge(sgu_done, t + 1)
                if t >= 2:
                    act.wait_ge(s_mid, t - 1)
                act.activation(gsil[:, t % 2], ps[:, t % 2, 0:DE], ACT.Silu).then_inc(s_gate, 1)
                act.activation(sreg[:, 1024 + (t % 2) * DE:1024 + (t % 2) * DE + DE], ps[:, t % 2, DE:2 * DE], ACT.Copy)\
                   .then_inc(s_up, 1)

            def shared_out(t):
                act.wait_ge(smt_done, t + 1)
                act.activation(hmT[:, t % 2], ps[:, 6, 0:256].rearrange("p (c n) -> p c n", c=2), ACT.Copy)\
                   .then_inc(smt_out, 1)

            def shared_y(t):
                act.wait_ge(sy_done, t + 1)
                act.activation(shy[:, t], psf[:, 1024:2048], ACT.Copy).then_inc(sy_out, 1)

            for t in range(NT):
                shared_gate(t)
                if t:
                    shared_out(t - 1)
                    shared_y(t - 1)
            shared_out(NT - 1)
            shared_y(NT - 1)

            def x_evac(n, s):
                act.wait_ge(xt_done, n + 1)
                act.activation(xgT[:, s, 0:4], ps[:, 4].rearrange("p (c n) -> p c n", c=4), ACT.Copy)\
                   .then_inc(xt_act, 1)

            def mid_evac(n, s):
                act.wait_ge(mt_done, n + 1)
                act.activation(hmT[:, s], ps[:, 6, 0:256].rearrange("p (c n) -> p c n", c=2), ACT.Copy)\
                   .then_inc(mt_out, 1)

            def y_evac(b, u):
                act.wait_ge(dn_done, b + 1)
                w = ids[:, u, 2:3].bitcast(F32)
                act.activation(yb[:, u % 2, 0:512], ps[:, 2], ACT.Copy, scale=w).then_inc(y_act, 1)

            def act_block(g, u):
                b = g * U + u
                first = isinstance(g, int) and b == 0
                if not first:
                    mid_evac(b - 1, (u - 1) % 2)
                act.wait_ge(gu_done, b + 1)
                act.activation(gsil[:, u % 2], ps[:, u % 2, 0:DE], ACT.Silu).then_inc(gate_ready, 1)
                x_evac(b + 1, (u + 1) % 2)
                if not first:
                    need(act, y_out[(u - 1) % 2], done_scatters(g, u))
                    y_evac(b - 1, (u - 1) % U)

            x_evac(0, 0)
            for u in range(U):
                act_block(0, u)
            act.wait_ge(steer_ready, 1)
            turns = act.value_load(steer[0:1, NB:NB + 1], min_val=1, max_val=TURNS)
            with act.Fori(1, TURNS) as g:
                with act.If(g < turns):
                    for u in range(U):
                        act_block(g, u)
            for t in range(NT):
                act.wait_ge(r_sum, t + 1)
                act.activation(sreg[:, 0:1024], shy[:, t], ACT.Square, accum_out=nrm[:, 0, 14 + t:15 + t])\
                   .then_inc(r_square, 1)
                act.wait_ge(r_square, t + 1)

        @block.tensor
        def _(pe):
            mm = nc.tensor.matmul
            pe.wait_ge(small_in, 16 * NSMALL)
            pe.wait_ge(wbd_in, 64)
            for j in range(2):
                for s in range(2):
                    last = mm(ps[:, 7, (2 * j + s) * P:(2 * j + s + 1) * P],
                              const[:, (C_CC, C_SC)[s]:(C_CC, C_SC)[s] + P], wbd[:, j], start=True, stop=True)
            last.then_inc(bd_done, 1)

            def modulation(m):
                item_landed(pe, f"mod{m}0")
                item_landed(pe, f"mod{m}1")
                if m >= 1:
                    pe.wait_ge(*((bd_ready, 1) if m == 1 else (mod_ready, m - 1 if m < 4 else m)))
                w = [item(f"mod{m}{h}").rearrange("p (k j c) -> p k j c", k=4, c=KC) for h in range(2)]
                for c in range(KC):
                    for k in range(KC):
                        last = mm(ps[:, 6 + m % 2, 2 * c:2 * c + 2], w[k // 4][:, k % 4, :, c], silc[:, k],
                                  start=(k == 0), stop=(k == KC - 1))
                last.then_inc(mod_done, 1)

            pe.wait_ge(silc_ready, 1)
            modulation(0)
            modulation(1)
            pe.wait_ge(xn_ready, NCT + NT)
            for c in range(KC):
                if c >= 2:
                    pe.wait_ge(hlat_ready, c - 1)
                    pe.wait_ge(hctx_ready, c - 1)
                for t in range(NCT + NT):
                    out = ps[:, 2 + c % 2, t * P:(t + 1) * P] if t < NCT else \
                        ps[:, c % 2, (t - NCT) * P:(t - NCT + 1) * P]
                    v = xn[:, t].rearrange("p (j c) -> p j c", c=KC)[:, :, c]
                    last = nc.tensor.transpose(out, v, ident)
                    if t == NCT - 1:
                        last.then_inc(tctx_done, 1)
                last.then_inc(tlat_done, 1)
            pe.wait_ge(hlat_ready, KC)
            pe.wait_ge(hctx_ready, KC)
            turns = plan_proj["pe"]
            n_turn = 0

            def turn(k):
                nonlocal n_turn
                if turns[k] is None:
                    return
                _, slot, nh, staged = turns[k]
                pe.wait_ge(*staged)
                if n_turn >= 2:
                    pe.wait_ge(turn_out, n_turn - 1)
                for x in range(nh):
                    last = nc.tensor.transpose(ps[:, 4 + n_turn % 2, x * P:(x + 1) * P],
                                               ropeA[:, slot, x * P:(x + 1) * P], ident)
                last.then_inc(turn_done, 1)
                n_turn += 1

            for i, (c, t) in enumerate(proj_units):
                item_landed(pe, f"win{c}")
                if i >= 4:
                    pe.wait_ge(*plan_proj["free"][i - 4])
                w = item(f"win{c}").rearrange("p (c n) -> p c n", c=KC)
                for k in range(KC):
                    last = mm(ps[:, i % 4], hT[:, k, t * P:(t + 1) * P], w[:, k], start=(k == 0), stop=(k == KC - 1))
                last.then_inc(proj_done, 1)
                if i:
                    turn(i - 1)
            turn(len(proj_units) - 1)
            pe.wait_ge(*plan_proj["free"][-1])
            pe.wait_ge(roped, sum(1 for s, _ in plan_proj["free"] if s is roped))
            pe.wait_ge(turn_out, n_turn)
            pe.wait_ge(bd_ready, 1)
            for t in range(NT):
                for j in range(2):
                    last = mm(ps[:, t, 256 * j:256 * j + 256], FT[:, j, t * P:(t + 1) * P],
                              bd[:, j].rearrange("p s n -> p (s n)"), start=True, stop=True)
                last.then_inc(g_done, 1)
            item_landed(pe, "dft")
            dft = item("dft").rearrange("p (s t n) -> p s t n", s=2, t=NT)
            pe.wait_ge(g_ready, NT)
            for j in range(2):
                for t in range(NT):
                    for s in range(2):
                        last = mm(ps[:, 4 + j], fg[:, t, j, s], dft[:, s, t], start=(t == 0 and s == 0),
                                  stop=(t == NT - 1 and s == 1))
                last.then_inc(fmix_done, 1)
            for m in range(2, 6):
                modulation(m)

            def scores(n, h, qt):
                pe.wait_ge(q_staged, n + 1)
                for m in range(2):
                    need(pe, exped[m], n)
                    mm(ps[:, 2 * m], qz[:, qt % 2, m], kT[:, at(h * NTOK, 512)], start=True, stop=True)
                    mm(ps[:, 2 * m + 1, 0:256], qz[:, qt % 2, m], kT[:, at(h * NTOK + 512, 256)],
                       start=True, stop=True).then_inc(s_done[m], 1)

            def values(n, h, qt):
                pe.wait_ge(at_out[0], n + 1)
                pe.wait_ge(at_out[1], n + 1)
                need(pe, o_normed, n)
                for k in range(NCT + NT):
                    last = mm(ps[:, 6, 0:VD], aT[:, qt % 2, k * P:(k + 1) * P], vt[:, k, at(h * VD, VD)],
                              start=(k == 0), stop=(k == NCT + NT - 1))
                last.then_inc(pv_done, 1)

            def turn_probs(n, qt):
                pe.wait_ge(combined, n + 1)
                for k in range(NCT + NT):
                    last = nc.tensor.transpose(psf[:, 2048 + k * P:2048 + (k + 1) * P],
                                               prob[:, qt % 2, 0, k * P:(k + 1) * P], ident)
                last.then_inc(at_done, 1)

            def turn_out_rows(n, qt):
                pe.wait_ge(o_normed, n + 1)
                need(pe, ot_out, n)
                nc.tensor.transpose(ps[:, 7, 0:P], onrm[:, qt % 2], ident).then_inc(ot_done, 1)

            def pe_unit(h, u):
                n = h * NT + u
                first = isinstance(h, int) and h == 0
                scores(n, h, u)
                if not first or u >= 2:
                    values(n - 2, h - (1 if u < 2 else 0), (u - 2) % 4)
                if not first or u >= 1:
                    turn_probs(n - 1, (u - 1) % 4)
                if not first or u >= 3:
                    turn_out_rows(n - 3, (u - 3) % 4)

            pe.wait_ge(fmix_ready, 2)
            pe.wait_ge(mod_ready, 7)
            for u in range(NT):
                pe_unit(0, u)
            with pe.Fori(1, HEADS) as h:
                for u in range(NT):
                    pe_unit(h, u)
            values(UNITS - 2, HEADS - 1, 2)
            turn_out_rows(UNITS - 3, 1)
            turn_probs(UNITS - 1, 3)
            values(UNITS - 1, HEADS - 1, 3)
            turn_out_rows(UNITS - 2, 2)
            turn_out_rows(UNITS - 1, 3)

            pe.wait_ge(rowc_ready, 1)
            for i in range(8):
                r, half = i // 2, i % 2
                if i >= 2:
                    pe.wait_ge(row_out[half], i // 2)
                for c in range(4):
                    last = mm(ps[:, 4 + half, c * P:(c + 1) * P],
                              rowc[:, r, 4 * half + c:4 * half + c + 1].broadcast_to([P, P]), ident,
                              start=True, stop=True)
                last.then_inc(row_done, 1)
            pe.wait_ge(ot_out, UNITS)
            item_landed(pe, "wo0")
            item_landed(pe, "wo1")
            w = [item(f"wo{n}").rearrange("p (c n) -> p c n", c=MIXC) for n in range(2)]

            def turn_h2(t):
                pe.wait_ge(h2_ready, t + 1)
                if t:
                    pe.wait_ge(h2t_act, t)
                    pe.wait_ge(h2t_dve, t)
                else:
                    pe.wait_ge(row_out[0], 4)
                    pe.wait_ge(row_out[1], 4)
                for c in range(KC):
                    last = nc.tensor.transpose(ps[:, 4 + c // 4, (c % 4) * P:(c % 4 + 1) * P],
                                               h2[:, t % 2].rearrange("p (j c) -> p j c", c=KC)[:, :, c], ident)
                last.then_inc(h2t_done, 1)

            for t in range(NT):
                if t >= 2:
                    pe.wait_ge(y_scaled, t - 1)
                for n in range(2):
                    for c in range(MIXC):
                        last = mm(ps[:, 2 * (t % 2) + n], mixTv[:, c, t * P:(t + 1) * P], w[n][:, c],
                                  start=(c == 0), stop=(c == MIXC - 1))
                last.then_inc(wo_done, 1)
                if t >= 2:
                    turn_h2(t - 2)
            turn_h2(NT - 2)
            turn_h2(NT - 1)
            pe.wait_ge(h2t_act, NT)
            pe.wait_ge(h2t_dve, NT)
            for t in range(NT):
                for k in range(KC):
                    last = mm(ps[:, 7, t * NE:(t + 1) * NE], hT2[:, k, t * P:(t + 1) * P], wrt[:, k],
                              start=(k == 0), stop=(k == KC - 1))
            last.then_inc(logits_done, 1)
            landed_shared(pe)
            item_landed(pe, "shd")
            gu = item("shgu").rearrange("p (w c n) -> p w c n", w=2, c=KC)
            dn = item("shd")[:, 0:GU_W].rearrange("p (c n) -> p c n", c=2)

            def shared_gu(t):
                pe.wait_ge(*((s_up, t - 1) if t >= 2 else (y_scaled, NT)))
                for k in range(KC):
                    last = mm(ps[:, t % 2], hT2[:, k, t * P:(t + 1) * P], gu[:, :, k], start=(k == 0), stop=(k == KC - 1))
                last.then_inc(sgu_done, 1)

            def shared_down(t):
                pe.wait_ge(s_mid, t + 1)
                if t:
                    pe.wait_ge(smt_out, t)
                v = hmid[:, t % 2].rearrange("p (j c) -> p j c", c=2)
                for c in range(2):
                    last = nc.tensor.transpose(ps[:, 6, c * P:(c + 1) * P], v[:, :, c], ident)
                last.then_inc(smt_done, 1)
                pe.wait_ge(smt_out, t + 1)
                if t:
                    pe.wait_ge(sy_out, t)
                for n in range(2):
                    for c in range(2):
                        last = mm(ps[:, 2 + n], hmT[:, t % 2, c], dn[:, c, n * 512:(n + 1) * 512],
                                  start=(c == 0), stop=(c == 1))
                last.then_inc(sy_done, 1)

            shared_gu(0)
            shared_gu(1)
            shared_down(0)
            pe.wait_ge(mask_ready, 1)
            mask = rt[:, 256:512].rearrange("p (t e) -> p t e", t=NT)
            for t in range(NT):
                mm(ps[:, 4, t * NE:(t + 1) * NE], tri, mask[:, t], start=True, stop=(t == 0))
                for s in range(t):
                    mm(ps[:, 4, t * NE:(t + 1) * NE], ones[:], mask[:, s], start=False, stop=(s == t - 1))
            for t in range(NT):
                last = mm(ps[:, 5, 0:NE], ones[:], mask[:, t], start=(t == 0), stop=(t == NT - 1))
            last.then_inc(pos_done, 1)
            shared_gu(2)
            shared_down(1)
            shared_gu(3)
            shared_down(2)
            shared_down(3)
            for t in range(NT):
                pe.wait_ge(hot_ready, t + 1)
                ph, bvw = hot(t)
                for k in range(TOPK):
                    last = mm(ps[:, 7, 0:2 * NB], ph[:, k], bvw[:, k], start=(t == 0 and k == 0),
                              stop=(t == NT - 1 and k == TOPK - 1))
                last.then_inc(hot_used, 1)

            def turn_x(n, s, k):
                pe.wait_ge(xg_in[s], 16 * (k + 1))
                for c in range(KC):
                    last = nc.tensor.transpose(ps[:, 4 + c // 4, (c % 4) * P:(c % 4 + 1) * P],
                                               xg[:, s].rearrange("p (j c) -> p j c", c=KC)[:, :, c], ident)
                last.then_inc(xt_done, 1)

            def pe_block(g, u):
                b = g * U + u
                first = isinstance(g, int) and b == 0
                pe.wait_ge(w_in[u], 48 * (g + 1))
                pe.wait_ge(xt_act, b + 1)
                pe.wait_ge(xt_dve, b + 1)
                need(pe, mid_ready, b - 1)
                gu = gate_up(u)
                for k in range(KC):
                    last = mm(ps[:, u % 2], xgT[:, u % 2, k], gu[:, :, k], start=(k == 0), stop=(k == KC - 1))
                last.then_inc(gu_done, 1)
                if not first:
                    pe.wait_ge(mid_ready, b)
                    need(pe, mt_out, b - 1)
                    v = hmid[:, (u - 1) % 2].rearrange("p (j c) -> p j c", c=2)
                    for c in range(2):
                        last = nc.tensor.transpose(ps[:, 6, c * P:(c + 1) * P], v[:, :, c], ident)
                    last.then_inc(mt_done, 1)
                turn_x(b + 1, (u + 1) % 2, g * 2 + (u + 1) // 2)
                if not first:
                    pe.wait_ge(mt_out, b)
                    need(pe, y_act, b - 1)
                    need(pe, y_dve, b - 1)
                    dn = down((u - 1) % U)
                    for n in range(2):
                        for c in range(2):
                            last = mm(ps[:, 2 + n], hmT[:, (u - 1) % 2, c], dn[:, c, n * 512:(n + 1) * 512],
                                      start=(c == 0), stop=(c == 1))
                    last.then_inc(dn_done, 1)

            pe.wait_ge(sy_out, NT)
            turn_x(0, 0, 0)
            for u in range(U):
                pe_block(0, u)
            pe.wait_ge(steer_ready, 1)
            turns = pe.value_load(steer[0:1, NB:NB + 1], min_val=1, max_val=TURNS)
            with pe.Fori(1, TURNS) as g:
                with pe.If(g < turns):
                    for u in range(U):
                        pe_block(g, u)

        @block.vector
        def _(dve):
            steps = [0]

            def link(ins):
                steps[0] += 1
                ins.then_inc(dve_step, 1)
                dve.wait_ge(dve_step, steps[0])

            dve.memset(wbd, 0.0).then_inc(wbd_zero, 1)
            link(dve.memset(ones[:], 1.0))
            dve.wait_ge(small_in, 16 * NSMALL)
            for i in range(2):
                last = dve.tensor_tensor_reduce(out=junk[:, i * HD:(i + 1) * HD], in0=lamv[:, 2 * i], in1=lamv[:, 2 * i + 1],
                                                scale=1.0, scalar=0.0, op0=ALU.mult, op1=ALU.add,
                                                accum_out=lam[:, i:i + 1])
            last.then_inc(lam_sum, 1)
            for t in range(NCT + NT):
                src = xctx[:, t] if t < NCT else xres[:, t - NCT]
                dve.wait_ge(x_in[t], 16)
                dve.wait_ge(rms_ready, t + 1)
                dve.tensor_scalar(xn[:, t], src, nrm[:, 2, t:t + 1], None, ALU.mult).then_inc(xn_ready, 1)
            dve.wait_ge(bd_done, 1)
            dve.tensor_copy(bd.rearrange("p j s n -> p (j s n)"), ps[:, 7]).then_inc(bd_ready, 1)
            dve.wait_ge(lam_exp, 1)
            dve.scalar_tensor_tensor(lam[:, 4:5], lam[:, 3:4], -LAM0, lam[:, 2:3], ALU.add, ALU.subtract)
            dve.tensor_scalar(gsub[:, 1:2], gsub[:, 0:1], 1.0 - LAM0, None, ALU.mult).then_inc(setup, 1)

            def modulation_out(m):
                dve.wait_ge(mod_done, m + 1)
                dve.tensor_tensor(modc[:, m], ps[:, 6 + m % 2, 0:2 * KC].rearrange("p (c s) -> p c s", s=2),
                                  bmod[:, m].unsqueeze(2).broadcast_to([P, KC, 2]), ALU.add).then_inc(mod_ready, 1)

            modulation_out(0)
            modulation_out(1)
            dve.wait_ge(mod_ready, 2)
            dve.scalar_tensor_tensor(scl1[:], modc[:, 1], 1.0, gain[:, 0].unsqueeze(2).broadcast_to([P, KC, 2]),
                                     ALU.add, ALU.mult).then_inc(mod_ready, 1)
            dve.wait_ge(mod_ready, 3)
            for c in range(KC):
                dve.wait_ge(tlat_done, c + 1)
                dve.tensor_scalar(hT[:, c, NCTX:], ps[:, c % 2], scl1[:, c, 0:1], modc[:, 0, c, 0:1], ALU.mult, ALU.add)\
                   .then_inc(hlat_ready, 1)
            for step in plan_proj["dve"]:
                step(dve)
            for t in range(1, NT, 2):
                dve.wait_ge(g_done, t + 1)
                dve.tensor_copy(fg[:, t].rearrange("p j s n -> p (j s n)"), ps[:, t]).then_inc(g_ready, 1)
            for m in range(2, 6):
                modulation_out(m)
            dve.wait_ge(mod_ready, 7)
            dve.tensor_tensor(rowc[:, 0], modc[:, 2, :, 0], gain[:, 1], ALU.mult)
            dve.scalar_tensor_tensor(rowc[:, 1], modc[:, 4, :, 0], 1.0, gain[:, 2], ALU.add, ALU.mult)
            dve.tensor_copy(rowc[:, 2], modc[:, 3, :, 0])
            dve.tensor_tensor(rowc[:, 3], modc[:, 5, :, 0], gain[:, 3], ALU.mult).then_inc(rowc_ready, 1)

            N_LINK = 3

            def alink(ins, n, k):
                ins.then_inc(dve_step, 1)
                dve.wait_ge(dve_step, att0 + k + 1 + n * N_LINK)

            att0 = steps[0]

            def o_norm(n, qt):
                dve.wait_ge(o_rms, n + 1)
                dve.tensor_scalar(onrm[:, qt % 2], ps[:, 6, 0:VD], stat[:, qt, 4:5], stat[:, qt, 9:10],
                                  ALU.mult, ALU.mult).then_inc(o_normed, 1)

            def at_evac(n, qt):
                dve.wait_ge(at_done, n + 1)
                dve.tensor_copy(aT[:, qt % 2, 512:768], ps[:, 5, 0:256]).then_inc(at_out[1], 1)

            def dve_unit(h, u):
                n = h * NT + u
                first = isinstance(h, int) and h == 0
                st = stat[:, u]
                for m in range(2):
                    dve.wait_ge(s_done[m], n + 1)
                    dve.tensor_reduce(st[:, m:m + 1], psf[:, 1024 * m:1024 * m + NTOK], AX, ALU.max, negate=True)\
                       .then_inc(nmax[m], 1)
                if not first or u >= 1:
                    at_evac(n - 1, (u - 1) % 4)
                if not first or u >= 2:
                    o_norm(n - 2, (u - 2) % 4)
                dve.wait_ge(exped[0], n + 1)
                dve.wait_ge(exped[1], n + 1)
                alink(dve.reciprocal(st[:, 4:6], st[:, 2:4]), n, 0)
                alink(dve.scalar_tensor_tensor(st[:, 6:7], st[:, 2:3], lam[:, 4:5], st[:, 5:6], ALU.mult, ALU.mult), n, 1)
                dve.scalar_tensor_tensor(prob[:, u % 2, 0], prob[:, u % 2, 1], st[:, 6:7], prob[:, u % 2, 0],
                                         ALU.mult, ALU.add).then_inc(combined, 1)
                alink(dve.engine_nop(), n, 2) if False else None

            N_LINK = 2
            dve.wait_ge(setup, 1)
            for u in range(NT):
                dve_unit(0, u)
            with dve.Fori(1, HEADS) as h:
                for u in range(NT):
                    dve_unit(h, u)
            steps[0] += N_LINK * UNITS
            o_norm(UNITS - 2, 2)
            at_evac(UNITS - 1, 3)
            o_norm(UNITS - 1, 3)

            for i in range(1, 8, 2):
                dve.wait_ge(row_done, i + 1)
                row_dst = (grow[:, 0], srow[:, 0], srow[:, 1], grow[:, 1])[i // 2]
                dve.tensor_copy(row_dst.rearrange("p (j c) -> p c j", c=KC)[:, 4:8],
                                ps[:, 5].rearrange("p (c j) -> p c j", c=4)).then_inc(row_out[1], 1)
            for half in range(2):
                dve.wait_ge(row_out[half], 4)

            def h2t_evac(t):
                dve.wait_ge(h2t_done, t + 1)
                dve.tensor_copy(hT2[:, 4:8, t * P:(t + 1) * P], ps[:, 5].rearrange("p (c n) -> p c n", c=4))\
                   .then_inc(h2t_dve, 1)

            for t in range(NT):
                b = 2 * (t % 2)
                dve.wait_ge(y_rms, t + 1)
                if t:
                    dve.wait_ge(x1_ready, t)
                dve.scalar_tensor_tensor(tmp1, psf[:, b * 512:b * 512 + D], nrm[:, 2, 6 + t:7 + t], grow[:, 0],
                                         ALU.mult, ALU.mult).then_inc(y_scaled, 1)
                dve.wait_ge(y_scaled, t + 1)
                dve.tensor_tensor(xres[:, t], xres[:, t], tmp1, ALU.add).then_inc(x1_ready, 1)
                dve.wait_ge(x1_rms, t + 1)
                if t >= 2:
                    dve.wait_ge(h2_stored[t % 2], 16 * (t // 2))
                    dve.wait_ge(h2t_done, t - 1)
                dve.scalar_tensor_tensor(h2[:, t % 2], xres[:, t], nrm[:, 2, 10 + t:11 + t], srow[:, 0],
                                         ALU.mult, ALU.mult).then_inc(h_scaled, 1)
                if t >= 2:
                    h2t_evac(t - 2)
            h2t_evac(NT - 2)
            h2t_evac(NT - 1)

            sc = rt[:, 0:256]
            mask = rt[:, 256:512]
            sel, selm, selr, wn, sslot = (rt[:, 512 + 256 * i:768 + 256 * i] for i in range(5))
            gsum, rank, idxf, skf, wkf, pf, bf = (rt[:, 1792 + 32 * i:1824 + 32 * i] for i in range(7))
            t4 = lambda v: v.rearrange("p (t e) -> p t e", t=NT)
            t48 = lambda v: v.rearrange("p (t g e) -> p t g e", t=NT, g=NGRP)
            m8 = qreg[:, 0:256].rearrange("p (t g k) -> p t g k", t=NT, g=NGRP)
            cmp1, cmp2 = qreg[:, 256:512], qreg[:, 512:768]
            v8, idx = qreg[:, 768:800], qreg[:, 800:832].bitcast(U32)
            ovf = hreg[:, 4096:4096 + 512]
            nb, ovend, base = (ovf[:, 64 * i:64 * i + 64] for i in range(3))
            small = ovf[:, 192:256]
            ints = hreg[:, 4608:4736].bitcast(I32)
            for s in h2_stored:
                dve.wait_ge(s, 16 * NT // 2)
            dve.wait_ge(h2t_done, NT)
            dve.wait_ge(scores_ready, 1)
            link(dve.tensor_tensor(t4(sel), t4(sc), rbias[:].unsqueeze(1).broadcast_to([P, NT, NE]), ALU.add))
            for t in range(NT):
                for g in range(NGRP):
                    last = dve.max(out=m8[:, t, g], in_=sel[:, t * NE + g * GE:t * NE + (g + 1) * GE])
            link(last)
            g3 = gsum.rearrange("p (t g) -> p t g", t=NT)
            link(dve.tensor_tensor(g3, m8[:, :, :, 0], m8[:, :, :, 1], ALU.add))
            other = g3.unsqueeze(2).broadcast_to([P, NT, NGRP, NGRP])
            own = g3.unsqueeze(3).broadcast_to([P, NT, NGRP, NGRP])
            dve.tensor_tensor(t48(cmp1), other, own, ALU.is_gt)
            link(dve.tensor_tensor(t48(cmp2), other, own, ALU.is_equal))
            earlier = const[:, C_LT:C_LT + 64].unsqueeze(1).broadcast_to([P, NT, 64])
            link(dve.tensor_tensor(t4(cmp2), t4(cmp2), earlier, ALU.mult))
            link(dve.tensor_tensor(cmp1, cmp1, cmp2, ALU.add))
            link(dve.tensor_reduce(rank, cmp1.rearrange("p (g k) -> p g k", k=NGRP), AX, ALU.add))
            link(dve.tensor_scalar(rank, rank, float(TOPG), -1e30, ALU.is_ge, ALU.mult))
            link(dve.tensor_tensor(selm.rearrange("p (g e) -> p g e", e=GE), sel.rearrange("p (g e) -> p g e", e=GE),
                                   rank.unsqueeze(2).broadcast_to([P, NT * NGRP, GE]), ALU.add))
            for t in range(NT):
                last = dve.max(out=v8[:, 8 * t:8 * t + 8], in_=selm[:, t * NE:(t + 1) * NE])
            link(last)
            for t in range(NT):
                dve.max_index(idx[:, 8 * t:8 * t + 8], v8[:, 8 * t:8 * t + 8], selm[:, t * NE:(t + 1) * NE])
            for t in range(NT):
                last = dve.match_replace(selr[:, t * NE:(t + 1) * NE], v8[:, 8 * t:8 * t + 8],
                                         selm[:, t * NE:(t + 1) * NE], -3e38)
            link(last)
            dve.tensor_tensor(mask, selm, selr, ALU.not_equal).then_inc(mask_ready, 1)
            dve.tensor_copy(idxf, idx)
            dve.wait_ge(mask_ready, 1)
            link(dve.tensor_tensor(selr, sc, mask, ALU.mult))
            link(dve.tensor_reduce(small[:, 0:4], t4(selr), AX, ALU.add))
            link(dve.tensor_scalar(small[:, 4:8], small[:, 0:4], 1e-20, None, ALU.add))
            link(dve.reciprocal(small[:, 8:12], small[:, 4:8]))
            link(dve.tensor_scalar(small[:, 12:16], small[:, 8:12], ROUTED_SCALE, None, ALU.mult))
            link(dve.tensor_tensor(t4(wn), t4(selr), small[:, 12:16].unsqueeze(2).broadcast_to([P, NT, NE]), ALU.mult))
            dve.wait_ge(pos_done, 1)
            link(dve.tensor_scalar(nb, ps[:, 5, 0:NE], float(P), None, ALU.is_gt))
            link(dve.scalar_tensor_tensor(nb, ps[:, 5, 0:NE], float(2 * P), nb, ALU.is_gt, ALU.add))
            link(dve.scalar_tensor_tensor(nb, ps[:, 5, 0:NE], float(3 * P), nb, ALU.is_gt, ALU.add))
            link(dve.tensor_tensor_scan(ovend, ones[:, 0:NE], nb, 0.0, ALU.mult, ALU.add))
            link(dve.tensor_tensor(base, ovend, nb, ALU.subtract))
            link(dve.scalar_tensor_tensor(base, base, float(NE - 1), iota[:, 0:NE], ALU.add, ALU.subtract))
            pos = ps[:, 4, 0:256]
            link(dve.scalar_tensor_tensor(t4(sslot), t4(pos), float(P), base.unsqueeze(1).broadcast_to([P, NT, NE]),
                                          ALU.is_ge, ALU.mult))
            link(dve.tensor_tensor(t4(sslot), t4(sslot), iota[:, 0:NE].unsqueeze(1).broadcast_to([P, NT, NE]), ALU.add))
            link(dve.scalar_tensor_tensor(sslot, sslot, float(P), pos, ALU.mult, ALU.add))
            oh, prod, prod2 = qreg[:, 1024:1536], qreg[:, 1536:2048], qreg[:, 2048:2560]
            k8 = lambda v: v.rearrange("p (k e) -> p k e", k=TOPK)
            for t in range(NT):
                link(dve.tensor_tensor(k8(oh), iota[:, 0:NE].unsqueeze(1).broadcast_to([P, TOPK, NE]),
                                       idxf[:, 8 * t:8 * t + 8].unsqueeze(2).broadcast_to([P, TOPK, NE]), ALU.is_equal))
                dve.tensor_tensor(k8(prod), k8(oh), sslot[:, t * NE:(t + 1) * NE].unsqueeze(1).broadcast_to([P, TOPK, NE]),
                                  ALU.mult)
                link(dve.tensor_tensor(k8(prod2), k8(oh), wn[:, t * NE:(t + 1) * NE].unsqueeze(1).broadcast_to([P, TOPK, NE]),
                                       ALU.mult))
                dve.tensor_reduce(skf[:, 8 * t:8 * t + 8], k8(prod), AX, ALU.add)
                link(dve.tensor_reduce(wkf[:, 8 * t:8 * t + 8], k8(prod2), AX, ALU.add))
            link(dve.tensor_copy(ints[:, 0:32], skf))
            dve.tensor_scalar(ints[:, 32:64], ints[:, 0:32], P - 1, None, ALU.bitwise_and)
            link(dve.tensor_scalar(ints[:, 64:96], ints[:, 0:32], 7, None, ALU.logical_shift_right))
            dve.tensor_copy(pf, ints[:, 32:64])
            link(dve.tensor_copy(bf, ints[:, 64:96]))
            ob = qreg[:, 5248:6048].rearrange("p (k n) -> p k n", k=TOPK)
            for t in range(NT):
                if t >= 2:
                    dve.wait_ge(hot_used, t - 1)
                ph, bvw = hot(t)
                by8 = lambda v, n: v[:, 8 * t:8 * t + 8].unsqueeze(2).broadcast_to([P, TOPK, n])
                dve.tensor_tensor(ph, iota.unsqueeze(1).broadcast_to([P, TOPK, P]), by8(pf, P), ALU.is_equal)
                link(dve.tensor_tensor(ob, iota[:, 0:NB].unsqueeze(1).broadcast_to([P, TOPK, NB]), by8(bf, NB),
                                       ALU.is_equal))
                dve.tensor_tensor(bvw[:, :, 0:NB], ob, by8(const[:, C_V:C_V + 32], NB), ALU.mult)
                dve.tensor_tensor(bvw[:, :, NB:2 * NB], ob, by8(wkf, NB), ALU.mult).then_inc(hot_ready, 1)
                dve.wait_ge(hot_ready, t + 1)
            nj = NB - NE
            ovc = hreg[0:1, 4736:4736 + 640].rearrange("p (j e) -> p j e", e=NE)
            ovn = hreg[0:1, 5376:5376 + NB + 4]
            dve.tensor_copy(ovn[:, 0:NE], iota[0:1, 0:NE])
            for j0 in range(0, nj, 9):
                link(dve.tensor_tensor(ovc[:, 0:9], ovend[0:1].unsqueeze(1).broadcast_to([1, 9, NE]),
                                       iota[0:1, j0:j0 + 9].unsqueeze(2).broadcast_to([1, 9, NE]), ALU.is_le))
                link(dve.tensor_reduce(ovn[:, NE + j0:NE + j0 + 9], ovc[:, 0:9], AX, ALU.add))
            link(dve.tensor_scalar(ovn[:, NE:NB], ovn[:, NE:NB], float(NE - 1), None, ALU.min))
            link(dve.tensor_scalar(ovn[:, NB:NB + 1], ovend[0:1, NE - 1:NE], float(NE + U), None, ALU.add))
            link(dve.tensor_copy(steer[:, 0:NB + 1], ovn[:, 0:NB + 1]))
            link(dve.tensor_scalar(steer[:, NB:NB + 1], steer[:, NB:NB + 1], 2, None, ALU.logical_shift_right))
            link(dve.tensor_copy(ovn[:, NB + 1:NB + 2], steer[:, NB:NB + 1]))
            per = 16.0 * U // 2
            link(dve.tensor_scalar(ovn[:, NB + 3:NB + 4], ovn[:, NB + 1:NB + 2], per, 16.0, ALU.mult, ALU.add))
            link(dve.tensor_scalar(ovn[:, NB + 2:NB + 3], ovn[:, NB + 1:NB + 2], per, -16.0, ALU.mult, ALU.add))
            link(dve.tensor_scalar(ovn[:, NB + 1:NB + 2], ovn[:, NB + 1:NB + 2], per, None, ALU.mult))
            link(dve.tensor_copy(steer[:, NB + 1:NB + 4], ovn[:, NB + 1:NB + 4]))
            dve.wait_ge(hot_used, NT)
            tv, tw = ps[:, 7, 0:NB], ps[:, 7, NB:2 * NB]
            emp, rowf = hreg[:, 4096:4096 + NB], hreg[:, 4256:4256 + NB]
            link(dve.tensor_scalar(emp, tv, 0.0, SKIP, ALU.is_equal, ALU.mult))
            link(dve.scalar_tensor_tensor(rowf, tv, -1.0, emp, ALU.add, ALU.add))
            dve.tensor_copy(slots[:, :, 1], rowf)
            link(dve.tensor_copy(slots[:].bitcast(F32)[:, :, 2], tw))
            link(dve.tensor_scalar(slots[:, :, 0], slots[:, :, 1], 3, None, ALU.logical_shift_right))
            dve.memset(hreg[:, 4096:6144], 0.0).then_inc(slots_ready, 1)
            dve.wait_ge(slots_ready, 1)
            dve.engine_nop().then_inc(steer_ready, 1)

            def take_ids(b, u):
                dve.tensor_copy(ids[:, u], slots[:, at(b, 1)].squeeze(1) if False else slots_flat[:, at(b * 3, 3)])\
                   .then_inc(ids_ready, 1)

            slots_flat = slots[:].rearrange("p b k -> p (b k)")

            def x_evac(n, s):
                dve.wait_ge(xt_done, n + 1)
                dve.tensor_copy(xgT[:, s, 4:8], ps[:, 5].rearrange("p (c n) -> p c n", c=4)).then_inc(xt_dve, 1)

            def dve_block(g, u):
                b = g * U + u
                first = isinstance(g, int) and b == 0
                need(dve, y_out[u % 2], g * (16 * U // 2) + 16 * ((u - 2) // 2 + 1))
                take_ids(b + 2, (u + 2) % U)
                dve.wait_ge(gate_ready, b + 1)
                dve.tensor_tensor(hmid[:, u % 2], ps[:, u % 2, DE:2 * DE], gsil[:, u % 2], ALU.mult).then_inc(mid_ready, 1)
                x_evac(b + 1, (u + 1) % 2)
                if not first:
                    dve.wait_ge(dn_done, b)
                    need(dve, y_out[(u - 1) % 2], done_scatters(g, u))
                    w = ids[:, (u - 1) % U, 2:3].bitcast(F32)
                    dve.tensor_scalar(yb[:, (u - 1) % 2, 512:1024], ps[:, 3], w, None, ALU.mult).then_inc(y_dve, 1)

            dve.wait_ge(sy_out, NT)
            take_ids(0, 0)
            take_ids(1, 1)
            x_evac(0, 0)
            for u in range(U):
                dve_block(0, u)
            turns = dve.value_load(steer[0:1, NB:NB + 1], min_val=1, max_val=TURNS)
            with dve.Fori(1, TURNS) as g:
                with dve.If(g < turns):
                    for u in range(U):
                        dve_block(g, u)

            for t in range(NT):
                dve.wait_ge(r_in[t % 2], 16 * (t // 2 + 1))
                v = ring[:, (t % 2) * 8192:(t % 2) * 8192 + 8192].rearrange("p (k n) -> p n k", k=TOPK)
                tail = qreg[:, (t % 2) * 1024:(t % 2) * 1024 + 1024]
                link(dve.tensor_reduce(tail, v, AX, ALU.add))
                dve.tensor_tensor(shy[:, t], shy[:, t], tail, ALU.add).then_inc(r_sum, 1)
                dve.wait_ge(r_rms, t + 1)
                dve.wait_ge(r_sum, t + 1)
                link(dve.scalar_tensor_tensor(shy[:, t], shy[:, t], nrm[:, 2, 14 + t:15 + t], grow[:, 1], ALU.mult, ALU.mult))
                dve.tensor_tensor(shy[:, t], shy[:, t], xres[:, t], ALU.add).then_inc(r_fin, 1)

        @block.gpsimd
        def _(pool):
            steps = [0]

            def link(ins):
                steps[0] += 1
                ins.then_inc(pool_step, 1)
                pool.wait_ge(pool_step, steps[0])

            link(pool.memset(mhalf[:], -0.5))

            def rms(i, ready):
                link(pool.tensor_scalar(nrm[:, 1, i:i + 1], nrm[:, 0, i:i + 1], 1.0 / D, EPS, ALU.mult, ALU.add))
                pool.tensor_tensor(nrm[:, 2, i:i + 1], nrm[:, 1, i:i + 1], mhalf[:], ALU.pow).then_inc(ready, 1)

            for t in range(NCT + NT):
                pool.wait_ge(squares, t + 1)
                rms(t, rms_ready)
            for step in plan_proj["pool"]:
                step(pool)

            def stage_q(n, h, qt):
                need(pool, s_done[1], n - 1)
                pool.tensor_tensor(qz[:, qt % 2], qT[:, at(h * NLAT + qt * P, P)].unsqueeze(1).broadcast_to([P, 2, P]),
                                   const[:, C_MAP:C_MAP + 2].unsqueeze(2).broadcast_to([P, 2, P]), ALU.mult)\
                    .then_inc(q_staged, 1)

            def o_rms_(n, qt):
                pool.wait_ge(o_square, n + 1)
                pool.sem_inc(pool_tick, 1)
                pool.tensor_scalar(stat[:, qt, 8:9], stat[:, qt, 7:8], 1.0 / VD, EPS, ALU.mult, ALU.add)\
                    .then_inc(pool_step, 1)
                pool.wait_ge(pool_step, n + (att0 + 1))
                pool.tensor_tensor(stat[:, qt, 9:10], stat[:, qt, 8:9], mhalf[:], ALU.pow).then_inc(o_rms, 1)

            att0 = steps[0]
            pool.wait_ge(g_done, NT)
            pool.wait_ge(turn_out, sum(1 for x in plan_proj["pe"] if x))
            stage_q(0, 0, 0)

            def pool_unit(h, u, last=False):
                n = h * NT + u
                first = isinstance(h, int) and h == 0
                if not last:
                    stage_q(n + 1, h + (1 if u == NT - 1 else 0), (u + 1) % NT)
                if not first or u >= 2:
                    o_rms_(n - 2, (u - 2) % 4)

            for u in range(NT):
                pool_unit(0, u)
            with pool.Fori(1, HEADS - 1) as h:
                for u in range(NT):
                    pool_unit(h, u)
            for u in range(NT):
                pool_unit(HEADS - 1, u, last=(u == NT - 1))
            o_rms_(UNITS - 2, 2)
            o_rms_(UNITS - 1, 3)
            steps[0] += UNITS
            for t in range(NT):
                pool.wait_ge(y_square, t + 1)
                rms(6 + t, y_rms)
                pool.wait_ge(x1_square, t + 1)
                rms(10 + t, x1_rms)
                pool.wait_ge(h_scaled, t + 1)
                pool.tensor_tensor(h2[:, t % 2], h2[:, t % 2], srow[:, 1], ALU.add).then_inc(h2_ready, 1)
            for t in range(NT):
                pool.wait_ge(s_up, t + 1)
                pool.wait_ge(s_gate, t + 1)
                if t >= 2:
                    pool.wait_ge(smt_done, t - 1)
                pool.tensor_tensor(hmid[:, t % 2], gsil[:, t % 2], sreg[:, 1024 + (t % 2) * DE:1024 + (t % 2) * DE + DE],
                                   ALU.mult).then_inc(s_mid, 1)

            def gather(b, u):
                pool.wait_ge(ids_ready, b + 1)
                pool.sem_inc(pool_tick, 1)
                pool.indirect_dma_start(xg[:, u % 2], None, h2_dram[:], bass.IndirectOffsetOnAxis(ids[:, u % U, 0:1], 0),
                                        bounds_check=NLAT - 1, oob_is_err=False).then_inc(xg_in[u % 2], 16)

            def pool_block(g, u):
                b = g * U + u
                first = isinstance(g, int) and b == 0
                pool.wait_ge(xt_done, b + 1)
                gather(b + 2, u + 2)
                if not first:
                    pool.wait_ge(y_act, b)
                    pool.wait_ge(y_dve, b)
                    pool.sem_inc(pool_tick, 1)
                    pool.indirect_dma_start(y_dram[:], bass.IndirectOffsetOnAxis(ids[:, (u - 1) % U, 1:2], 0),
                                            yb[:, (u - 1) % 2], None, bounds_check=NLAT * TOPK - 1,
                                            oob_is_err=False).then_inc(y_out[(u - 1) % 2], 16)

            for s in h2_stored:
                pool.wait_ge(s, 16 * NT // 2)
            pool.wait_ge(slots_ready, 1)
            gather(0, 0)
            gather(1, 1)
            for u in range(U):
                pool_block(0, u)
            pool.wait_ge(steer_ready, 1)
            turns = pool.value_load(steer[0:1, NB:NB + 1], min_val=1, max_val=TURNS)
            with pool.Fori(1, TURNS) as g:
                with pool.If(g < turns):
                    for u in range(U):
                        pool_block(g, u)
            counts = [pool.value_load(steer[0:1, NB + 1 + i:NB + 2 + i], min_val=0, max_val=16 * U * TURNS)
                      for i in range(3)]
            for x, i in ((y_out[0], 0), (y_out[1], 1), (xg_in[0], 2), (xg_in[1], 2)):
                pool.wait_ge(x, counts[i])
            pool.sem_inc(moe_done, 1)
            for t in range(NT):
                pool.wait_ge(r_square, t + 1)
                rms(14 + t, r_rms)


_OUT = ((1, NLAT, D), "float32")


def shape_tables():
    import numpy as np

    c = np.zeros((P, C_ALL), np.float32)
    p = np.arange(P)
    c[:, C_ID:C_ID + P] = np.eye(P)
    c[:, C_TRI:C_TRI + P] = p[:, None] < p[None, :]
    c[:, C_IOTA:C_IOTA + P] = p[None, :]
    g = np.arange(NGRP)
    c[:, C_LT:C_LT + 64] = (g[None, :] < g[:, None]).reshape(1, 64)
    t, k = np.arange(NT), np.arange(TOPK)
    c[:, C_V:C_V + 32] = ((t[None, :, None] * P + p[:, None, None]) * TOPK + k[None, None, :] + 1).reshape(P, 32)
    c[0:64, C_MAP], c[64:128, C_MAP + 1] = 1.0, 1.0
    j = np.arange(64)
    ang = 2 * np.pi * (np.outer(j, j) % 64) / 64
    for h in range(2):
        s = slice(64 * h, 64 * h + 64)
        c[s, C_CC + 64 * h:C_CC + 64 * h + 64] = np.cos(ang) / 8
        c[s, C_SC + 64 * h:C_SC + 64 * h + 64] = -np.sin(ang) / 8
    n = np.arange(NLAT)
    ang = 2 * np.pi * (np.outer(n, n) % NLAT) / NLAT
    d = np.stack([np.cos(ang), np.sin(ang)]) / np.sqrt(NLAT)
    dft = d.reshape(2, NT, P, NLAT).transpose(2, 0, 1, 3).reshape(P, 2 * NT * NLAT).astype(np.float32)
    inv = (10000.0 ** (-np.arange(0, 32, 2, dtype=np.float32) / np.float32(32))).astype(np.float32)
    pos = np.stack([n // 64, n % 64], -1).astype(np.float32)
    ang = (pos[:, :, None] * inv).astype(np.float32)
    cos, sin = np.cos(ang), np.sin(ang)
    rope = np.stack([np.stack([cos, cos], 2).reshape(NLAT, HD), np.stack([-sin, sin], 2).reshape(NLAT, HD)], 1)
    return {"consts": c, "dft": dft, "rope": rope.astype(np.float32)}


def kernel(**inputs):
    import numpy as np
    import concourse.bacc as bacc
    from concourse.bass_utils import run_bass_kernel_spmd

    nc = bacc.Bacc("TRN2", target_bir_lowering=False, num_devices=1)
    arrays, args = {}, {}
    for name, a in {**inputs, **shape_tables()}.items():
        a = np.ascontiguousarray(a)
        arrays[f"in_{name}"] = a
        args[name] = nc.dram_tensor(f"in_{name}", a.shape, mybir.dt.from_np(a.dtype), kind="ExternalInput").ap()
    args["out"] = nc.dram_tensor("out_x", _OUT[0], F32, kind="ExternalOutput").ap()
    build(nc, args)
    r = run_bass_kernel_spmd(nc, [arrays], core_ids=[0])
    return r.results[0]["out_x"]
```

```python
import math
from contextlib import ExitStack

import concourse.bass as bass
from concourse import mybir

F32 = mybir.dt.float32
I32 = mybir.dt.int32
U32 = mybir.dt.uint32
ALU = mybir.AluOpType
ACT = mybir.ActivationFunctionType
AX = mybir.AxisListType.X

P = 128
D = 1024
KC = D // P
NLAT, NCTX = 512, 256
NT = NLAT // P
NCT = NCTX // P
NTOK = NLAT + NCTX
FW = 256
HEADS, HD = 6, 64
VD = 2 * HD
QKW = HEADS * VD
NE, TOPK, NGRP, TOPG = 64, 8, 8, 4
GE = NE // NGRP
DE = 256
MIXC = (FW + QKW) // P
EPS = 1e-6
LAM0 = 0.8 - 0.6 * math.exp(-0.3 * 0)
ROUTED_SCALE = 2.5
UNITS = HEADS * NT
U = 4
MAXOV = NLAT * TOPK // P - 1
TURNS = NE // U + MAXOV
SPAN, SPANS = 6, 8
assert SPAN * SPANS >= TURNS - 1
NB = (TURNS + 1) * U
SKIP = 100000.0
GU_W = KC * DE
WBUF = 3 * GU_W
FRONT = 8 * 512
NFRONT = 5

C_ID, C_TRI, C_IOTA, C_LT, C_V, C_CC, C_SC = 0, 128, 256, 448, 512, 544, 672
C_MAP = 800
C_ROW = 802
C_ALL = 803


def at(index, size):
    return slice(index, index + size) if isinstance(index, int) else bass.ds(index, size)


def need(eng, sem, value):
    if not (isinstance(value, int) and value <= 0):
        eng.wait_ge(sem, value)


def build(nc, A):
    ctx = ExitStack()
    sb = lambda name, shape, dt=F32: ctx.enter_context(nc.sbuf_tensor(name, shape, dt))
    sem = lambda name: ctx.enter_context(nc.semaphore(name))
    with ctx:
        xres = sb("xres", [P, NT, D])
        heap = sb("heap", [P, 2 * WBUF + NFRONT * FRONT])
        ring = heap[:, 2 * WBUF:]
        hreg = sb("hreg", [P, KC * NTOK])
        sreg = sb("sreg", [P, 3072])
        freg = sb("freg", [P, 2560])
        grow = sb("grow", [P, 2, D])
        const = sb("const", [P, C_ALL])
        ones = sb("ones", [P, P])
        stat = sb("stat", [P, 4, 16])
        colc = sb("colc", [P, 2, KC])
        bmod = sb("bmod", [P, 6, KC])
        gain = sb("gain", [P, 4, KC])
        modc = sb("modc", [P, 6, KC, 2])
        scl1 = sb("scl1", [P, KC, 2])
        rowc = sb("rowc", [P, 4, KC])
        lam = sb("lam", [P, 8])
        gsub = sb("gsub", [P, 2])
        nrm = sb("nrm", [P, 3, 24])
        mhalf = sb("mhalf", [P, 1])
        wrt = sb("wrt", [P, KC, NE])
        rbias = sb("rbias", [P, NE])
        take = sb("take", [P, U], I32)
        put = sb("put", [P, U, 4], I32)
        ps = ctx.enter_context(nc.psum_tensor("ps", [P, 8, 512], F32))
        psf = ps[:].rearrange("p b n -> p (b n)")
        h2_dram = nc.dram_tensor("h2_rows", [NLAT, D], F32, kind="Internal").ap()
        y_dram = nc.dram_tensor("y_rows", [NLAT * TOPK, D], F32, kind="Internal").ap()

        hT = hreg[:].rearrange("p (c n) -> p c n", c=KC)
        mixT = hreg[:, 0:MIXC * NLAT]
        mixTv = mixT.rearrange("p (c n) -> p c n", c=MIXC)
        fg = hreg[:, 4096:6144].rearrange("p (t j s n) -> p t j s n", t=NT, j=2, s=2)
        hT2 = hreg[:, 0:KC * NLAT].rearrange("p (c n) -> p c n", c=KC)
        xg = hreg[:, 4096:6144].rearrange("p (s n) -> p s n", s=2)
        qreg = heap[:, 0:2 * WBUF]
        xn = qreg[:, 0:6144].rearrange("p (t n) -> p t n", t=NCT + NT)
        qT = qreg[:, 0:3072]
        kT = qreg[:, 3072:7680]
        vt = qreg[:, 7680:12288].rearrange("p (t n) -> p t n", t=NCT + NT)
        tmp1 = qreg[:, 6144:7168]
        h2 = qreg[:, 7168:9216].rearrange("p (s n) -> p s n", s=2)
        shy = qreg[:, 0:4096].rearrange("p (t n) -> p t n", t=NT)
        rt = qreg[:, 4096:6144]
        gsum, rank, idxf, skf, wkf, pf, bf = (rt[:, 1792 + 32 * i:1824 + 32 * i] for i in range(7))
        slots = rt[:, 0:5 * NB].bitcast(I32).rearrange("p (b k) -> p b k", k=5)
        steer = rt[0:1, 1408:1408 + NB + 3].bitcast(I32)
        table = rt[:, 1024:1024 + 2 * NB]
        prob = sreg[:].rearrange("p (s m n) -> p s m n", s=2, m=2)
        xctx = sreg[:, 0:2048].rearrange("p (t n) -> p t n", t=NCT)
        ropeA = sreg[:, 0:1024].rearrange("p (s n) -> p s n", s=2)
        ropeB = sreg[:, 1024:2048].rearrange("p (s n) -> p s n", s=2)
        srow = sreg[:, 0:2048].rearrange("p (s n) -> p s n", s=2)
        xgT = sreg[:, 0:2048].rearrange("p (s c n) -> p s c n", s=2, c=KC)
        hmid = sreg[:, 2048:2560].rearrange("p (s n) -> p s n", s=2)
        hmT = sreg[:, 2560:3072].rearrange("p (s c n) -> p s c n", s=2, c=2)
        lamv = sreg[:, 2048:2304].rearrange("p (i d) -> p i d", i=4)
        wbd = sreg[:, 2304:2560].rearrange("p (j n) -> p j n", j=2)
        bd = sreg[:, 2560:3072].rearrange("p (j s n) -> p j s n", j=2, s=2)
        ropet = freg[:, 1024:1536].rearrange("p (t s d) -> p t s d", t=NT, s=2)
        qz = freg[:, 0:512].rearrange("p (s m n) -> p s m n", s=2, m=2)
        onrm = freg[:, 512:768].rearrange("p (s n) -> p s n", s=2)
        junk = freg[:, 768:896]
        silc = grow[:, 1, 0:256].rearrange("p (c s) -> p c s", c=KC)
        osb = grow[:, 1, 256:512].rearrange("p (s n) -> p s n", s=2)
        FT = freg[:, 0:1024].rearrange("p (j n) -> p j n", j=2)
        aT = freg[:, 1024:2560].rearrange("p (s n) -> p s n", s=2)
        sq = freg[:, 1024:2048]
        yb = freg[:, 0:2048].rearrange("p (s n) -> p s n", s=2)
        gsil = freg[:, 2048:2560].rearrange("p (s n) -> p s n", s=2)

        ident = const[:, C_ID:C_ID + P]
        tri = const[:, C_TRI:C_TRI + P]
        iota = const[:, C_IOTA:C_IOTA + NB]

        small_in = sem("small_in")
        wbd_zero, wbd_in = sem("wbd_zero"), sem("wbd_in")
        x_in = [sem(f"x_in{t}") for t in range(NCT + NT)]
        item_in = [sem(f"item_in{s}") for s in range(NFRONT)]
        dve_step, pool_step = sem("dve_step"), sem("pool_step")
        setup = sem("setup")
        silc_ready, lam_sum, lam_exp = sem("silc_ready"), sem("lam_sum"), sem("lam_exp")
        squares, rms_ready, xn_ready = sem("squares"), sem("rms_ready"), sem("xn_ready")
        bd_done, bd_ready = sem("bd_done"), sem("bd_ready")
        mod_done, mod_ready = sem("mod_done"), sem("mod_ready")
        tlat_done, tctx_done = sem("tlat_done"), sem("tctx_done")
        hlat_ready, hctx_ready = sem("hlat_ready"), sem("hctx_ready")
        proj_done, roped, rope_sum, copied = sem("proj_done"), sem("roped"), sem("rope_sum"), sem("copied")
        turn_done, turn_out = sem("turn_done"), sem("turn_out")
        g_done, g_ready, fmix_done, fmix_ready = sem("g_done"), sem("g_ready"), sem("fmix_done"), sem("fmix_ready")
        q_staged = sem("q_staged")
        s_done = [sem("s_done0"), sem("s_done1")]
        nmax = [sem("nmax0"), sem("nmax1")]
        exped = [sem("exped0"), sem("exped1")]
        combined, at_done = sem("combined"), sem("at_done")
        at_out = [sem("at_out_act"), sem("at_out_dve")]
        pv_done, o_copied, o_square, o_rms, o_normed = sem("pv_done"), sem("o_copied"), sem("o_square"), sem("o_rms"), sem("o_normed")
        ot_done, ot_out = sem("ot_done"), sem("ot_out")
        rowc_ready, row_done = sem("rowc_ready"), sem("row_done")
        row_out = [sem("row_out_act"), sem("row_out_dve")]
        pool_tick = sem("pool_tick")
        wo_done, y_square, y_rms, y_scaled, x1_ready = (sem(n) for n in ("wo_done", "y_square", "y_rms", "y_scaled", "x1_ready"))
        x1_square, x1_rms, h_scaled, h2_ready = (sem(n) for n in ("x1_square", "x1_rms", "h_scaled", "h2_ready"))
        h2_stored = [sem("h2_stored0"), sem("h2_stored1")]
        h2t_done, h2t_act, h2t_dve = sem("h2t_done"), sem("h2t_act"), sem("h2t_dve")
        logits_done, scores_ready, mask_ready, pos_done = sem("logits_done"), sem("scores_ready"), sem("mask_ready"), sem("pos_done")
        place_ready, places, table_copied, table_spread, xg_zero = (
            sem(n) for n in ("place_ready", "places", "table_copied", "table_spread", "xg_zero"))
        hot_ready, hot_used, slots_ready, steer_ready = sem("hot_ready"), sem("hot_used"), sem("slots_ready"), sem("steer_ready")
        sgu_done, s_gate, s_up, s_mid, smt_done, smt_out, sy_done, sy_out = (
            sem(n) for n in ("sgu_done", "s_gate", "s_up", "s_mid", "smt_done", "smt_out", "sy_done", "sy_out"))
        w_in = [sem(f"w_in{s}") for s in range(U)]
        take_ready, put_ready = sem("take_ready"), sem("put_ready")
        xg_in = [sem("xg_in0"), sem("xg_in1")]
        gu_done, gate_ready, mid_ready = sem("gu_done"), sem("gate_ready"), sem("mid_ready")
        mt_done, mt_out = sem("mt_done"), sem("mt_out")
        xt_done, xt_act, xt_dve = sem("xt_done"), sem("xt_act"), sem("xt_dve")
        dn_done, y_act, y_dve = sem("dn_done"), sem("y_act"), sem("y_dve")
        y_out = [sem("y_out0"), sem("y_out1")]
        moe_done = sem("moe_done")
        r_in = [sem(f"r_in{s}") for s in range(2)]
        r_sum, r_square, r_rms, r_scaled, r_fin, stored = (sem(n) for n in ("r_sum", "r_square", "r_rms", "r_scaled", "r_fin", "stored"))

        CHUNK_TILES = [range(2, 6), range(2, 6), range(6), range(6), range(6)]
        proj_units = [(c, t) for c in range(5) for t in CHUNK_TILES[c]]
        chunk_end = [max(i for i, (c, _) in enumerate(proj_units) if c == k) + 1 for k in range(5)]
        mod_items = lambda m: [(f"mod{m}{h}", mod_done, m + 1) for h in range(2)]
        items = mod_items(0) + mod_items(1) + [(f"win{c}", proj_done, chunk_end[c]) for c in range(5)]
        items += [("dft", fmix_done, 2)]
        for m in range(2, 6):
            items += mod_items(m)
        items += [("wo0", wo_done, NT), ("wo1", wo_done, NT), ("shgu", sgu_done, NT), ("shd", sy_done, NT)]
        place = {name: i for i, (name, _, _) in enumerate(items)}

        def item(name):
            s = place[name] % NFRONT
            return ring[:, s * FRONT:(s + 1) * FRONT]

        def item_landed(eng, name):
            i = place[name]
            eng.wait_ge(item_in[i % NFRONT], 16 * (i // NFRONT + 1))

        def source(name):
            if name.startswith("mod"):
                m, h = int(name[3]), int(name[4])
                w = A["w_mod"][0].rearrange("(p c) n -> p c n", c=KC)
                return [(item(name).rearrange("p (c n) -> p c n", c=4), w[:, 4 * h:4 * h + 4, m * D:(m + 1) * D])]
            if name.startswith("win"):
                c = int(name[3])
                w = A["w_in"][0].rearrange("(p c) n -> p c n", c=KC)
                return [(item(name).rearrange("p (c n) -> p c n", c=KC), w[:, :, c * 512:(c + 1) * 512])]
            if name == "dft":
                return [(item(name), A["dft"])]
            if name.startswith("wo"):
                n = int(name[2])
                w = A["w_out"][0].rearrange("(c p) n -> p c n", p=P)
                return [(item(name).rearrange("p (c n) -> p c n", c=MIXC), w[:, :, n * 512:(n + 1) * 512])]
            if name == "shgu":
                v = item(name).rearrange("p (s n) -> p s n", s=2)
                return [(v[:, 0], A["ws_gate"][0].rearrange("(p c) n -> p (c n)", c=KC)),
                        (v[:, 1], A["ws_up"][0].rearrange("(p c) n -> p (c n)", c=KC))]
            return [(item(name)[:, 0:GU_W], A["ws_down"][0].rearrange("(p c) n -> p (c n)", c=2))]

        def landed_shared(eng):
            i = place["shgu"]
            eng.wait_ge(item_in[i % NFRONT], 16 * (i // NFRONT + 2))

        def wbuf(s):
            k = 1 + (s + 2) % U
            return heap[:, k * WBUF:(k + 1) * WBUF]

        def gate_up(buf):
            return buf[:, 0:2 * GU_W].rearrange("p (w c n) -> p w c n", w=2, c=KC)

        def down(buf):
            return buf[:, 2 * GU_W:].rearrange("p (c n) -> p c n", c=2)

        def done_scatters(g, u):
            k = (u - 3) // 2 + 1 if (u - 1) % 2 == 0 else (u - 4) // 2 + 1
            return g * (32 * U // 2) + 32 * k

        def halves(bank):
            return ps[:, bank].rearrange("p (a w n) -> p a w n", a=2, w=2)

        def hot(t):
            area = (qreg[:, WBUF:], hreg[:, 0:TOPK * (P + 2 * NB)])[t % 2]
            ph = area[:, 0:TOPK * P].rearrange("p (k n) -> p k n", k=TOPK)
            bvw = area[:, TOPK * P:TOPK * (P + 2 * NB)].rearrange("p (k n) -> p k n", k=TOPK)
            return ph, bvw

        def proj_plan():
            pe_turns, act_steps, dve_steps, pool_steps = [], [], [], []
            n_rope = n_copy = n_turn = 0
            unit_free = []
            for i, (c, t) in enumerate(proj_units):
                bank, tok = i % 4, t * P
                rope = t >= NCT and c < 4
                width = (512, 512, 512, 256, 0)[c]
                slot = n_turn % 2
                if rope:
                    n_rope += 1
                    unit_free.append((roped, n_rope))

                    def dve_step_(e, i=i, c=c, t=t, bank=bank, width=width, slot=slot, n=n_turn):
                        e.wait_ge(proj_done, i + 1)
                        if n >= 2:
                            e.wait_ge(turn_done, n - 1)
                        lo = FW if c == 0 else 0
                        g = (width - lo) // HD
                        src = ps[:, bank, lo:width]
                        a, b = ropeA[:, slot, lo:width], ropeB[:, slot, lo:width]
                        cs = ropet[:, t - NCT, 0].unsqueeze(1).broadcast_to([P, g, HD])
                        sn = ropet[:, t - NCT, 1].rearrange("p (a h i) -> p a h i", a=2, h=2)
                        e.tensor_tensor(a.rearrange("p (g d) -> p g d", d=HD), src.rearrange("p (g d) -> p g d", d=HD),
                                        cs, ALU.mult)
                        sv = src.rearrange("p (g a h i) -> p g a h i", a=2, h=2, i=16)
                        bv = b.rearrange("p (g a h i) -> p g a h i", a=2, h=2, i=16)
                        if c == 0:
                            e.tensor_copy(ropeA[:, slot, 0:FW], ps[:, bank, 0:FW])
                        if c == 3:
                            e.tensor_copy(vt[:, t, 0:256], ps[:, bank, 256:512])
                        for x in range(2):
                            snx = sn[:, x].unsqueeze(1).broadcast_to([P, g, 2, 16])
                            for half in range(2):
                                snh = sn[:, x, half].unsqueeze(1).broadcast_to([P, g, 16])
                                last = e.tensor_tensor(bv[:, :, x, half], sv[:, :, x, 1 - half], snh, ALU.mult)
                        last.then_inc(roped, 1)

                    dve_steps.append(dve_step_)

                    def pool_step_(e, c=c, width=width, slot=slot, n=n_rope):
                        e.wait_ge(roped, n)
                        lo = FW if c == 0 else 0
                        a, b = ropeA[:, slot, lo:width], ropeB[:, slot, lo:width]
                        e.tensor_tensor(a, a, b, ALU.add).then_inc(rope_sum, 1)

                    pool_steps.append(pool_step_)
                    staged = (rope_sum, n_rope)
                else:
                    n_copy += 1
                    unit_free.append((copied, n_copy))

                    def copy_step(e, i=i, c=c, t=t, bank=bank, width=width, slot=slot, n=n_turn):
                        e.wait_ge(proj_done, i + 1)
                        if width and n >= 2:
                            e.wait_ge(turn_done, n - 1)
                        if width:
                            last = e.activation(ropeA[:, slot, 0:width], ps[:, bank, 0:width], ACT.Copy)
                        if width < 512:
                            v0 = 0 if c == 3 else 256
                            last = e.activation(vt[:, t, v0:v0 + 512 - width], ps[:, bank, width:512], ACT.Copy)
                        last.then_inc(copied, 1)

                    act_steps.append(copy_step)
                    staged = (copied, n_copy)
                if width:
                    n_turn += 1
                    pe_turns.append((i, slot, width // P, staged))

                    def turn_out_step(e, c=c, t=t, width=width, n=n_turn):
                        e.wait_ge(turn_done, n)
                        bank = 4 + (n - 1) % 2
                        v = ps[:, bank].rearrange("p (h n) -> p h n", h=4)
                        tl = (t - NCT) * P
                        qv = qT.rearrange("p (h n) -> p h n", h=HEADS)
                        kv = kT.rearrange("p (h n) -> p h n", h=HEADS)
                        if c == 0:
                            e.activation(FT[:, :, tl:tl + P], v[:, 0:2], ACT.Copy)
                            last = e.activation(qv[:, 0:2, tl:tl + P], v[:, 2:4], ACT.Copy, scale=HD ** -0.5)
                        elif c == 1:
                            last = e.activation(qv[:, 2:6, tl:tl + P], v, ACT.Copy, scale=HD ** -0.5)
                        elif c == 2:
                            last = e.activation(kv[:, 0:4, t * P:(t + 1) * P], v, ACT.Copy)
                        else:
                            last = e.activation(kv[:, 4:6, t * P:(t + 1) * P], v[:, 0:2], ACT.Copy)
                        last.then_inc(turn_out, 1)

                    act_steps.append(turn_out_step)
                else:
                    pe_turns.append(None)
            return {"pe": pe_turns, "act": act_steps, "dve": dve_steps, "pool": pool_steps, "free": unit_free}

        plan_proj = proj_plan()

        NSMALL = 16
        block = ctx.enter_context(nc.Block())

        @block.sync
        def _(sp):
            xl = A["x"][0].rearrange("(t p) n -> t p n", p=P)
            xc = A["ctx"][0].rearrange("(t p) n -> t p n", p=P)
            for t in range(NCT):
                sp.dma_start(xctx[:, t], xc[t]).then_inc(x_in[t], 16)
            for t in range(NT):
                sp.dma_start(xres[:, t], xl[t]).then_inc(x_in[NCT + t], 16)
            for i, (name, _, _) in enumerate(items):
                if i >= NFRONT:
                    _, used, count = items[i - NFRONT]
                    sp.wait_ge(used, count)
                for dst, src in source(name):
                    sp.dma_start(dst, src).then_inc(item_in[i % NFRONT], 16)
                if name == "shd":
                    break
            for t in range(NT):
                sp.wait_ge(h2_ready, t + 1)
                sp.dma_start(h2_dram[t * P:(t + 1) * P, :], h2[:, t % 2]).then_inc(h2_stored[t % 2], 16)

            def load_expert(s, e):
                v = gate_up(wbuf(s))
                sp.dma_start(v[:, 0], A["w_gate"][0, e].rearrange("(p c) n -> p c n", c=KC)).then_inc(w_in[s], 16)
                sp.dma_start(v[:, 1], A["w_up"][0, e].rearrange("(p c) n -> p c n", c=KC)).then_inc(w_in[s], 16)
                sp.dma_start(down(wbuf(s)), A["w_down"][0, e].rearrange("(c p) n -> p c n", c=2)).then_inc(w_in[s], 16)

            load_expert(0, 0)
            load_expert(1, 1)
            sp.wait_ge(sgu_done, NT)
            sp.wait_ge(sy_done, NT)
            load_expert(3, 3)
            sp.wait_ge(hot_used, NT)
            load_expert(2, 2)
            sp.wait_ge(steer_ready, 1)
            turns = sp.value_load(steer[0:1, NB:NB + 1], min_val=0, max_val=TURNS - 1) + 1
            with sp.Fori(0, SPANS) as q:
                with sp.If(q * SPAN + 1 < turns):
                    with sp.Fori(1, SPAN + 1) as i:
                        g = (q * SPAN + i).with_bounds(min_val=1, max_val=TURNS - 1)
                        with sp.If(g < turns):
                            for u in range(U):
                                code = [sp.value_load(steer[0:1, at(u * (NB // U) + g - i, 1)], min_val=0,
                                                      max_val=2 * (NE // U) - 1) for i in range(2)]
                                sp.wait_ge(dn_done, g * U + (u - U + 1))
                                with sp.If((code[0] >> 1) > (code[1] >> 1)):
                                    e = (code[0] >> 1).with_bounds(min_val=1, max_val=NE // U - 1) * U + u
                                    v = gate_up(wbuf(u))
                                    for k, name in enumerate(("w_gate", "w_up")):
                                        w = A[name][0].rearrange("e (p c) n -> p e (c n)", c=KC)
                                        sp.dma_start(v[:, k].rearrange("p c n -> p (c n)").unsqueeze(1),
                                                     w[:, bass.ds(e, 1)]).then_inc(w_in[u], 16)
                                    w = A["w_down"][0].rearrange("e (c p) n -> p e c n", c=2)
                                    sp.dma_start(down(wbuf(u)).unsqueeze(1), w[:, bass.ds(e, 1)]).then_inc(w_in[u], 16)
            sp.wait_ge(moe_done, 1)
            yv = y_dram.rearrange("(t p k) n -> t p (k n)", p=P, k=TOPK)
            for t in range(NT):
                if t >= 2:
                    sp.wait_ge(r_sum, t - 1)
                sp.dma_start(ring[:, (t % 2) * 8192:(t % 2) * 8192 + 8192], yv[t]).then_inc(r_in[t % 2], 16)
            for t in range(NT):
                sp.wait_ge(r_fin, t + 1)
                sp.dma_start(A["out"][0, t * P:(t + 1) * P, :], shy[:, t]).then_inc(stored, 16)
            sp.wait_ge(stored, 16 * NT)
            for s in h2_stored:
                sp.wait_ge(s, 16 * NT // 2)

        @block.scalar
        def _(act):
            col = lambda a: a.rearrange("(p c) -> p c", c=KC)
            loads = [(const[:], A["consts"]), (colc[:, 0], col(A["c"][0])), (colc[:, 1], col(A["c_ctx"])),
                     (bmod[:], A["b_mod"][0].rearrange("(m p c) -> p m c", m=6, c=KC)),
                     (gain[:, 0], col(A["g_attn_pre"][0])), (gain[:, 1], col(A["g_attn_post"][0])),
                     (gain[:, 2], col(A["g_ffn_pre"][0])), (gain[:, 3], col(A["g_ffn_post"][0])),
                     (ropet, A["rope"].rearrange("(t p) s n -> p t s n", p=P)),
                     (gsub[:, 0:1], A["g_subln"][0].rearrange("(p c) -> p c", c=1)),
                     (wrt[:], A["w_router"][0].rearrange("(p c) n -> p c n", c=KC)),
                     (rbias[:], A["router_bias"][0].partition_broadcast(P))]
            loads += [(lamv[:, i], A[n][0].partition_broadcast(P))
                      for i, n in enumerate(("lambda_q1", "lambda_k1", "lambda_q2", "lambda_k2"))]
            assert len(loads) == NSMALL
            for dst, src in loads:
                act.dma_start(dst, src).then_inc(small_in, 16)
            act.wait_ge(wbd_zero, 1)
            for g in range(4):
                r = slice(64 * (g % 2), 64 * (g % 2) + 64)
                act.dma_start(wbd[r, g // 2, r], A["w_fourier"][0, g]).then_inc(wbd_in, 16)
            act.wait_ge(small_in, 16 * NSMALL)
            act.wait_ge(wbd_zero, 2)
            act.activation(silc[:, :, 0:2].rearrange("p c s -> p s c"), colc[:], ACT.Silu).then_inc(silc_ready, 1)
            for t in range(NCT + NT):
                act.wait_ge(x_in[t], 16)
                src = xctx[:, t] if t < NCT else xres[:, t - NCT]
                act.activation(xn[:, t], src, ACT.Square, accum_out=nrm[:, 0, t:t + 1]).then_inc(squares, 1)
            act.wait_ge(lam_sum, 1)
            act.activation(lam[:, 2:4], lam[:, 0:2], ACT.Exp).then_inc(lam_exp, 1)
            act.wait_ge(mod_ready, 3)
            for c in range(KC):
                act.wait_ge(tctx_done, c + 1)
                act.activation(hT[:, c, 0:NCTX], ps[:, 2 + c % 2, 0:NCTX], ACT.Identity,
                               bias=modc[:, 0, c, 1:2], scale=scl1[:, c, 1:2]).then_inc(hctx_ready, 1)
            for step in plan_proj["act"]:
                step(act)
            for t in range(0, NT, 2):
                act.wait_ge(g_done, t + 1)
                act.activation(fg[:, t].rearrange("p j s n -> p (j s n)"), ps[:, t], ACT.Copy).then_inc(g_ready, 1)
            act.wait_ge(fmix_done, 2)
            for j in range(2):
                act.activation(mixTv[:, j], ps[:, 4 + j], ACT.Copy).then_inc(fmix_ready, 1)

            def exps(n, h, qt):
                need(act, at_done, n - 1)
                for m in range(2):
                    act.wait_ge(nmax[m], n + 1)
                    act.activation(prob[:, qt % 2, m], psf[:, 1024 * m:1024 * m + NTOK], ACT.Exp,
                                   bias=stat[:, qt, m:m + 1], accum_out=stat[:, qt, 2 + m:3 + m]).then_inc(exped[m], 1)

            def at_evac(n, qt):
                act.wait_ge(at_done, n + 1)
                act.activation(aT[:, qt % 2, 0:512], ps[:, 4], ACT.Copy).then_inc(at_out[0], 1)

            def square(n, qt):
                act.wait_ge(pv_done, n + 1)
                act.wait_ge(combined, n + 1)
                act.activation(osb[:, qt % 2], ps[:, 6, 0:VD], ACT.Copy, scale=stat[:, qt, 4:5]).then_inc(o_copied, 1)
                act.wait_ge(o_copied, n + 1)
                act.activation(junk, osb[:, qt % 2], ACT.Square, accum_out=stat[:, qt, 7:8]).then_inc(o_square, 1)

            def ot_evac(n, h, qt):
                act.wait_ge(ot_done, n + 1)
                act.activation(mixT[:, at((2 + h) * NLAT + qt * P, P)], ps[:, 7, 0:P], ACT.Copy,
                               scale=gsub[:, 1:2]).then_inc(ot_out, 1)

            def act_unit(h, u):
                n = h * NT + u
                first = isinstance(h, int) and h == 0
                if not first or u >= 2:
                    at_evac(n - 2, (u - 2) % 4)
                exps(n, h, u)
                if not first or u >= 3:
                    square(n - 3, (u - 3) % 4)
                if not first:
                    ot_evac(n - 4, h - 1, u)

            act.wait_ge(setup, 1)
            for u in range(NT):
                act_unit(0, u)
            with act.Fori(1, HEADS) as h:
                for u in range(NT):
                    act_unit(h, u)
            at_evac(UNITS - 2, 2)
            square(UNITS - 3, 1)
            ot_evac(UNITS - 4, HEADS - 1, 0)
            at_evac(UNITS - 1, 3)
            square(UNITS - 2, 2)
            ot_evac(UNITS - 3, HEADS - 1, 1)
            square(UNITS - 1, 3)
            ot_evac(UNITS - 2, HEADS - 1, 2)
            ot_evac(UNITS - 1, HEADS - 1, 3)

            for i in range(0, 8, 2):
                act.wait_ge(row_done, i + 1)
                row_dst = (grow[:, 0], srow[:, 0], srow[:, 1], grow[:, 1])[i // 2]
                act.activation(row_dst.rearrange("p (j c) -> p c j", c=KC)[:, 0:4],
                               ps[:, 4].rearrange("p (c j) -> p c j", c=4), ACT.Copy).then_inc(row_out[0], 1)

            def h2t_evac(t):
                act.wait_ge(h2t_done, t + 1)
                act.activation(hT2[:, 0:4, t * P:(t + 1) * P], ps[:, 4].rearrange("p (c n) -> p c n", c=4), ACT.Copy)\
                    .then_inc(h2t_act, 1)

            for t in range(NT):
                act.wait_ge(wo_done, t + 1)
                b = 2 * (t % 2)
                act.activation(sq, psf[:, b * 512:b * 512 + D], ACT.Square, accum_out=nrm[:, 0, 6 + t:7 + t])\
                   .then_inc(y_square, 1)
                act.wait_ge(x1_ready, t + 1)
                act.wait_ge(y_square, t + 1)
                act.activation(sq, xres[:, t], ACT.Square, accum_out=nrm[:, 0, 10 + t:11 + t]).then_inc(x1_square, 1)
                act.wait_ge(x1_square, t + 1)
                if t >= 2:
                    h2t_evac(t - 2)
            h2t_evac(NT - 2)
            h2t_evac(NT - 1)
            act.wait_ge(logits_done, 1)
            act.activation(rt[:, 0:256], ps[:, 7, 0:256], ACT.Sigmoid).then_inc(scores_ready, 1)

            def shared_gate(t):
                act.wait_ge(sgu_done, t + 1)
                if t >= 2:
                    act.wait_ge(s_mid, t - 1)
                act.activation(gsil[:, t % 2], ps[:, t % 2, 0:DE], ACT.Silu).then_inc(s_gate, 1)
                act.activation(sreg[:, 1024 + (t % 2) * DE:1024 + (t % 2) * DE + DE], ps[:, t % 2, DE:2 * DE], ACT.Copy)\
                   .then_inc(s_up, 1)

            def shared_out(t):
                act.wait_ge(smt_done, t + 1)
                act.activation(hmT[:, t % 2], ps[:, 6, 0:256].rearrange("p (c n) -> p c n", c=2), ACT.Copy)\
                   .then_inc(smt_out, 1)

            def shared_y(t):
                act.wait_ge(sy_done, t + 1)
                act.activation(shy[:, t], psf[:, 1024:2048], ACT.Copy).then_inc(sy_out, 1)

            for t in range(NT):
                shared_gate(t)
                if t:
                    shared_out(t - 1)
                    shared_y(t - 1)
            shared_out(NT - 1)
            shared_y(NT - 1)

            def x_evac(n, s):
                act.wait_ge(xt_done, n + 1)
                act.activation(xgT[:, s, 0:4], ps[:, 4].rearrange("p (c n) -> p c n", c=4), ACT.Copy)\
                   .then_inc(xt_act, 1)

            def mid_evac(n, s):
                act.wait_ge(mt_done, n + 1)
                act.activation(hmT[:, s], ps[:, 6, 0:256].rearrange("p (c n) -> p c n", c=2), ACT.Copy)\
                   .then_inc(mt_out, 1)

            def y_evac(b, u):
                act.wait_ge(put_ready, b + 1)
                act.wait_ge(dn_done, b + 1)
                w = put[:, u, 2:3].bitcast(F32)
                act.activation(yb[:, u % 2, 0:512], ps[:, 2], ACT.Copy, scale=w).then_inc(y_act, 1)

            def act_block(g, u):
                b = g * U + u
                first = isinstance(g, int) and b == 0
                if not first:
                    mid_evac(b - 1, (u - 1) % 2)
                act.wait_ge(gu_done, b + 1)
                act.activation(gsil[:, u % 2].rearrange("p (a n) -> p a n", a=2), halves(u % 2)[:, :, 0], ACT.Silu)\
                    .then_inc(gate_ready, 1)
                x_evac(b + 1, (u + 1) % 2)
                if not first:
                    need(act, y_out[(u - 1) % 2], done_scatters(g, u))
                    y_evac(b - 1, (u - 1) % U)

            def act_ending(g):
                mid_evac(g * U - 1, 1)
                act.wait_ge(y_out[1], done_scatters(g, 0))
                y_evac(g * U - 1, U - 1)

            x_evac(0, 0)
            for u in range(U):
                act_block(0, u)
            act.wait_ge(steer_ready, 1)
            turns = act.value_load(steer[0:1, NB:NB + 1], min_val=0, max_val=TURNS - 1) + 1
            with act.Fori(0, SPANS) as q:
                with act.If(q * SPAN + 1 < turns):
                    with act.Fori(1, SPAN + 1) as i:
                        g = (q * SPAN + i).with_bounds(min_val=1, max_val=TURNS - 1)
                        with act.If(g < turns):
                            for u in range(U):
                                act_block(g, u)
            act_ending(turns)
            for t in range(NT):
                act.wait_ge(r_sum, t + 1)
                act.activation(sreg[:, 0:1024], shy[:, t], ACT.Square, accum_out=nrm[:, 0, 14 + t:15 + t])\
                   .then_inc(r_square, 1)
                act.wait_ge(r_square, t + 1)

        @block.tensor
        def _(pe):
            mm = nc.tensor.matmul
            pe.wait_ge(small_in, 16 * NSMALL)
            pe.wait_ge(wbd_in, 64)
            for j in range(2):
                for s in range(2):
                    last = mm(ps[:, 7, (2 * j + s) * P:(2 * j + s + 1) * P],
                              const[:, (C_CC, C_SC)[s]:(C_CC, C_SC)[s] + P], wbd[:, j], start=True, stop=True)
            last.then_inc(bd_done, 1)

            def modulation(m):
                item_landed(pe, f"mod{m}0")
                item_landed(pe, f"mod{m}1")
                if m >= 1:
                    pe.wait_ge(*((bd_ready, 1) if m == 1 else (mod_ready, m - 1 if m < 4 else m)))
                w = [item(f"mod{m}{h}").rearrange("p (k n) -> p k n", k=4) for h in range(2)]
                for k in range(KC):
                    for g in range(4):
                        last = mm(ps[32 * g:32 * g + 32, 6 + m % 2, 0:256], silc[:, k],
                                  w[k // 4][:, k % 4, 256 * g:256 * g + 256], start=(k == 0), stop=(k == KC - 1))
                last.then_inc(mod_done, 1)

            pe.wait_ge(silc_ready, 1)
            modulation(0)
            modulation(1)
            pe.wait_ge(xn_ready, NCT + NT)
            for c in range(KC):
                if c >= 2:
                    pe.wait_ge(hlat_ready, c - 1)
                    pe.wait_ge(hctx_ready, c - 1)
                for t in range(NCT + NT):
                    out = ps[:, 2 + c % 2, t * P:(t + 1) * P] if t < NCT else \
                        ps[:, c % 2, (t - NCT) * P:(t - NCT + 1) * P]
                    v = xn[:, t].rearrange("p (j c) -> p j c", c=KC)[:, :, c]
                    last = nc.tensor.transpose(out, v, ident)
                    if t == NCT - 1:
                        last.then_inc(tctx_done, 1)
                last.then_inc(tlat_done, 1)
            pe.wait_ge(hlat_ready, KC)
            pe.wait_ge(hctx_ready, KC)
            turns = plan_proj["pe"]
            n_turn = 0

            def turn(k):
                nonlocal n_turn
                if turns[k] is None:
                    return
                _, slot, nh, staged = turns[k]
                pe.wait_ge(*staged)
                if n_turn >= 2:
                    pe.wait_ge(turn_out, n_turn - 1)
                for x in range(nh):
                    last = nc.tensor.transpose(ps[:, 4 + n_turn % 2, x * P:(x + 1) * P],
                                               ropeA[:, slot, x * P:(x + 1) * P], ident)
                last.then_inc(turn_done, 1)
                n_turn += 1

            for i, (c, t) in enumerate(proj_units):
                item_landed(pe, f"win{c}")
                if i >= 4:
                    pe.wait_ge(*plan_proj["free"][i - 4])
                w = item(f"win{c}").rearrange("p (c n) -> p c n", c=KC)
                for k in range(KC):
                    last = mm(ps[:, i % 4], hT[:, k, t * P:(t + 1) * P], w[:, k], start=(k == 0), stop=(k == KC - 1))
                last.then_inc(proj_done, 1)
                if i:
                    turn(i - 1)
            turn(len(proj_units) - 1)
            pe.wait_ge(*plan_proj["free"][-1])
            pe.wait_ge(roped, sum(1 for s, _ in plan_proj["free"] if s is roped))
            pe.wait_ge(turn_out, n_turn)
            pe.wait_ge(bd_ready, 1)
            for t in range(NT):
                for j in range(2):
                    last = mm(ps[:, t, 256 * j:256 * j + 256], FT[:, j, t * P:(t + 1) * P],
                              bd[:, j].rearrange("p s n -> p (s n)"), start=True, stop=True)
                last.then_inc(g_done, 1)
            item_landed(pe, "dft")
            dft = item("dft").rearrange("p (s t n) -> p s t n", s=2, t=NT)
            pe.wait_ge(g_ready, NT)
            for j in range(2):
                for t in range(NT):
                    for s in range(2):
                        last = mm(ps[:, 4 + j], fg[:, t, j, s], dft[:, s, t], start=(t == 0 and s == 0),
                                  stop=(t == NT - 1 and s == 1))
                last.then_inc(fmix_done, 1)
            for m in range(2, 6):
                modulation(m)

            def scores(n, h, qt, m):
                if m == 0:
                    pe.wait_ge(q_staged, n + 1)
                need(pe, exped[m], n)
                mm(ps[:, 2 * m], qz[:, qt % 2, m], kT[:, at(h * NTOK, 512)], start=True, stop=True)
                mm(ps[:, 2 * m + 1, 0:256], qz[:, qt % 2, m], kT[:, at(h * NTOK + 512, 256)],
                   start=True, stop=True).then_inc(s_done[m], 1)

            def values(n, h, qt):
                pe.wait_ge(at_out[0], n + 1)
                pe.wait_ge(at_out[1], n + 1)
                need(pe, o_copied, n)
                for k in range(NCT + NT):
                    last = mm(ps[:, 6, 0:VD], aT[:, qt % 2, k * P:(k + 1) * P], vt[:, k, at(h * VD, VD)],
                              start=(k == 0), stop=(k == NCT + NT - 1))
                last.then_inc(pv_done, 1)

            def turn_probs(n, qt):
                pe.wait_ge(combined, n + 1)
                need(pe, at_out[0], n)
                need(pe, at_out[1], n)
                for k in range(NCT + NT):
                    last = nc.tensor.transpose(psf[:, 2048 + k * P:2048 + (k + 1) * P],
                                               prob[:, qt % 2, 0, k * P:(k + 1) * P], ident)
                last.then_inc(at_done, 1)

            def turn_out_rows(n, qt):
                pe.wait_ge(o_normed, n + 1)
                need(pe, ot_out, n)
                nc.tensor.transpose(ps[:, 7, 0:P], onrm[:, qt % 2], ident).then_inc(ot_done, 1)

            def pe_unit(h, u):
                n = h * NT + u
                first = isinstance(h, int) and h == 0
                scores(n, h, u, 0)
                if not first or u >= 2:
                    turn_probs(n - 2, (u - 2) % 4)
                scores(n, h, u, 1)
                if not first or u >= 3:
                    values(n - 3, h - (1 if u < 3 else 0), (u - 3) % 4)
                if not first:
                    turn_out_rows(n - 4, u)

            pe.wait_ge(fmix_ready, 2)
            pe.wait_ge(mod_ready, 7)
            for u in range(NT):
                pe_unit(0, u)
            with pe.Fori(1, HEADS) as h:
                for u in range(NT):
                    pe_unit(h, u)
            turn_probs(UNITS - 2, 2)
            values(UNITS - 3, HEADS - 1, 1)
            turn_out_rows(UNITS - 4, 0)
            turn_probs(UNITS - 1, 3)
            values(UNITS - 2, HEADS - 1, 2)
            turn_out_rows(UNITS - 3, 1)
            values(UNITS - 1, HEADS - 1, 3)
            turn_out_rows(UNITS - 2, 2)
            turn_out_rows(UNITS - 1, 3)

            pe.wait_ge(rowc_ready, 1)
            for i in range(8):
                r, half = i // 2, i % 2
                if i >= 2:
                    pe.wait_ge(row_out[half], i // 2)
                for c in range(4):
                    last = mm(ps[:, 4 + half, c * P:(c + 1) * P],
                              rowc[:, r, 4 * half + c:4 * half + c + 1].broadcast_to([P, P]), ident,
                              start=True, stop=True)
                last.then_inc(row_done, 1)
            pe.wait_ge(ot_out, UNITS)
            item_landed(pe, "wo0")
            item_landed(pe, "wo1")
            w = [item(f"wo{n}").rearrange("p (c n) -> p c n", c=MIXC) for n in range(2)]

            def turn_h2(t):
                pe.wait_ge(h2_ready, t + 1)
                if t:
                    pe.wait_ge(h2t_act, t)
                    pe.wait_ge(h2t_dve, t)
                else:
                    pe.wait_ge(row_out[0], 4)
                    pe.wait_ge(row_out[1], 4)
                for c in range(KC):
                    last = nc.tensor.transpose(ps[:, 4 + c // 4, (c % 4) * P:(c % 4 + 1) * P],
                                               h2[:, t % 2].rearrange("p (j c) -> p j c", c=KC)[:, :, c], ident)
                last.then_inc(h2t_done, 1)

            for t in range(NT):
                if t >= 2:
                    pe.wait_ge(y_scaled, t - 1)
                for n in range(2):
                    for c in range(MIXC):
                        last = mm(ps[:, 2 * (t % 2) + n], mixTv[:, c, t * P:(t + 1) * P], w[n][:, c],
                                  start=(c == 0), stop=(c == MIXC - 1))
                last.then_inc(wo_done, 1)
                if t >= 2:
                    turn_h2(t - 2)
            turn_h2(NT - 2)
            turn_h2(NT - 1)
            pe.wait_ge(h2t_act, NT)
            pe.wait_ge(h2t_dve, NT)
            for t in range(NT):
                for k in range(KC):
                    last = mm(ps[:, 7, t * NE:(t + 1) * NE], hT2[:, k, t * P:(t + 1) * P], wrt[:, k],
                              start=(k == 0), stop=(k == KC - 1))
            last.then_inc(logits_done, 1)
            landed_shared(pe)
            item_landed(pe, "shd")
            gu = item("shgu").rearrange("p (w c n) -> p w c n", w=2, c=KC)
            dn = item("shd")[:, 0:GU_W].rearrange("p (c n) -> p c n", c=2)

            def shared_gu(t):
                pe.wait_ge(*((s_up, t - 1) if t >= 2 else (y_scaled, NT)))
                for k in range(KC):
                    last = mm(ps[:, t % 2], hT2[:, k, t * P:(t + 1) * P], gu[:, :, k], start=(k == 0), stop=(k == KC - 1))
                last.then_inc(sgu_done, 1)

            def shared_down(t):
                pe.wait_ge(s_mid, t + 1)
                if t:
                    pe.wait_ge(smt_out, t)
                v = hmid[:, t % 2].rearrange("p (j c) -> p j c", c=2)
                for c in range(2):
                    last = nc.tensor.transpose(ps[:, 6, c * P:(c + 1) * P], v[:, :, c], ident)
                last.then_inc(smt_done, 1)
                pe.wait_ge(smt_out, t + 1)
                if t:
                    pe.wait_ge(sy_out, t)
                for n in range(2):
                    for c in range(2):
                        last = mm(ps[:, 2 + n], hmT[:, t % 2, c], dn[:, c, n * 512:(n + 1) * 512],
                                  start=(c == 0), stop=(c == 1))
                last.then_inc(sy_done, 1)

            shared_gu(0)
            shared_gu(1)
            shared_down(0)
            pe.wait_ge(mask_ready, 1)
            mask = rt[:, 256:512].rearrange("p (t e) -> p t e", t=NT)
            for t in range(NT):
                mm(ps[:, 4, t * NE:(t + 1) * NE], tri, mask[:, t], start=True, stop=(t == 0))
                for s in range(t):
                    mm(ps[:, 4, t * NE:(t + 1) * NE], ones[:], mask[:, s], start=False, stop=(s == t - 1))
            for t in range(NT):
                last = mm(ps[:, 5, 0:NE], ones[:], mask[:, t], start=(t == 0), stop=(t == NT - 1))
            last.then_inc(pos_done, 1)
            shared_gu(2)
            shared_down(1)
            shared_gu(3)
            shared_down(2)
            shared_down(3)
            for t in range(NT):
                pe.wait_ge(hot_ready, t + 1)
                pe.wait_ge(places, t + 1)
                ph, bvw = hot(t)
                for k in range(TOPK):
                    last = mm(ps[:, 7, 0:2 * NB], ph[:, k], bvw[:, k], start=(t == 0 and k == 0),
                              stop=(t == NT - 1 and k == TOPK - 1))
                last.then_inc(hot_used, 1)

            pe.wait_ge(table_copied, 1)
            for a in range(2):
                for n in range(2):
                    mm(ps[64 * n:64 * n + 64, 4 + a, 0:2 * NB], ident[:, 64 * a:64 * a + 64], table,
                       start=True, stop=True)
            mm(ps[0:1, 6, 0:NB], const[:, C_MAP + 1:C_MAP + 2], table[:, 0:NB], start=True, stop=True)
            for u in range(U):
                last = mm(ps[0:1, 6, NB + u * (NB // U):NB + (u + 1) * (NB // U)], freg[:, 224 + u:225 + u],
                          ident[:, 0:NB // U], start=True, stop=True)
            last.then_inc(table_spread, 1)

            def turn_x(n, s, k):
                pe.wait_ge(xg_in[s], 16 * (k + 1))
                for c in range(KC):
                    last = nc.tensor.transpose(ps[:, 4 + c // 4, (c % 4) * P:(c % 4 + 1) * P],
                                               xg[:, s].rearrange("p (j c) -> p j c", c=KC)[:, :, c], ident)
                last.then_inc(xt_done, 1)

            def pe_block(g, u):
                b = g * U + u
                first = isinstance(g, int) and b == 0
                code = pe.value_load(steer[0:1, at(u * (NB // U) + g, 1)], min_val=0, max_val=2 * (NE // U) - 1)
                if not first:
                    before = pe.value_load(steer[0:1, code_before(g, u)], min_val=0, max_val=2 * (NE // U) - 1)
                pe.wait_ge(w_in[u], 48 + 48 * (code >> 1))
                pe.wait_ge(xt_act, b + 1)
                pe.wait_ge(xt_dve, b + 1)
                need(pe, mid_ready, b - 1)
                gu = gate_up(wbuf(u))

                def gate_up_half(a):
                    for k in range(KC):
                        for f in range(2):
                            last = mm(halves(u % 2)[64 * f:64 * f + 64, a], xgT[:, u % 2, k, 64 * a:64 * a + 64],
                                      gu[:, :, k, P * f:P * f + P], start=(k == 0), stop=(k == KC - 1))
                    return last

                with pe.If((code & 1) > 0):
                    gate_up_half(1)
                gate_up_half(0).then_inc(gu_done, 1)
                if not first:
                    mid_turn(b, u)
                turn_x(b + 1, (u + 1) % 2, g * 2 + (u + 1) // 2)
                if not first:
                    down_turn(b, u, before)

            def code_before(g, u):
                return at((u - 1) % U * (NB // U) + (g if u else g - 1), 1)

            def mid_turn(b, u):
                pe.wait_ge(mid_ready, b)
                need(pe, mt_out, b - 1)
                for a in range(2):
                    last = nc.tensor.transpose(ps[:, 6, a * P:(a + 1) * P], hmid[:, (u - 1) % 2, a * P:(a + 1) * P], ident)
                last.then_inc(mt_done, 1)

            def down_turn(b, u, code):
                pe.wait_ge(mt_out, b)
                need(pe, y_act, b - 1)
                need(pe, y_dve, b - 1)
                dn = down(wbuf((u - 1) % U))

                def down_half(a):
                    m = hmT[:, (u - 1) % 2].rearrange("p a (c n) -> p a c n", c=2)
                    for c in range(2):
                        for n in range(2):
                            last = mm(ps[64 * n:64 * n + 64, 2 + a], m[:, a, c], dn[:, c, n * 512:(n + 1) * 512],
                                      start=(c == 0), stop=(c == 1))
                    return last

                with pe.If((code & 1) > 0):
                    down_half(1)
                down_half(0).then_inc(dn_done, 1)

            def pe_ending(g):
                code = pe.value_load(steer[0:1, code_before(g, 0)], min_val=0, max_val=2 * (NE // U) - 1)
                mid_turn(g * U, 0)
                down_turn(g * U, 0, code)

            pe.wait_ge(sy_out, NT)
            pe.wait_ge(slots_ready, 1)
            turn_x(0, 0, 0)
            pe.wait_ge(steer_ready, 1)
            for u in range(U):
                pe_block(0, u)
            pe.wait_ge(steer_ready, 1)
            turns = pe.value_load(steer[0:1, NB:NB + 1], min_val=0, max_val=TURNS - 1) + 1
            with pe.Fori(0, SPANS) as q:
                with pe.If(q * SPAN + 1 < turns):
                    with pe.Fori(1, SPAN + 1) as i:
                        g = (q * SPAN + i).with_bounds(min_val=1, max_val=TURNS - 1)
                        with pe.If(g < turns):
                            for u in range(U):
                                pe_block(g, u)
            pe_ending(turns)

        @block.vector
        def _(dve):
            steps = [0]

            def link(ins):
                steps[0] += 1
                ins.then_inc(dve_step, 1)
                dve.wait_ge(dve_step, steps[0])

            dve.memset(wbd, 0.0).then_inc(wbd_zero, 1)
            dve.memset(silc, 0.0).then_inc(wbd_zero, 1)
            link(dve.memset(ones[:], 1.0))
            dve.wait_ge(small_in, 16 * NSMALL)
            for i in range(2):
                last = dve.tensor_tensor_reduce(out=junk[:, i * HD:(i + 1) * HD], in0=lamv[:, 2 * i], in1=lamv[:, 2 * i + 1],
                                                scale=1.0, scalar=0.0, op0=ALU.mult, op1=ALU.add,
                                                accum_out=lam[:, i:i + 1])
            last.then_inc(lam_sum, 1)
            for t in range(NCT + NT):
                src = xctx[:, t] if t < NCT else xres[:, t - NCT]
                dve.wait_ge(x_in[t], 16)
                dve.wait_ge(rms_ready, t + 1)
                dve.tensor_scalar(xn[:, t], src, nrm[:, 2, t:t + 1], None, ALU.mult).then_inc(xn_ready, 1)
            dve.wait_ge(bd_done, 1)
            dve.tensor_copy(bd.rearrange("p j s n -> p (j s n)"), ps[:, 7]).then_inc(bd_ready, 1)
            dve.wait_ge(lam_exp, 1)
            dve.scalar_tensor_tensor(lam[:, 4:5], lam[:, 3:4], -LAM0, lam[:, 2:3], ALU.add, ALU.subtract)
            dve.tensor_scalar(gsub[:, 1:2], gsub[:, 0:1], 1.0 - LAM0, None, ALU.mult).then_inc(setup, 1)

            def modulation_out(m):
                dve.wait_ge(mod_done, m + 1)
                rows, cols = grow[:, 0, 0:256], grow[:, 0, 256:512]
                link(dve.tensor_copy(rows.rearrange("p (c j) -> p c j", c=KC),
                                     ps[:, 6 + m % 2, 0:256].rearrange("p (j c) -> p c j", c=KC)))
                link(dve.transpose(cols, rows))
                dve.tensor_tensor(modc[:, m], cols.rearrange("p (c s) -> p c s", c=KC)[:, :, 0:2],
                                  bmod[:, m].unsqueeze(2).broadcast_to([P, KC, 2]), ALU.add).then_inc(mod_ready, 1)
                dve.wait_ge(mod_ready, m + 1 if m < 2 else m + 2)

            modulation_out(0)
            modulation_out(1)
            dve.wait_ge(mod_ready, 2)
            dve.scalar_tensor_tensor(scl1[:], modc[:, 1], 1.0, gain[:, 0].unsqueeze(2).broadcast_to([P, KC, 2]),
                                     ALU.add, ALU.mult).then_inc(mod_ready, 1)
            dve.wait_ge(mod_ready, 3)
            for c in range(KC):
                dve.wait_ge(tlat_done, c + 1)
                dve.tensor_scalar(hT[:, c, NCTX:], ps[:, c % 2], scl1[:, c, 0:1], modc[:, 0, c, 0:1], ALU.mult, ALU.add)\
                   .then_inc(hlat_ready, 1)
            for step in plan_proj["dve"]:
                step(dve)
            for t in range(1, NT, 2):
                dve.wait_ge(g_done, t + 1)
                dve.tensor_copy(fg[:, t].rearrange("p j s n -> p (j s n)"), ps[:, t]).then_inc(g_ready, 1)
            for m in range(2, 6):
                modulation_out(m)
            dve.wait_ge(mod_ready, 7)
            dve.tensor_tensor(rowc[:, 0], modc[:, 2, :, 0], gain[:, 1], ALU.mult)
            dve.scalar_tensor_tensor(rowc[:, 1], modc[:, 4, :, 0], 1.0, gain[:, 2], ALU.add, ALU.mult)
            dve.tensor_copy(rowc[:, 2], modc[:, 3, :, 0])
            dve.tensor_tensor(rowc[:, 3], modc[:, 5, :, 0], gain[:, 3], ALU.mult).then_inc(rowc_ready, 1)

            N_LINK = 2

            def alink(ins, n, k):
                ins.then_inc(dve_step, 1)
                dve.wait_ge(dve_step, att0 + k + 1 + n * N_LINK)

            att0 = steps[0]

            def at_evac(n, qt):
                dve.wait_ge(at_done, n + 1)
                dve.tensor_copy(aT[:, qt % 2, 512:768], ps[:, 5, 0:256]).then_inc(at_out[1], 1)

            def dve_unit(h, u):
                n = h * NT + u
                first = isinstance(h, int) and h == 0
                st = stat[:, u]
                for m in range(2):
                    dve.wait_ge(s_done[m], n + 1)
                    dve.tensor_reduce(st[:, m:m + 1], psf[:, 1024 * m:1024 * m + NTOK], AX, ALU.max, negate=True)\
                       .then_inc(nmax[m], 1)
                    if m == 0 and (not first or u >= 2):
                        at_evac(n - 2, (u - 2) % 4)
                dve.wait_ge(exped[0], n + 1)
                dve.wait_ge(exped[1], n + 1)
                alink(dve.reciprocal(st[:, 4:6], st[:, 2:4]), n, 0)
                alink(dve.scalar_tensor_tensor(st[:, 6:7], st[:, 2:3], lam[:, 4:5], st[:, 5:6], ALU.mult, ALU.mult), n, 1)
                dve.scalar_tensor_tensor(prob[:, u % 2, 0], prob[:, u % 2, 1], st[:, 6:7], prob[:, u % 2, 0],
                                         ALU.mult, ALU.add).then_inc(combined, 1)

            dve.wait_ge(setup, 1)
            for u in range(NT):
                dve_unit(0, u)
            with dve.Fori(1, HEADS) as h:
                for u in range(NT):
                    dve_unit(h, u)
            steps[0] += N_LINK * UNITS
            at_evac(UNITS - 2, 2)
            at_evac(UNITS - 1, 3)

            for i in range(1, 8, 2):
                dve.wait_ge(row_done, i + 1)
                row_dst = (grow[:, 0], srow[:, 0], srow[:, 1], grow[:, 1])[i // 2]
                dve.tensor_copy(row_dst.rearrange("p (j c) -> p c j", c=KC)[:, 4:8],
                                ps[:, 5].rearrange("p (c j) -> p c j", c=4)).then_inc(row_out[1], 1)
            for half in range(2):
                dve.wait_ge(row_out[half], 4)

            def h2t_evac(t):
                dve.wait_ge(h2t_done, t + 1)
                dve.tensor_copy(hT2[:, 4:8, t * P:(t + 1) * P], ps[:, 5].rearrange("p (c n) -> p c n", c=4))\
                   .then_inc(h2t_dve, 1)

            for t in range(NT):
                b = 2 * (t % 2)
                dve.wait_ge(y_rms, t + 1)
                if t:
                    dve.wait_ge(x1_ready, t)
                dve.scalar_tensor_tensor(tmp1, psf[:, b * 512:b * 512 + D], nrm[:, 2, 6 + t:7 + t], grow[:, 0],
                                         ALU.mult, ALU.mult).then_inc(y_scaled, 1)
                dve.wait_ge(y_scaled, t + 1)
                dve.tensor_tensor(xres[:, t], xres[:, t], tmp1, ALU.add).then_inc(x1_ready, 1)
                dve.wait_ge(x1_rms, t + 1)
                if t >= 2:
                    dve.wait_ge(h2_stored[t % 2], 16 * (t // 2))
                    dve.wait_ge(h2t_done, t - 1)
                dve.scalar_tensor_tensor(h2[:, t % 2], xres[:, t], nrm[:, 2, 10 + t:11 + t], srow[:, 0],
                                         ALU.mult, ALU.mult).then_inc(h_scaled, 1)
                if t >= 2:
                    h2t_evac(t - 2)
            h2t_evac(NT - 2)
            h2t_evac(NT - 1)

            sc = rt[:, 0:256]
            mask = rt[:, 256:512]
            sel, selm, selr, wn, sslot = (rt[:, 512 + 256 * i:768 + 256 * i] for i in range(5))
            t4 = lambda v: v.rearrange("p (t e) -> p t e", t=NT)
            t48 = lambda v: v.rearrange("p (t g e) -> p t g e", t=NT, g=NGRP)
            m8 = qreg[:, WBUF:WBUF + 256].rearrange("p (t g k) -> p t g k", t=NT, g=NGRP)
            cmp1, cmp2 = qreg[:, WBUF + 256:WBUF + 512], qreg[:, WBUF + 512:WBUF + 768]
            v8, idx = qreg[:, WBUF + 768:WBUF + 800], qreg[:, WBUF + 800:WBUF + 832].bitcast(U32)
            ovf = freg[:, 0:512]
            nb, bend, base = (ovf[:, 64 * i:64 * i + 64] for i in range(3))
            small = ovf[:, 192:256]
            ints = freg[:, 256:384].bitcast(I32)
            intl = freg[:, 384:416].bitcast(I32)
            cmp3 = freg[:, 416:480]
            for s in h2_stored:
                dve.wait_ge(s, 16 * NT // 2)
            dve.wait_ge(h2t_done, NT)
            dve.wait_ge(scores_ready, 1)
            link(dve.tensor_tensor(t4(sel), t4(sc), rbias[:].unsqueeze(1).broadcast_to([P, NT, NE]), ALU.add))
            for t in range(NT):
                for g in range(NGRP):
                    last = dve.max(out=m8[:, t, g], in_=sel[:, t * NE + g * GE:t * NE + (g + 1) * GE])
            link(last)
            g3 = gsum.rearrange("p (t g) -> p t g", t=NT)
            link(dve.tensor_tensor(g3, m8[:, :, :, 0], m8[:, :, :, 1], ALU.add))
            other = g3.unsqueeze(2).broadcast_to([P, NT, NGRP, NGRP])
            own = g3.unsqueeze(3).broadcast_to([P, NT, NGRP, NGRP])
            dve.tensor_tensor(t48(cmp1), other, own, ALU.is_gt)
            link(dve.tensor_tensor(t48(cmp2), other, own, ALU.is_equal))
            earlier = const[:, C_LT:C_LT + 64].unsqueeze(1).broadcast_to([P, NT, 64])
            link(dve.tensor_tensor(t4(cmp2), t4(cmp2), earlier, ALU.mult))
            link(dve.tensor_tensor(cmp1, cmp1, cmp2, ALU.add))
            link(dve.tensor_reduce(rank, cmp1.rearrange("p (g k) -> p g k", k=NGRP), AX, ALU.add))
            link(dve.tensor_scalar(rank, rank, float(TOPG), -1e30, ALU.is_ge, ALU.mult))
            link(dve.tensor_tensor(selm.rearrange("p (g e) -> p g e", e=GE), sel.rearrange("p (g e) -> p g e", e=GE),
                                   rank.unsqueeze(2).broadcast_to([P, NT * NGRP, GE]), ALU.add))
            for t in range(NT):
                last = dve.max(out=v8[:, 8 * t:8 * t + 8], in_=selm[:, t * NE:(t + 1) * NE])
            link(last)
            for t in range(NT):
                dve.max_index(idx[:, 8 * t:8 * t + 8], v8[:, 8 * t:8 * t + 8], selm[:, t * NE:(t + 1) * NE])
            for t in range(NT):
                last = dve.match_replace(selr[:, t * NE:(t + 1) * NE], v8[:, 8 * t:8 * t + 8],
                                         selm[:, t * NE:(t + 1) * NE], -3e38)
            link(last)
            dve.tensor_tensor(mask, selm, selr, ALU.not_equal).then_inc(mask_ready, 1)
            dve.tensor_copy(idxf, idx)
            dve.wait_ge(mask_ready, 1)
            link(dve.tensor_tensor(selr, sc, mask, ALU.mult))
            link(dve.tensor_reduce(small[:, 0:4], t4(selr), AX, ALU.add))
            link(dve.tensor_scalar(small[:, 4:8], small[:, 0:4], 1e-20, None, ALU.add))
            link(dve.reciprocal(small[:, 8:12], small[:, 4:8]))
            link(dve.tensor_scalar(small[:, 12:16], small[:, 8:12], ROUTED_SCALE, None, ALU.mult))
            link(dve.tensor_tensor(t4(wn), t4(selr), small[:, 12:16].unsqueeze(2).broadcast_to([P, NT, NE]), ALU.mult))
            dve.wait_ge(pos_done, 1)
            link(dve.tensor_scalar(nb, ps[:, 5, 0:NE], float(P), 1.0, ALU.is_gt, ALU.add))
            link(dve.scalar_tensor_tensor(nb, ps[:, 5, 0:NE], float(2 * P), nb, ALU.is_gt, ALU.add))
            link(dve.scalar_tensor_tensor(nb, ps[:, 5, 0:NE], float(3 * P), nb, ALU.is_gt, ALU.add))
            lane = lambda v, u: v.rearrange("p (j u) -> p u j", u=U)[:, u]
            for u in range(U):
                last = dve.tensor_tensor_scan(lane(bend, u), ones[:, 0:NE // U], lane(nb, u), 0.0, ALU.mult, ALU.add)
            link(last)
            link(dve.tensor_tensor(base, bend, nb, ALU.subtract))
            pos = ps[:, 4, 0:256]
            link(dve.scalar_tensor_tensor(t4(sslot), base.unsqueeze(1).broadcast_to([P, NT, NE]), 1024.0, t4(pos),
                                          ALU.mult, ALU.add))
            pick = qreg[:, WBUF + 1024:WBUF + 1024 + 2 * NT * TOPK * NE].rearrange("p (i e) -> p i e", e=NE)
            for t in range(NT):
                for k in range(TOPK):
                    i = t * TOPK + k
                    for j, (table_, out) in enumerate(((sslot, skf), (wn, wkf))):
                        last = dve.scalar_tensor_tensor(pick[:, 2 * i + j], iota[:, 0:NE], idxf[:, i:i + 1],
                                                        table_[:, t * NE:(t + 1) * NE], ALU.is_equal, ALU.mult,
                                                        accum_out=out[:, i:i + 1])
            link(last)
            link(dve.tensor_copy(ints[:, 0:32], skf))
            dve.tensor_scalar(ints[:, 32:64], ints[:, 0:32], P - 1, None, ALU.bitwise_and)
            dve.tensor_scalar(intl, idx.bitcast(I32), U - 1, None, ALU.bitwise_and)
            dve.tensor_scalar(ints[:, 96:128], ints[:, 0:32], 8, 256 - U, ALU.logical_shift_right, ALU.bitwise_and)
            link(dve.tensor_scalar(ints[:, 64:96], ints[:, 0:32], 5, 7 * U, ALU.logical_shift_right, ALU.bitwise_and))
            link(dve.tensor_tensor(intl, intl, ints[:, 96:128], ALU.bitwise_or))
            dve.tensor_copy(pf, ints[:, 32:64])
            dve.tensor_tensor(bf, intl, ints[:, 64:96], ALU.add).then_inc(place_ready, 1)
            dve.wait_ge(place_ready, 1)
            for t in range(NT):
                if t >= 2:
                    dve.wait_ge(hot_used, t - 1)
                elif t == 1:
                    dve.wait_ge(sgu_done, NT)
                _, bvw = hot(t)
                for k in range(TOPK):
                    i = t * TOPK + k
                    dve.tensor_scalar(bvw[:, k, 0:NB], iota[:, 0:NB], bf[:, i:i + 1], const[:, C_V + i:C_V + i + 1],
                                      ALU.is_equal, ALU.mult)
                    last = dve.tensor_scalar(bvw[:, k, NB:2 * NB], iota[:, 0:NB], bf[:, i:i + 1], wkf[:, i:i + 1],
                                             ALU.is_equal, ALU.mult)
                last.then_inc(hot_ready, 1)
            link(dve.tensor_scalar(cmp3, bend, const[:, C_ROW:C_ROW + 1], None, ALU.is_le))
            link(dve.tensor_reduce(small[:, 32:32 + U], cmp3.rearrange("p (j u) -> p u j", u=U), AX, ALU.add))
            link(dve.tensor_reduce(small[0:1, 43:44], bend[0:1, NE - U:NE], AX, ALU.max))
            dve.tensor_scalar(small[0:1, 40:41], small[0:1, 43:44], -1.0, None, ALU.add)
            dve.tensor_scalar(small[0:1, 41:42], small[0:1, 43:44], 32.0 * U // 2, None, ALU.mult)
            link(dve.tensor_scalar(small[0:1, 42:43], small[0:1, 43:44], 16.0 * U // 2, 16.0, ALU.mult, ALU.add))
            link(dve.tensor_copy(steer[:, NB:NB + 3], small[0:1, 40:43]))
            dve.wait_ge(hot_used, NT)
            dve.tensor_copy(table, ps[:, 7, 0:2 * NB]).then_inc(table_copied, 1)
            dve.wait_ge(table_copied, 1)
            emp, rowf = freg[:, 512:512 + NB], freg[:, 704:704 + NB]
            emp2, rowf2 = (freg[:, 896 + 384 * i:896 + 384 * i + 2 * NB].rearrange("p (a n) -> p a n", a=2) for i in range(2))
            link(dve.tensor_scalar(emp, table[:, 0:NB], 0.0, SKIP, ALU.is_equal, ALU.mult))
            link(dve.scalar_tensor_tensor(rowf, table[:, 0:NB], -1.0, emp, ALU.add, ALU.add))
            rowi = freg[:, 1664:1664 + NB].bitcast(I32)
            link(dve.tensor_copy(rowi, rowf))
            dve.tensor_scalar(slots[:, :, 0], rowi, 3, None, ALU.logical_shift_right)
            dve.wait_ge(table_spread, 1)
            tv, tw = ps[:, 4:6, 0:NB], ps[:, 4:6, NB:2 * NB]
            e2 = freg[0:1, 1856:1856 + NB]
            link(dve.tensor_scalar(e2, ps[0:1, 6, NB:2 * NB], float(NE // U - 1), 2.0, ALU.min, ALU.mult))
            by_lane = lambda v: v.rearrange("p (u t) -> p u t", u=U)
            dve.scalar_tensor_tensor(by_lane(steer[:, 0:NB]), ps[0:1, 6, 0:NB].rearrange("p (t u) -> p u t", u=U), 0.0,
                                     by_lane(e2), ALU.is_gt, ALU.add).then_inc(steer_ready, 1)
            dve.tensor_copy(slots.bitcast(F32)[:, :, 3:5].rearrange("p b a -> p a b"), tw)
            link(dve.tensor_scalar(emp2, tv, 0.0, SKIP, ALU.is_equal, ALU.mult))
            link(dve.scalar_tensor_tensor(rowf2, tv, 2.0, emp2, ALU.mult, ALU.add))
            dve.tensor_scalar(slots[:, :, 1:3].rearrange("p b a -> p a b"), rowf2, const[:, C_MAP + 1:C_MAP + 2], -2.0,
                              ALU.add, ALU.add).then_inc(slots_ready, 1)
            dve.wait_ge(slots_ready, 1)

            def take_tokens(b, u):
                dve.tensor_copy(take[:, u:u + 1], slots_flat[:, at(b * 5, 1)]).then_inc(take_ready, 1)

            def take_rows(g, u):
                need(dve, y_out[u % 2], g * (32 * U // 2) + 32 * ((u - 4) // 2 + 1))
                dve.tensor_copy(put[:, u], slots_flat[:, at((g * U + u) * 5 + 1, 4)]).then_inc(put_ready, 1)

            slots_flat = slots.rearrange("p b k -> p (b k)")

            def x_evac(n, s):
                dve.wait_ge(xt_done, n + 1)
                dve.tensor_copy(xgT[:, s, 4:8], ps[:, 5].rearrange("p (c n) -> p c n", c=4)).then_inc(xt_dve, 1)

            def dve_block(g, u):
                b = g * U + u
                first = isinstance(g, int) and b == 0
                take_tokens(b + 2, (u + 2) % U)
                take_rows(g, u)
                dve.wait_ge(gate_ready, b + 1)
                two = lambda v: v.rearrange("p (a n) -> p a n", a=2)
                dve.tensor_tensor(two(hmid[:, u % 2]), halves(u % 2)[:, :, 1], two(gsil[:, u % 2]), ALU.mult)\
                    .then_inc(mid_ready, 1)
                x_evac(b + 1, (u + 1) % 2)
                if not first:
                    y_evac(g, u)

            def y_evac(g, u):
                dve.wait_ge(dn_done, g * U + u)
                need(dve, y_out[(u - 1) % 2], done_scatters(g, u))
                dve.wait_ge(put_ready, g * U + u)
                w = put[:, (u - 1) % U, 3:4].bitcast(F32)
                dve.tensor_scalar(yb[:, (u - 1) % 2, 512:1024], ps[:, 3], w, None, ALU.mult).then_inc(y_dve, 1)

            dve.wait_ge(sy_out, NT)
            take_tokens(0, 0)
            take_tokens(1, 1)
            x_evac(0, 0)
            for u in range(U):
                dve_block(0, u)
            dve.wait_ge(steer_ready, 1)
            turns = dve.value_load(steer[0:1, NB:NB + 1], min_val=0, max_val=TURNS - 1) + 1
            with dve.Fori(0, SPANS) as q:
                with dve.If(q * SPAN + 1 < turns):
                    with dve.Fori(1, SPAN + 1) as i:
                        g = (q * SPAN + i).with_bounds(min_val=1, max_val=TURNS - 1)
                        with dve.If(g < turns):
                            for u in range(U):
                                dve_block(g, u)
            y_evac(turns, 0)

            for t in range(NT):
                dve.wait_ge(r_in[t % 2], 16 * (t // 2 + 1))
                v = ring[:, (t % 2) * 8192:(t % 2) * 8192 + 8192].rearrange("p (k n) -> p n k", k=TOPK)
                tail = qreg[:, WBUF + (t % 2) * 1024:WBUF + (t % 2) * 1024 + 1024]
                link(dve.tensor_reduce(tail, v, AX, ALU.add))
                dve.tensor_tensor(shy[:, t], shy[:, t], tail, ALU.add).then_inc(r_sum, 1)
                dve.wait_ge(r_rms, t + 1)
                dve.wait_ge(r_sum, t + 1)
                link(dve.scalar_tensor_tensor(shy[:, t], shy[:, t], nrm[:, 2, 14 + t:15 + t], grow[:, 1], ALU.mult, ALU.mult))
                dve.tensor_tensor(shy[:, t], shy[:, t], xres[:, t], ALU.add).then_inc(r_fin, 1)

        @block.gpsimd
        def _(pool):
            steps = [0]

            def link(ins):
                steps[0] += 1
                ins.then_inc(pool_step, 1)
                pool.wait_ge(pool_step, steps[0])

            link(pool.memset(mhalf[:], -0.5))

            def rms(i, ready):
                link(pool.tensor_scalar(nrm[:, 1, i:i + 1], nrm[:, 0, i:i + 1], 1.0 / D, EPS, ALU.mult, ALU.add))
                pool.tensor_tensor(nrm[:, 2, i:i + 1], nrm[:, 1, i:i + 1], mhalf[:], ALU.pow).then_inc(ready, 1)

            for t in range(NCT + NT):
                pool.wait_ge(squares, t + 1)
                rms(t, rms_ready)
            for step in plan_proj["pool"]:
                step(pool)

            def stage_q(n, h, qt):
                need(pool, s_done[1], n - 1)
                pool.tensor_tensor(qz[:, qt % 2], qT[:, at(h * NLAT + qt * P, P)].unsqueeze(1).broadcast_to([P, 2, P]),
                                   const[:, C_MAP:C_MAP + 2].unsqueeze(2).broadcast_to([P, 2, P]), ALU.mult)\
                    .then_inc(q_staged, 1)

            def o_rms_(n, qt):
                pool.wait_ge(o_square, n + 1)
                pool.sem_inc(pool_tick, 1)
                pool.tensor_scalar(stat[:, qt, 8:9], stat[:, qt, 7:8], 1.0 / VD, EPS, ALU.mult, ALU.add)\
                    .then_inc(pool_step, 1)
                pool.wait_ge(pool_step, n + (att0 + 1))
                pool.tensor_tensor(stat[:, qt, 9:10], stat[:, qt, 8:9], mhalf[:], ALU.pow).then_inc(o_rms, 1)
                pool.wait_ge(o_rms, n + 1)
                pool.tensor_tensor(onrm[:, qt % 2], osb[:, qt % 2], stat[:, qt, 9:10].broadcast_to([P, P]), ALU.mult)\
                    .then_inc(o_normed, 1)

            att0 = steps[0]
            pool.wait_ge(g_done, NT)
            pool.wait_ge(turn_out, sum(1 for x in plan_proj["pe"] if x))
            stage_q(0, 0, 0)

            def pool_unit(h, u, last=False):
                n = h * NT + u
                first = isinstance(h, int) and h == 0
                if not last:
                    stage_q(n + 1, h + (1 if u == NT - 1 else 0), (u + 1) % NT)
                if not first or u >= 3:
                    o_rms_(n - 3, (u - 3) % 4)

            for u in range(NT):
                pool_unit(0, u)
            with pool.Fori(1, HEADS - 1) as h:
                for u in range(NT):
                    pool_unit(h, u)
            for u in range(NT):
                pool_unit(HEADS - 1, u, last=(u == NT - 1))
            o_rms_(UNITS - 3, 1)
            o_rms_(UNITS - 2, 2)
            o_rms_(UNITS - 1, 3)
            steps[0] += UNITS
            for t in range(NT):
                pool.wait_ge(y_square, t + 1)
                rms(6 + t, y_rms)
                pool.wait_ge(x1_square, t + 1)
                rms(10 + t, x1_rms)
                pool.wait_ge(h_scaled, t + 1)
                pool.tensor_tensor(h2[:, t % 2], h2[:, t % 2], srow[:, 1], ALU.add).then_inc(h2_ready, 1)
            for t in range(NT):
                pool.wait_ge(s_up, t + 1)
                pool.wait_ge(s_gate, t + 1)
                if t >= 2:
                    pool.wait_ge(smt_done, t - 1)
                pool.tensor_tensor(hmid[:, t % 2], gsil[:, t % 2], sreg[:, 1024 + (t % 2) * DE:1024 + (t % 2) * DE + DE],
                                   ALU.mult).then_inc(s_mid, 1)

            pool.wait_ge(h2t_done, NT)
            pool.memset(xg, 0.0).then_inc(xg_zero, 1)
            pool.wait_ge(xg_zero, 1)
            pool.wait_ge(place_ready, 1)
            for t in range(NT):
                if t >= 2:
                    pool.wait_ge(hot_used, t - 1)
                ph, _ = hot(t)
                for k in range(TOPK):
                    last = pool.tensor_scalar(ph[:, k], iota[:, 0:P], pf[:, t * TOPK + k:t * TOPK + k + 1], None, ALU.is_equal)
                last.then_inc(places, 1)

            def gather(b, u):
                pool.wait_ge(take_ready, b + 1)
                pool.sem_inc(pool_tick, 1)
                pool.indirect_dma_start(xg[:, u % 2], None, h2_dram[:], bass.IndirectOffsetOnAxis(take[:, u % U:u % U + 1], 0),
                                        bounds_check=NLAT - 1, oob_is_err=False).then_inc(xg_in[u % 2], 16)

            def pool_block(g, u):
                b = g * U + u
                first = isinstance(g, int) and b == 0
                pool.wait_ge(xt_done, b + 1)
                gather(b + 2, u + 2)
                if not first:
                    scatter(b, u)

            def scatter(b, u):
                pool.wait_ge(put_ready, b)
                pool.wait_ge(y_act, b)
                pool.wait_ge(y_dve, b)
                pool.sem_inc(pool_tick, 1)
                for a in range(2):
                    pool.indirect_dma_start(y_dram.rearrange("r (f n) -> (r f) n", f=2),
                                            bass.IndirectOffsetOnAxis(put[:, (u - 1) % U, a:1 + a], 0),
                                            yb[:, (u - 1) % 2, 512 * a:512 * a + 512], None,
                                            bounds_check=2 * NLAT * TOPK - 1, oob_is_err=False)\
                        .then_inc(y_out[(u - 1) % 2], 16)

            for s in h2_stored:
                pool.wait_ge(s, 16 * NT // 2)
            pool.wait_ge(slots_ready, 1)
            gather(0, 0)
            gather(1, 1)
            for u in range(U):
                pool_block(0, u)
            pool.wait_ge(steer_ready, 1)
            turns = pool.value_load(steer[0:1, NB:NB + 1], min_val=0, max_val=TURNS - 1) + 1
            with pool.Fori(0, SPANS) as q:
                with pool.If(q * SPAN + 1 < turns):
                    with pool.Fori(1, SPAN + 1) as i:
                        g = (q * SPAN + i).with_bounds(min_val=1, max_val=TURNS - 1)
                        with pool.If(g < turns):
                            for u in range(U):
                                pool_block(g, u)
            scatter(turns * U, 0)
            counts = [pool.value_load(steer[0:1, NB + 1 + i:NB + 2 + i], min_val=0, max_val=16 * U * TURNS)
                      for i in range(2)]
            for x, i in ((y_out[0], 0), (y_out[1], 0), (xg_in[0], 1), (xg_in[1], 1)):
                pool.wait_ge(x, counts[i])
            pool.sem_inc(moe_done, 1)
            for t in range(NT):
                pool.wait_ge(r_square, t + 1)
                rms(14 + t, r_rms)


_OUT = ((1, NLAT, D), "float32")


def shape_tables():
    import numpy as np

    c = np.zeros((P, C_ALL), np.float32)
    p = np.arange(P)
    c[:, C_ID:C_ID + P] = np.eye(P)
    c[:, C_TRI:C_TRI + P] = p[:, None] < p[None, :]
    c[:, C_IOTA:C_IOTA + NB] = np.arange(NB)
    c[:, C_ROW] = p
    g = np.arange(NGRP)
    c[:, C_LT:C_LT + 64] = (g[None, :] < g[:, None]).reshape(1, 64)
    t, k = np.arange(NT), np.arange(TOPK)
    c[:, C_V:C_V + 32] = ((t[None, :, None] * P + p[:, None, None]) * TOPK + k[None, None, :] + 1).reshape(P, 32)
    c[0:64, C_MAP], c[64:128, C_MAP + 1] = 1.0, 1.0
    j = np.arange(64)
    ang = 2 * np.pi * (np.outer(j, j) % 64) / 64
    for h in range(2):
        s = slice(64 * h, 64 * h + 64)
        c[s, C_CC + 64 * h:C_CC + 64 * h + 64] = np.cos(ang) / 8
        c[s, C_SC + 64 * h:C_SC + 64 * h + 64] = -np.sin(ang) / 8
    n = np.arange(NLAT)
    ang = 2 * np.pi * (np.outer(n, n) % NLAT) / NLAT
    d = np.stack([np.cos(ang), np.sin(ang)]) / np.sqrt(NLAT)
    dft = d.reshape(2, NT, P, NLAT).transpose(2, 0, 1, 3).reshape(P, 2 * NT * NLAT).astype(np.float32)
    inv = (10000.0 ** (-np.arange(0, 32, 2, dtype=np.float32) / np.float32(32))).astype(np.float32)
    pos = np.stack([n // 64, n % 64], -1).astype(np.float32)
    ang = (pos[:, :, None] * inv).astype(np.float32)
    cos, sin = np.cos(ang), np.sin(ang)
    rope = np.stack([np.stack([cos, cos], 2).reshape(NLAT, HD), np.stack([-sin, sin], 2).reshape(NLAT, HD)], 1)
    return {"consts": c, "dft": dft, "rope": rope.astype(np.float32)}


def kernel(**inputs):
    import numpy as np
    import concourse.bacc as bacc
    from concourse.bass_utils import run_bass_kernel_spmd

    nc = bacc.Bacc("TRN2", target_bir_lowering=False, num_devices=1)
    arrays, args = {}, {}
    for name, a in {**inputs, **shape_tables()}.items():
        a = np.ascontiguousarray(a)
        arrays[f"in_{name}"] = a
        args[name] = nc.dram_tensor(f"in_{name}", a.shape, mybir.dt.from_np(a.dtype), kind="ExternalInput").ap()
    args["out"] = nc.dram_tensor("out_x", _OUT[0], F32, kind="ExternalOutput").ap()
    build(nc, args)
    r = run_bass_kernel_spmd(nc, [arrays], core_ids=[0])
    return r.results[0]["out_x"]
```

```python
import math
from contextlib import ExitStack

import concourse.bass as bass
from concourse import mybir

F32 = mybir.dt.float32
I32 = mybir.dt.int32
U32 = mybir.dt.uint32
ALU = mybir.AluOpType
ACT = mybir.ActivationFunctionType
AX = mybir.AxisListType.X

P = 128
D = 1024
KC = D // P
NLAT, NCTX = 512, 256
NT = NLAT // P
NCT = NCTX // P
NTOK = NLAT + NCTX
FW = 256
HEADS, HD = 6, 64
VD = 2 * HD
QKW = HEADS * VD
NE, TOPK, NGRP, TOPG = 64, 8, 8, 4
GE = NE // NGRP
DE = 256
MIXC = (FW + QKW) // P
EPS = 1e-6
LAM0 = 0.8 - 0.6 * math.exp(-0.3 * 0)
ROUTED_SCALE = 2.5
UNITS = HEADS * NT
U = 4
MAXOV = NLAT * TOPK // P - 1
TURNS = NE // U + MAXOV
SPAN, SPANS = 6, 8
assert SPAN * SPANS >= TURNS - 1
NB = (TURNS + 1) * U
SKIP = 100000.0
GU_W = KC * DE
WBUF = 3 * GU_W
FRONT = 8 * 512
NFRONT = 5
RBUFS = 6

C_ID, C_TRI, C_IOTA, C_LT, C_V, C_CC, C_SC = 0, 128, 256, 448, 512, 544, 672
C_MAP = 800
C_ROW = 802
C_ALL = 803


def at(index, size):
    return slice(index, index + size) if isinstance(index, int) else bass.ds(index, size)


def need(eng, sem, value):
    if not (isinstance(value, int) and value <= 0):
        eng.wait_ge(sem, value)


def build(nc, A):
    ctx = ExitStack()
    sb = lambda name, shape, dt=F32: ctx.enter_context(nc.sbuf_tensor(name, shape, dt))
    sem = lambda name: ctx.enter_context(nc.semaphore(name))
    with ctx:
        xres = sb("xres", [P, NT, D])
        heap = sb("heap", [P, 2 * WBUF + NFRONT * FRONT])
        ring = heap[:, 2 * WBUF:]
        hreg = sb("hreg", [P, KC * NTOK])
        sreg = sb("sreg", [P, 3072])
        freg = sb("freg", [P, 2560])
        grow = sb("grow", [P, 2, D])
        const = sb("const", [P, C_ALL])
        ones = sb("ones", [P, P])
        stat = sb("stat", [P, 4, 16])
        colc = sb("colc", [P, 2, KC])
        bmod = sb("bmod", [P, 6, KC])
        gain = sb("gain", [P, 4, KC])
        modc = sb("modc", [P, 6, KC, 2])
        scl1 = sb("scl1", [P, KC, 2])
        rowc = sb("rowc", [P, 4, KC])
        lam = sb("lam", [P, 8])
        gsub = sb("gsub", [P, 2])
        nrm = sb("nrm", [P, 3, 24])
        mhalf = sb("mhalf", [P, 1])
        wrt = sb("wrt", [P, KC, NE])
        rbias = sb("rbias", [P, NE])
        take = sb("take", [P, U], I32)
        put = sb("put", [P, U, 4], I32)
        ps = ctx.enter_context(nc.psum_tensor("ps", [P, 8, 512], F32))
        psf = ps[:].rearrange("p b n -> p (b n)")
        h2_dram = nc.dram_tensor("h2_rows", [NLAT, D], F32, kind="Internal").ap()
        y_dram = nc.dram_tensor("y_rows", [NLAT * TOPK, D], F32, kind="Internal").ap()

        hT = hreg[:].rearrange("p (c n) -> p c n", c=KC)
        mixT = hreg[:, 0:MIXC * NLAT]
        mixTv = mixT.rearrange("p (c n) -> p c n", c=MIXC)
        fg = hreg[:, 4096:6144].rearrange("p (t j s n) -> p t j s n", t=NT, j=2, s=2)
        hT2 = hreg[:, 0:KC * NLAT].rearrange("p (c n) -> p c n", c=KC)
        xg = [hreg[:, k:k + D] for k in (4096, 5120, 2048, 3072)]
        qreg = heap[:, 0:2 * WBUF]
        xn = qreg[:, 0:6144].rearrange("p (t n) -> p t n", t=NCT + NT)
        qT = qreg[:, 0:3072]
        kT = qreg[:, 3072:7680]
        vt = qreg[:, 7680:12288].rearrange("p (t n) -> p t n", t=NCT + NT)
        tmp1 = qreg[:, 6144:7168]
        h2 = qreg[:, 7168:9216].rearrange("p (s n) -> p s n", s=2)
        shy = qreg[:, 0:4096].rearrange("p (t n) -> p t n", t=NT)
        rt = qreg[:, 4096:6144]
        gsum, rank, idxf, skf, wkf, pf, bf = (rt[:, 1792 + 32 * i:1824 + 32 * i] for i in range(7))
        slots = rt[:, 0:5 * NB].bitcast(I32).rearrange("p (b k) -> p b k", k=5)
        steer = rt[0:1, 1408:1408 + NB + 3].bitcast(I32)
        table = rt[:, 1024:1024 + 2 * NB]
        prob = sreg[:].rearrange("p (s m n) -> p s m n", s=2, m=2)
        xctx = sreg[:, 0:2048].rearrange("p (t n) -> p t n", t=NCT)
        ropeA = sreg[:, 0:1024].rearrange("p (s n) -> p s n", s=2)
        ropeB = sreg[:, 1024:2048].rearrange("p (s n) -> p s n", s=2)
        srow = sreg[:, 0:2048].rearrange("p (s n) -> p s n", s=2)
        xgT = sreg[:, 0:2048].rearrange("p (s c n) -> p s c n", s=2, c=KC)
        hmid = sreg[:, 2048:2560].rearrange("p (s n) -> p s n", s=2)
        smid = grow[:, 0].rearrange("p (t n) -> p t n", t=NT)
        hmT = sreg[:, 2560:3072].rearrange("p (s c n) -> p s c n", s=2, c=2)
        lamv = sreg[:, 2048:2304].rearrange("p (i d) -> p i d", i=4)
        wbd = sreg[:, 2304:2560].rearrange("p (j n) -> p j n", j=2)
        bd = sreg[:, 2560:3072].rearrange("p (j s n) -> p j s n", j=2, s=2)
        ropet = freg[:, 1024:1536].rearrange("p (t s d) -> p t s d", t=NT, s=2)
        qz = freg[:, 0:512].rearrange("p (s m n) -> p s m n", s=2, m=2)
        onrm = freg[:, 512:768].rearrange("p (s n) -> p s n", s=2)
        junk = freg[:, 768:896]
        silc = grow[:, 1, 0:256].rearrange("p (c s) -> p c s", c=KC)
        osb = grow[:, 1, 256:512].rearrange("p (s n) -> p s n", s=2)
        FT = freg[:, 0:1024].rearrange("p (j n) -> p j n", j=2)
        aT = freg[:, 1024:2560].rearrange("p (s n) -> p s n", s=2)
        sq = freg[:, 1024:2048]
        yb = freg[:, 0:2048].rearrange("p (s n) -> p s n", s=2)
        scT = freg[:, 0:256]
        gsil = freg[:, 2048:2560].rearrange("p (s n) -> p s n", s=2)

        ident = const[:, C_ID:C_ID + P]
        tri = const[:, C_TRI:C_TRI + P]
        iota = const[:, C_IOTA:C_IOTA + NB]

        cond_in, const_in, small_in, late_in = sem("cond_in"), sem("const_in"), sem("small_in"), sem("late_in")
        wbd_zero, wbd_in = sem("wbd_zero"), sem("wbd_in")
        x_in = [sem(f"x_in{t}") for t in range(NCT + NT)]
        item_in = [sem(f"item_in{s}") for s in range(NFRONT)]
        dve_step, pool_step = sem("dve_step"), sem("pool_step")
        setup = sem("setup")
        silc_ready, lam_sum, lam_exp = sem("silc_ready"), sem("lam_sum"), sem("lam_exp")
        squares, rms_ready, xn_ready = sem("squares"), sem("rms_ready"), sem("xn_ready")
        bd_done, bd_ready = sem("bd_done"), sem("bd_ready")
        mod_done, mod_ready = sem("mod_done"), sem("mod_ready")
        tlat_done, tctx_done = sem("tlat_done"), sem("tctx_done")
        hlat_raw, hctx_raw = sem("hlat_raw"), sem("hctx_raw")
        hlat_ready, hctx_ready = sem("hlat_ready"), sem("hctx_ready")
        proj_done, roped, rope_sum, copied = sem("proj_done"), sem("roped"), sem("rope_sum"), sem("copied")
        turn_done, turn_out = sem("turn_done"), sem("turn_out")
        g_done, g_ready, fmix_done, fmix_ready = sem("g_done"), sem("g_ready"), sem("fmix_done"), sem("fmix_ready")
        q_staged = sem("q_staged")
        s_done = [sem("s_done0"), sem("s_done1")]
        nmax = [sem("nmax0"), sem("nmax1")]
        exped = [sem("exped0"), sem("exped1")]
        combined, at_done = sem("combined"), sem("at_done")
        at_out = [sem("at_out_act"), sem("at_out_dve")]
        pv_done, o_copied, o_square, o_rms, o_normed = sem("pv_done"), sem("o_copied"), sem("o_square"), sem("o_rms"), sem("o_normed")
        ot_done, ot_out = sem("ot_done"), sem("ot_out")
        rowc_ready, row_done = sem("rowc_ready"), sem("row_done")
        row_out = [sem("row_out_act"), sem("row_out_dve")]
        pool_tick = sem("pool_tick")
        wo_done, y_square, y_rms, y_scaled, x1_ready = (sem(n) for n in ("wo_done", "y_square", "y_rms", "y_scaled", "x1_ready"))
        x1_square, x1_rms, h_scaled, h2_ready = (sem(n) for n in ("x1_square", "x1_rms", "h_scaled", "h2_ready"))
        h2_stored = [sem("h2_stored0"), sem("h2_stored1")]
        h2t_done, h2t_act, h2t_dve = sem("h2t_done"), sem("h2t_act"), sem("h2t_dve")
        logits_done, scores_ready, mask_ready, pos_done = sem("logits_done"), sem("scores_ready"), sem("mask_ready"), sem("pos_done")
        place_ready, places, table_copied, table_spread, xg_zero = (
            sem(n) for n in ("place_ready", "places", "table_copied", "table_spread", "xg_zero"))
        scores_turned = sem("scores_turned")
        hot_ready, hot_used, slots_ready, steer_ready = sem("hot_ready"), sem("hot_used"), sem("slots_ready"), sem("steer_ready")
        sgu_done, s_gate, s_up, s_mid, smt_done, smt_out, sy_done, sy_out = (
            sem(n) for n in ("sgu_done", "s_gate", "s_up", "s_mid", "smt_done", "smt_out", "sy_done", "sy_out"))
        shd_in = sem("shd_in")
        w_in = [sem(f"w_in{s}") for s in range(U)]
        d_in = [sem(f"d_in{s}") for s in range(U)]
        take_ready, put_ready = sem("take_ready"), sem("put_ready")
        xg_in = [sem(f"xg_in{s}") for s in range(U)]
        gu_done, gate_ready, mid_ready = sem("gu_done"), sem("gate_ready"), sem("mid_ready")
        mt_done, mt_out = sem("mt_done"), sem("mt_out")
        xt_done, xt_act, xt_dve = sem("xt_done"), sem("xt_act"), sem("xt_dve")
        dn_done, y_act, y_dve = sem("dn_done"), sem("y_act"), sem("y_dve")
        y_out = [sem("y_out0"), sem("y_out1")]
        moe_done = sem("moe_done")
        r_in = [sem(f"r_in{c}") for c in range(2 * NT)]
        r_red, r_sum, r_square, r_rms, r_scaled, r_gated, stored = (
            sem(n) for n in ("r_red", "r_sum", "r_square", "r_rms", "r_scaled", "r_gated", "stored"))
        r_fin = [sem("r_fin_pool"), sem("r_fin_dve")]

        CHUNK_TILES = [range(2, 6), range(2, 6), range(6), range(6), range(6)]
        proj_units = [(c, t) for c in range(5) for t in CHUNK_TILES[c]]
        chunk_end = [max(i for i, (c, _) in enumerate(proj_units) if c == k) + 1 for k in range(5)]
        mod_items = lambda m: [(f"mod{m}{h}", mod_done, m + 1) for h in range(2)]
        items = mod_items(0) + mod_items(1) + [(f"win{c}", proj_done, chunk_end[c]) for c in range(5)]
        items += [("dft", fmix_done, 2)]
        for m in range(2, 6):
            items += mod_items(m)
        items += [("wo0", wo_done, NT), ("wo1", wo_done, NT), ("shgu", sgu_done, NT)]
        place = {name: i for i, (name, _, _) in enumerate(items)}

        def item(name):
            s = place[name] % NFRONT
            return ring[:, s * FRONT:(s + 1) * FRONT]

        def item_landed(eng, name):
            i = place[name]
            eng.wait_ge(item_in[i % NFRONT], 16 * (i // NFRONT + 1))

        def source(name):
            if name.startswith("mod"):
                m, h = int(name[3]), int(name[4])
                w = A["w_mod"][0].rearrange("(p c) n -> p c n", c=KC)
                return [(item(name).rearrange("p (c n) -> p c n", c=4), w[:, 4 * h:4 * h + 4, m * D:(m + 1) * D])]
            if name.startswith("win"):
                c = int(name[3])
                w = A["w_in"][0].rearrange("(p c) n -> p c n", c=KC)
                return [(item(name).rearrange("p (c n) -> p c n", c=KC), w[:, :, c * 512:(c + 1) * 512])]
            if name == "dft":
                return [(item(name), A["dft"])]
            if name.startswith("wo"):
                n = int(name[2])
                w = A["w_out"][0].rearrange("(c p) n -> p c n", p=P)
                return [(item(name).rearrange("p (c n) -> p c n", c=MIXC), w[:, :, n * 512:(n + 1) * 512])]
            v = item(name).rearrange("p (s n) -> p s n", s=2)
            return [(v[:, 0], A["ws_gate"][0].rearrange("(p c) n -> p (c n)", c=KC)),
                    (v[:, 1], A["ws_up"][0].rearrange("(p c) n -> p (c n)", c=KC))]

        def landed_shared(eng):
            i = place["shgu"]
            eng.wait_ge(item_in[i % NFRONT], 16 * (i // NFRONT + 2))

        shd = ring[:, 3 * WBUF:3 * WBUF + GU_W]

        def wbuf(s):
            k = 1 + (s + 2) % U
            return heap[:, k * WBUF:(k + 1) * WBUF]

        def gate_up(buf):
            return buf[:, 0:2 * GU_W].rearrange("p (w c n) -> p w c n", w=2, c=KC)

        def down(buf):
            return buf[:, 2 * GU_W:].rearrange("p (c n) -> p c n", c=2)

        def done_scatters(g, u):
            k = (u - 3) // 2 + 1 if (u - 1) % 2 == 0 else (u - 4) // 2 + 1
            return g * (32 * U // 2) + 32 * k

        def ranks(c):
            k = 1 + c % RBUFS
            return heap[:, k * 4096:(k + 1) * 4096].rearrange("p (k n) -> p k n", k=TOPK)

        rsum = lambda c: sreg[:, 1024 + 512 * (c % 2):1536 + 512 * (c % 2)]
        part = lambda t, h: shy[:, t, 512 * h:512 * h + 512]
        pool_part, dve_part = (lambda v, t: v[:, t, 0:256]), (lambda v, t: v[:, t, 256:D])

        def halves(bank):
            return ps[:, bank].rearrange("p (a w n) -> p a w n", a=2, w=2)

        def hot(t):
            places_, blocks = ((freg[:, 512:512 + TOPK * P], qreg[:, D:D + TOPK * 2 * NB]),
                               (hreg[:, 0:TOPK * P], hreg[:, TOPK * P:TOPK * (P + 2 * NB)]))[t % 2]
            ph = places_.rearrange("p (k n) -> p k n", k=TOPK)
            bvw = blocks.rearrange("p (k n) -> p k n", k=TOPK)
            return ph, bvw

        def proj_plan():
            pe_turns, act_steps, dve_steps, pool_steps = [], [], [], []
            n_rope = n_copy = n_turn = 0
            unit_free = []
            for i, (c, t) in enumerate(proj_units):
                bank, tok = i % 4, t * P
                rope = t >= NCT and c < 4
                width = (512, 512, 512, 256, 0)[c]
                slot = n_turn % 2
                if rope:
                    n_rope += 1
                    unit_free.append((roped, n_rope))

                    def dve_step_(e, i=i, c=c, t=t, bank=bank, width=width, slot=slot, n=n_turn):
                        e.wait_ge(proj_done, i + 1)
                        if n >= 2:
                            e.wait_ge(turn_done, n - 1)
                        lo = FW if c == 0 else 0
                        g = (width - lo) // HD
                        src = ps[:, bank, lo:width]
                        a, b = ropeA[:, slot, lo:width], ropeB[:, slot, lo:width]
                        cs = ropet[:, t - NCT, 0].unsqueeze(1).broadcast_to([P, g, HD])
                        sn = ropet[:, t - NCT, 1].rearrange("p (a h i) -> p a h i", a=2, h=2)
                        e.tensor_tensor(a.rearrange("p (g d) -> p g d", d=HD), src.rearrange("p (g d) -> p g d", d=HD),
                                        cs, ALU.mult)
                        sv = src.rearrange("p (g a h i) -> p g a h i", a=2, h=2, i=16)
                        bv = b.rearrange("p (g a h i) -> p g a h i", a=2, h=2, i=16)
                        if c == 0:
                            e.tensor_copy(ropeA[:, slot, 0:FW], ps[:, bank, 0:FW])
                        if c == 3:
                            e.tensor_copy(vt[:, t, 0:256], ps[:, bank, 256:512])
                        for x in range(2):
                            snx = sn[:, x].unsqueeze(1).broadcast_to([P, g, 2, 16])
                            for half in range(2):
                                snh = sn[:, x, half].unsqueeze(1).broadcast_to([P, g, 16])
                                last = e.tensor_tensor(bv[:, :, x, half], sv[:, :, x, 1 - half], snh, ALU.mult)
                        last.then_inc(roped, 1)

                    dve_steps.append(dve_step_)

                    def pool_step_(e, c=c, width=width, slot=slot, n=n_rope):
                        e.wait_ge(roped, n)
                        lo = FW if c == 0 else 0
                        a, b = ropeA[:, slot, lo:width], ropeB[:, slot, lo:width]
                        e.tensor_tensor(a, a, b, ALU.add).then_inc(rope_sum, 1)

                    pool_steps.append(pool_step_)
                    staged = (rope_sum, n_rope)
                else:
                    n_copy += 1
                    unit_free.append((copied, n_copy))

                    def copy_step(e, i=i, c=c, t=t, bank=bank, width=width, slot=slot, n=n_turn):
                        e.wait_ge(proj_done, i + 1)
                        if width and n >= 2:
                            e.wait_ge(turn_done, n - 1)
                        if width:
                            last = e.activation(ropeA[:, slot, 0:width], ps[:, bank, 0:width], ACT.Copy)
                        if width < 512:
                            v0 = 0 if c == 3 else 256
                            last = e.activation(vt[:, t, v0:v0 + 512 - width], ps[:, bank, width:512], ACT.Copy)
                        last.then_inc(copied, 1)

                    act_steps.append(copy_step)
                    staged = (copied, n_copy)
                if width:
                    n_turn += 1
                    pe_turns.append((i, slot, width // P, staged))

                    def turn_out_step(e, c=c, t=t, width=width, n=n_turn):
                        e.wait_ge(turn_done, n)
                        bank = 4 + (n - 1) % 2
                        v = ps[:, bank].rearrange("p (h n) -> p h n", h=4)
                        tl = (t - NCT) * P
                        qv = qT.rearrange("p (h n) -> p h n", h=HEADS)
                        kv = kT.rearrange("p (h n) -> p h n", h=HEADS)
                        if c == 0:
                            e.activation(FT[:, :, tl:tl + P], v[:, 0:2], ACT.Copy)
                            last = e.activation(qv[:, 0:2, tl:tl + P], v[:, 2:4], ACT.Copy, scale=HD ** -0.5)
                        elif c == 1:
                            last = e.activation(qv[:, 2:6, tl:tl + P], v, ACT.Copy, scale=HD ** -0.5)
                        elif c == 2:
                            last = e.activation(kv[:, 0:4, t * P:(t + 1) * P], v, ACT.Copy)
                        else:
                            last = e.activation(kv[:, 4:6, t * P:(t + 1) * P], v[:, 0:2], ACT.Copy)
                        last.then_inc(turn_out, 1)

                    act_steps.append(turn_out_step)
                else:
                    pe_turns.append(None)
            return {"pe": pe_turns, "act": act_steps, "dve": dve_steps, "pool": pool_steps, "free": unit_free}

        plan_proj = proj_plan()

        NSMALL, NLATE = 6, 7
        block = ctx.enter_context(nc.Block())

        @block.sync
        def _(sp):
            col = lambda a: a.rearrange("(p c) -> p c", c=KC)
            sp.dma_start(colc[:, 0], col(A["c"][0])).then_inc(cond_in, 16)
            sp.dma_start(colc[:, 1], col(A["c_ctx"])).then_inc(cond_in, 16)
            sp.dma_start(const[:], A["consts"]).then_inc(const_in, 16)
            xl = A["x"][0].rearrange("(t p) n -> t p n", p=P)
            xc = A["ctx"][0].rearrange("(t p) n -> t p n", p=P)
            for t in range(NCT):
                sp.dma_start(xctx[:, t], xc[t]).then_inc(x_in[t], 16)
            for t in range(NT):
                sp.dma_start(xres[:, t], xl[t]).then_inc(x_in[NCT + t], 16)
            for i, (name, _, _) in enumerate(items):
                if i >= NFRONT:
                    _, used, count = items[i - NFRONT]
                    sp.wait_ge(used, count)
                for dst, src in source(name):
                    sp.dma_start(dst, src).then_inc(item_in[i % NFRONT], 16)
            for t in range(NT):
                sp.wait_ge(h2_ready, t + 1)
                sp.dma_start(h2_dram[t * P:(t + 1) * P, :], h2[:, t % 2]).then_inc(h2_stored[t % 2], 16)

            def load_expert(s, e):
                v = gate_up(wbuf(s))
                sp.dma_start(v[:, 0], A["w_gate"][0, e].rearrange("(p c) n -> p c n", c=KC)).then_inc(w_in[s], 16)
                sp.dma_start(v[:, 1], A["w_up"][0, e].rearrange("(p c) n -> p c n", c=KC)).then_inc(w_in[s], 16)
                sp.dma_start(down(wbuf(s)), A["w_down"][0, e].rearrange("(c p) n -> p c n", c=2)).then_inc(d_in[s], 16)

            def next_expert(g, u):
                code = [sp.value_load(steer[0:1, at(u * (NB // U) + g - i, 1)], min_val=0,
                                      max_val=2 * (NE // U) - 1) for i in range(2)]
                return code[0] >> 1, code[1] >> 1

            def expert(number, u):
                return bass.ds(number.with_bounds(min_val=1, max_val=NE // U - 1) * U + u, 1)

            def load_gate_up(g, u):
                now, before = next_expert(g, u)
                sp.wait_ge(gu_done, g * U + (u - U + 1))
                with sp.If(now > before):
                    v = gate_up(wbuf(u))
                    for k, name in enumerate(("w_gate", "w_up")):
                        w = A[name][0].rearrange("e (p c) n -> p e (c n)", c=KC)
                        sp.dma_start(v[:, k].rearrange("p c n -> p (c n)").unsqueeze(1),
                                     w[:, expert(now, u)]).then_inc(w_in[u], 16)

            def load_down(g, u):
                now, before = next_expert(g, u)
                sp.wait_ge(dn_done, g * U + (u - U + 1))
                with sp.If(now > before):
                    w = A["w_down"][0].rearrange("e (c p) n -> p e c n", c=2)
                    sp.dma_start(down(wbuf(u)).unsqueeze(1), w[:, expert(now, u)]).then_inc(d_in[u], 16)

            sp.dma_start(shd, A["ws_down"][0].rearrange("(p c) n -> p (c n)", c=2)).then_inc(shd_in, 16)
            load_expert(0, 0)
            load_expert(1, 1)
            for s in h2_stored:
                sp.wait_ge(s, 16 * NT // 2)
            sp.wait_ge(h2t_done, NT)
            load_expert(2, 2)
            sp.wait_ge(sgu_done, NT)
            load_expert(3, 3)
            sp.wait_ge(steer_ready, 1)
            turns = sp.value_load(steer[0:1, NB:NB + 1], min_val=0, max_val=TURNS - 1) + 1
            with sp.Fori(0, SPANS) as q:
                with sp.If(q * SPAN + 1 < turns):
                    with sp.Fori(1, SPAN + 1) as i:
                        g = (q * SPAN + i).with_bounds(min_val=1, max_val=TURNS - 1)
                        with sp.If(g < turns):
                            for u in range(U + 1):
                                if u:
                                    load_down(g, u - 1)
                                if u < U:
                                    load_gate_up(g, u)
            sp.wait_ge(moe_done, 1)
            yv = y_dram.rearrange("(t p k) (h n) -> t h p k n", p=P, k=TOPK, h=2)
            for c in range(2 * NT):
                if c >= RBUFS:
                    sp.wait_ge(r_red, c - RBUFS + 1)
                sp.dma_start(ranks(c), yv[c // 2, c % 2]).then_inc(r_in[c], 16)
            for t in range(NT):
                for x in r_fin:
                    sp.wait_ge(x, t + 1)
                sp.dma_start(A["out"][0, t * P:(t + 1) * P, :], shy[:, t]).then_inc(stored, 16)
            sp.wait_ge(stored, 16 * NT)
            for s in h2_stored:
                sp.wait_ge(s, 16 * NT // 2)

        @block.scalar
        def _(act):
            col = lambda a: a.rearrange("(p c) -> p c", c=KC)
            small = [(bmod[:], A["b_mod"][0].rearrange("(m p c) -> p m c", m=6, c=KC)),
                     (gain[:, 0], col(A["g_attn_pre"][0])), (gain[:, 1], col(A["g_attn_post"][0])),
                     (gain[:, 2], col(A["g_ffn_pre"][0])), (gain[:, 3], col(A["g_ffn_post"][0])),
                     (gsub[:, 0:1], A["g_subln"][0].rearrange("(p c) -> p c", c=1))]
            late = [(ropet, A["rope"].rearrange("(t p) s n -> p t s n", p=P)),
                    (wrt[:], A["w_router"][0].rearrange("(p c) n -> p c n", c=KC)),
                    (rbias[:], A["router_bias"][0].partition_broadcast(P))]
            late += [(lamv[:, i], A[n][0].partition_broadcast(P))
                     for i, n in enumerate(("lambda_q1", "lambda_k1", "lambda_q2", "lambda_k2"))]
            assert len(small) == NSMALL and len(late) == NLATE
            for dst, src in small:
                act.dma_start(dst, src).then_inc(small_in, 16)
            act.wait_ge(cond_in, 32)
            act.wait_ge(wbd_zero, 2)
            act.activation(silc[:, :, 0:2].rearrange("p c s -> p s c"), colc[:], ACT.Silu).then_inc(silc_ready, 1)
            for t in range(NCT + NT):
                act.wait_ge(x_in[t], 16)
                src = xctx[:, t] if t < NCT else xres[:, t - NCT]
                act.activation(xn[:, t], src, ACT.Square, accum_out=nrm[:, 0, t:t + 1]).then_inc(squares, 1)
            for dst, src in late:
                act.dma_start(dst, src).then_inc(late_in, 16)
            for g in range(4):
                r = slice(64 * (g % 2), 64 * (g % 2) + 64)
                act.dma_start(wbd[r, g // 2, r], A["w_fourier"][0, g]).then_inc(wbd_in, 16)
            for c in range(KC):
                act.wait_ge(tctx_done, c + 1)
                act.activation(hT[:, c, 0:NCTX], ps[:, 2 + c % 2, 0:NCTX], ACT.Copy).then_inc(hctx_raw, 1)
            act.wait_ge(mod_ready, 3)
            for c in range(KC):
                act.wait_ge(hctx_raw, c + 1)
                act.activation(hT[:, c, 0:NCTX], hT[:, c, 0:NCTX], ACT.Identity,
                               bias=modc[:, 0, c, 1:2], scale=scl1[:, c, 1:2]).then_inc(hctx_ready, 1)
            act.wait_ge(lam_sum, 1)
            act.activation(lam[:, 2:4], lam[:, 0:2], ACT.Exp).then_inc(lam_exp, 1)
            for step in plan_proj["act"]:
                step(act)
            for t in range(0, NT, 2):
                act.wait_ge(g_done, t + 1)
                act.activation(fg[:, t].rearrange("p j s n -> p (j s n)"), ps[:, t], ACT.Copy).then_inc(g_ready, 1)
            act.wait_ge(fmix_done, 2)
            for j in range(2):
                act.activation(mixTv[:, j], ps[:, 4 + j], ACT.Copy).then_inc(fmix_ready, 1)

            def exps(n, h, qt):
                need(act, at_done, n - 1)
                for m in range(2):
                    act.wait_ge(nmax[m], n + 1)
                    act.activation(prob[:, qt % 2, m], psf[:, 1024 * m:1024 * m + NTOK], ACT.Exp,
                                   bias=stat[:, qt, m:m + 1], accum_out=stat[:, qt, 2 + m:3 + m]).then_inc(exped[m], 1)

            def at_evac(n, qt):
                act.wait_ge(at_done, n + 1)
                act.activation(aT[:, qt % 2, 0:512], ps[:, 4], ACT.Copy).then_inc(at_out[0], 1)

            def square(n, qt):
                act.wait_ge(pv_done, n + 1)
                act.wait_ge(combined, n + 1)
                act.activation(osb[:, qt % 2], ps[:, 6, 0:VD], ACT.Copy, scale=stat[:, qt, 4:5]).then_inc(o_copied, 1)
                act.wait_ge(o_copied, n + 1)
                act.activation(junk, osb[:, qt % 2], ACT.Square, accum_out=stat[:, qt, 7:8]).then_inc(o_square, 1)

            def ot_evac(n, h, qt):
                act.wait_ge(ot_done, n + 1)
                act.activation(mixT[:, at((2 + h) * NLAT + qt * P, P)], ps[:, 7, 0:P], ACT.Copy,
                               scale=gsub[:, 1:2]).then_inc(ot_out, 1)

            def act_unit(h, u):
                n = h * NT + u
                first = isinstance(h, int) and h == 0
                if not first or u >= 2:
                    at_evac(n - 2, (u - 2) % 4)
                exps(n, h, u)
                if not first or u >= 3:
                    square(n - 3, (u - 3) % 4)
                if not first:
                    ot_evac(n - 4, h - 1, u)

            act.wait_ge(setup, 1)
            for u in range(NT):
                act_unit(0, u)
            with act.Fori(1, HEADS) as h:
                for u in range(NT):
                    act_unit(h, u)
            at_evac(UNITS - 2, 2)
            square(UNITS - 3, 1)
            ot_evac(UNITS - 4, HEADS - 1, 0)
            at_evac(UNITS - 1, 3)
            square(UNITS - 2, 2)
            ot_evac(UNITS - 3, HEADS - 1, 1)
            square(UNITS - 1, 3)
            ot_evac(UNITS - 2, HEADS - 1, 2)
            ot_evac(UNITS - 1, HEADS - 1, 3)

            for i in range(0, 8, 2):
                act.wait_ge(row_done, i + 1)
                row_dst = (grow[:, 0], srow[:, 0], srow[:, 1], grow[:, 1])[i // 2]
                act.activation(row_dst.rearrange("p (j c) -> p c j", c=KC)[:, 0:4],
                               ps[:, 4].rearrange("p (c j) -> p c j", c=4), ACT.Copy).then_inc(row_out[0], 1)

            def h2t_evac(t):
                act.wait_ge(h2t_done, t + 1)
                act.activation(hT2[:, 0:4, t * P:(t + 1) * P], ps[:, 4].rearrange("p (c n) -> p c n", c=4), ACT.Copy)\
                    .then_inc(h2t_act, 1)

            for t in range(NT):
                act.wait_ge(wo_done, t + 1)
                b = 2 * (t % 2)
                act.activation(sq, psf[:, b * 512:b * 512 + D], ACT.Square, accum_out=nrm[:, 0, 6 + t:7 + t])\
                   .then_inc(y_square, 1)
                act.wait_ge(x1_ready, t + 1)
                act.wait_ge(y_square, t + 1)
                act.activation(sq, xres[:, t], ACT.Square, accum_out=nrm[:, 0, 10 + t:11 + t]).then_inc(x1_square, 1)
                act.wait_ge(x1_square, t + 1)
                if t >= 2:
                    h2t_evac(t - 2)
            h2t_evac(NT - 2)
            h2t_evac(NT - 1)
            act.wait_ge(logits_done, 1)
            act.activation(scT, ps[:, 7, 0:256], ACT.Sigmoid).then_inc(scores_ready, 1)

            def shared_gate(t):
                act.wait_ge(sgu_done, t + 1)
                if t >= 2:
                    act.wait_ge(s_mid, t - 1)
                act.activation(gsil[:, t % 2], ps[:, t % 2, 0:DE], ACT.Silu).then_inc(s_gate, 1)
                act.activation(sreg[:, 1024 + (t % 2) * DE:1024 + (t % 2) * DE + DE], ps[:, t % 2, DE:2 * DE], ACT.Copy)\
                   .then_inc(s_up, 1)

            def shared_out(t):
                act.wait_ge(smt_done, t + 1)
                act.activation(hmT[:, t % 2], ps[:, 6, 0:256].rearrange("p (c n) -> p c n", c=2), ACT.Copy)\
                   .then_inc(smt_out, 1)

            def shared_y(t):
                act.wait_ge(sy_done, t + 1)
                act.activation(shy[:, t], psf[:, 1024:2048], ACT.Copy).then_inc(sy_out, 1)

            for t in range(NT):
                shared_gate(t)

            def x_evac(n, s):
                act.wait_ge(xt_done, n + 1)
                act.activation(xgT[:, s, 0:4], ps[:, 4].rearrange("p (c n) -> p c n", c=4), ACT.Copy)\
                   .then_inc(xt_act, 1)

            x_evac(0, 0)

            def mid_evac(n, s):
                act.wait_ge(mt_done, n + 1)
                act.activation(hmT[:, s], ps[:, 6, 0:256].rearrange("p (c n) -> p c n", c=2), ACT.Copy)\
                   .then_inc(mt_out, 1)

            def y_evac(b, u):
                act.wait_ge(put_ready, b + 1)
                act.wait_ge(dn_done, b + 1)
                w = put[:, u, 2:3].bitcast(F32)
                act.activation(yb[:, u % 2, 0:512], ps[:, 2], ACT.Copy, scale=w).then_inc(y_act, 1)

            def act_block(g, u):
                b = g * U + u
                first = isinstance(g, int) and b == 0
                if not first:
                    mid_evac(b - 1, (u - 1) % 2)
                act.wait_ge(gu_done, b + 1)
                act.activation(gsil[:, u % 2].rearrange("p (a n) -> p a n", a=2), halves(u % 2)[:, :, 0], ACT.Silu)\
                    .then_inc(gate_ready, 1)
                x_evac(b + 1, (u + 1) % 2)
                if not first:
                    need(act, y_out[(u - 1) % 2], done_scatters(g, u))
                    y_evac(b - 1, (u - 1) % U)

            def act_ending(g):
                mid_evac(g * U - 1, 1)
                act.wait_ge(y_out[1], done_scatters(g, 0))
                y_evac(g * U - 1, U - 1)

            for u in range(U):
                act_block(0, u)
            act.wait_ge(steer_ready, 1)
            turns = act.value_load(steer[0:1, NB:NB + 1], min_val=0, max_val=TURNS - 1) + 1
            with act.Fori(0, SPANS) as q:
                with act.If(q * SPAN + 1 < turns):
                    with act.Fori(1, SPAN + 1) as i:
                        g = (q * SPAN + i).with_bounds(min_val=1, max_val=TURNS - 1)
                        with act.If(g < turns):
                            for u in range(U):
                                act_block(g, u)
            act_ending(turns)
            for t in range(NT):
                shared_out(t)
                shared_y(t)
            for t in range(NT):
                act.wait_ge(r_sum, 2 * t + 2)
                act.activation(sreg[:, 0:1024], shy[:, t], ACT.Square, accum_out=nrm[:, 0, 14 + t:15 + t])\
                   .then_inc(r_square, 1)
                act.wait_ge(r_square, t + 1)
                act.wait_ge(r_rms, t + 1)
                act.activation(pool_part(shy, t), pool_part(shy, t), ACT.Copy, scale=nrm[:, 2, 14 + t:15 + t]).then_inc(r_scaled, 1)

        @block.tensor
        def _(pe):
            mm = nc.tensor.matmul
            def modulation(m):
                item_landed(pe, f"mod{m}0")
                if m >= 2:
                    pe.wait_ge(mod_ready, m - 1 if m < 4 else m)
                w = [item(f"mod{m}{h}").rearrange("p (k n) -> p k n", k=4) for h in range(2)]
                for k in range(KC):
                    if k == 4:
                        item_landed(pe, f"mod{m}1")
                    for g in range(4):
                        last = mm(ps[32 * g:32 * g + 32, 6 + m % 2, 0:256], silc[:, k],
                                  w[k // 4][:, k % 4, 256 * g:256 * g + 256], start=(k == 0), stop=(k == KC - 1))
                last.then_inc(mod_done, 1)

            pe.wait_ge(const_in, 16)
            pe.wait_ge(xn_ready, NCT + NT)
            for c in range(KC):
                if c >= 2:
                    pe.wait_ge(hlat_raw, c - 1)
                    pe.wait_ge(hctx_raw, c - 1)
                for t in range(NCT + NT):
                    out = ps[:, 2 + c % 2, t * P:(t + 1) * P] if t < NCT else \
                        ps[:, c % 2, (t - NCT) * P:(t - NCT + 1) * P]
                    v = xn[:, t].rearrange("p (j c) -> p j c", c=KC)[:, :, c]
                    last = nc.tensor.transpose(out, v, ident)
                    if t == NCT - 1:
                        last.then_inc(tctx_done, 1)
                last.then_inc(tlat_done, 1)
            pe.wait_ge(silc_ready, 1)
            modulation(0)
            modulation(1)
            pe.wait_ge(hlat_raw, KC)
            pe.wait_ge(hctx_raw, KC)
            turns = plan_proj["pe"]
            n_turn = 0

            def turn(k):
                nonlocal n_turn
                if turns[k] is None:
                    return
                _, slot, nh, staged = turns[k]
                pe.wait_ge(*staged)
                if n_turn >= 2:
                    pe.wait_ge(turn_out, n_turn - 1)
                for x in range(nh):
                    last = nc.tensor.transpose(ps[:, 4 + n_turn % 2, x * P:(x + 1) * P],
                                               ropeA[:, slot, x * P:(x + 1) * P], ident)
                last.then_inc(turn_done, 1)
                n_turn += 1

            for i, (c, t) in enumerate(proj_units):
                item_landed(pe, f"win{c}")
                if i >= 4:
                    pe.wait_ge(*plan_proj["free"][i - 4])
                w = item(f"win{c}").rearrange("p (c n) -> p c n", c=KC)
                for k in range(KC):
                    if i == 0:
                        pe.wait_ge(hlat_ready, k + 1)
                    if k == 0 and t < NCT:
                        pe.wait_ge(hctx_ready, KC)
                    last = mm(ps[:, i % 4], hT[:, k, t * P:(t + 1) * P], w[:, k], start=(k == 0), stop=(k == KC - 1))
                last.then_inc(proj_done, 1)
                if i == 0:
                    pe.wait_ge(wbd_in, 64)
                    for j in range(2):
                        for s in range(2):
                            last = mm(ps[:, 7, (2 * j + s) * P:(2 * j + s + 1) * P],
                                      const[:, (C_CC, C_SC)[s]:(C_CC, C_SC)[s] + P], wbd[:, j], start=True, stop=True)
                    last.then_inc(bd_done, 1)
                if i:
                    turn(i - 1)
            turn(len(proj_units) - 1)
            pe.wait_ge(*plan_proj["free"][-1])
            pe.wait_ge(roped, sum(1 for s, _ in plan_proj["free"] if s is roped))
            pe.wait_ge(turn_out, n_turn)
            pe.wait_ge(bd_ready, 1)
            for t in range(NT):
                for j in range(2):
                    last = mm(ps[:, t, 256 * j:256 * j + 256], FT[:, j, t * P:(t + 1) * P],
                              bd[:, j].rearrange("p s n -> p (s n)"), start=True, stop=True)
                last.then_inc(g_done, 1)
            item_landed(pe, "dft")
            dft = item("dft").rearrange("p (s t n) -> p s t n", s=2, t=NT)
            pe.wait_ge(g_ready, NT)
            for j in range(2):
                for t in range(NT):
                    for s in range(2):
                        last = mm(ps[:, 4 + j], fg[:, t, j, s], dft[:, s, t], start=(t == 0 and s == 0),
                                  stop=(t == NT - 1 and s == 1))
                last.then_inc(fmix_done, 1)
            for m in range(2, 4):
                modulation(m)

            def scores(n, h, qt, m):
                if m == 0:
                    pe.wait_ge(q_staged, n + 1)
                need(pe, exped[m], n)
                mm(ps[:, 2 * m], qz[:, qt % 2, m], kT[:, at(h * NTOK, 512)], start=True, stop=True)
                mm(ps[:, 2 * m + 1, 0:256], qz[:, qt % 2, m], kT[:, at(h * NTOK + 512, 256)],
                   start=True, stop=True).then_inc(s_done[m], 1)

            def values(n, h, qt):
                pe.wait_ge(at_out[0], n + 1)
                pe.wait_ge(at_out[1], n + 1)
                need(pe, o_copied, n)
                for k in range(NCT + NT):
                    last = mm(ps[:, 6, 0:VD], aT[:, qt % 2, k * P:(k + 1) * P], vt[:, k, at(h * VD, VD)],
                              start=(k == 0), stop=(k == NCT + NT - 1))
                last.then_inc(pv_done, 1)

            def turn_probs(n, qt):
                pe.wait_ge(combined, n + 1)
                need(pe, at_out[0], n)
                need(pe, at_out[1], n)
                for k in range(NCT + NT):
                    last = nc.tensor.transpose(psf[:, 2048 + k * P:2048 + (k + 1) * P],
                                               prob[:, qt % 2, 0, k * P:(k + 1) * P], ident)
                last.then_inc(at_done, 1)

            def turn_out_rows(n, qt):
                pe.wait_ge(o_normed, n + 1)
                need(pe, ot_out, n)
                nc.tensor.transpose(ps[:, 7, 0:P], onrm[:, qt % 2], ident).then_inc(ot_done, 1)

            def pe_unit(h, u):
                n = h * NT + u
                first = isinstance(h, int) and h == 0
                scores(n, h, u, 0)
                if not first or u >= 2:
                    turn_probs(n - 2, (u - 2) % 4)
                scores(n, h, u, 1)
                if not first or u >= 3:
                    values(n - 3, h - (1 if u < 3 else 0), (u - 3) % 4)
                if not first:
                    turn_out_rows(n - 4, u)

            pe.wait_ge(fmix_ready, 2)
            pe.wait_ge(mod_ready, 5)
            for u in range(NT):
                pe_unit(0, u)
            with pe.Fori(1, HEADS) as h:
                for u in range(NT):
                    pe_unit(h, u)
            turn_probs(UNITS - 2, 2)
            values(UNITS - 3, HEADS - 1, 1)
            turn_out_rows(UNITS - 4, 0)
            turn_probs(UNITS - 1, 3)
            values(UNITS - 2, HEADS - 1, 2)
            turn_out_rows(UNITS - 3, 1)
            values(UNITS - 1, HEADS - 1, 3)
            turn_out_rows(UNITS - 2, 2)
            turn_out_rows(UNITS - 1, 3)

            pe.wait_ge(o_copied, UNITS)
            modulation(4)
            pe.wait_ge(ot_out, UNITS)
            modulation(5)
            pe.wait_ge(rowc_ready, 1)
            for i in range(8):
                r, half = i // 2, i % 2
                if i >= 2:
                    pe.wait_ge(row_out[half], i // 2)
                for c in range(4):
                    last = mm(ps[:, 4 + half, c * P:(c + 1) * P],
                              rowc[:, r, 4 * half + c:4 * half + c + 1].broadcast_to([P, P]), ident,
                              start=True, stop=True)
                last.then_inc(row_done, 1)
            pe.wait_ge(ot_out, UNITS)
            item_landed(pe, "wo0")
            w = [item(f"wo{n}").rearrange("p (c n) -> p c n", c=MIXC) for n in range(2)]

            def turn_h2(t):
                pe.wait_ge(h2_ready, t + 1)
                if t:
                    pe.wait_ge(h2t_act, t)
                    pe.wait_ge(h2t_dve, t)
                else:
                    pe.wait_ge(row_out[0], 4)
                    pe.wait_ge(row_out[1], 4)
                for c in range(KC):
                    last = nc.tensor.transpose(ps[:, 4 + c // 4, (c % 4) * P:(c % 4 + 1) * P],
                                               h2[:, t % 2].rearrange("p (j c) -> p j c", c=KC)[:, :, c], ident)
                last.then_inc(h2t_done, 1)

            for t in range(NT):
                if t >= 2:
                    pe.wait_ge(y_scaled, t - 1)
                for n in range(2):
                    if t == 0 and n == 1:
                        item_landed(pe, "wo1")
                    for c in range(MIXC):
                        last = mm(ps[:, 2 * (t % 2) + n], mixTv[:, c, t * P:(t + 1) * P], w[n][:, c],
                                  start=(c == 0), stop=(c == MIXC - 1))
                last.then_inc(wo_done, 1)
                if t >= 2:
                    turn_h2(t - 2)

            landed_shared(pe)
            gu = item("shgu").rearrange("p (w c n) -> p w c n", w=2, c=KC)
            dn = shd.rearrange("p (c n) -> p c n", c=2)

            def shared_gu(t):
                pe.wait_ge(*((s_up, t - 1) if t >= 2 else (y_scaled, NT - 1 + t)))
                pe.wait_ge(h2t_act, t + 1)
                pe.wait_ge(h2t_dve, t + 1)
                for k in range(KC):
                    last = mm(ps[:, t % 2], hT2[:, k, t * P:(t + 1) * P], gu[:, :, k], start=(k == 0), stop=(k == KC - 1))
                last.then_inc(sgu_done, 1)

            def shared_down(t):
                if t == 0:
                    pe.wait_ge(shd_in, 16)
                if t:
                    pe.wait_ge(smt_out, t)
                v = smid[:, t].rearrange("p (j c) -> p j c", c=2)
                for c in range(2):
                    last = nc.tensor.transpose(ps[:, 6, c * P:(c + 1) * P], v[:, :, c], ident)
                last.then_inc(smt_done, 1)
                pe.wait_ge(smt_out, t + 1)
                if t:
                    pe.wait_ge(sy_out, t)
                for n in range(2):
                    for c in range(2):
                        last = mm(ps[:, 2 + n], hmT[:, t % 2, c], dn[:, c, n * 512:(n + 1) * 512],
                                  start=(c == 0), stop=(c == 1))
                last.then_inc(sy_done, 1)

            shared_gu(0)
            turn_h2(NT - 2)
            turn_h2(NT - 1)
            pe.wait_ge(h2t_act, NT)
            pe.wait_ge(h2t_dve, NT)
            for k in range(KC):
                for h in range(2):
                    last = mm(ps[NE * h:NE * h + NE, 7, 0:256], wrt[:, k], hT2[:, k, 256 * h:256 * h + 256],
                              start=(k == 0), stop=(k == KC - 1))
            last.then_inc(logits_done, 1)
            pe.wait_ge(scores_ready, 1)
            for j in range(2):
                last = nc.tensor.transpose(ps[:, 7, 256 + P * j:256 + P * j + P], scT[:, P * j:P * j + P], ident)
            last.then_inc(scores_turned, 1)
            shared_gu(1)
            pe.wait_ge(mask_ready, 1)
            mask = rt[:, 256:512].rearrange("p (t e) -> p t e", t=NT)
            for t in range(NT):
                mm(ps[:, 4, t * NE:(t + 1) * NE], tri, mask[:, t], start=True, stop=(t == 0))
                for s in range(t):
                    mm(ps[:, 4, t * NE:(t + 1) * NE], ones[:], mask[:, s], start=False, stop=(s == t - 1))
            for t in range(NT):
                last = mm(ps[:, 5, 0:NE], ones[:], mask[:, t], start=(t == 0), stop=(t == NT - 1))
            last.then_inc(pos_done, 1)
            shared_gu(2)
            shared_gu(3)
            for t in range(NT):
                pe.wait_ge(hot_ready, t + 1)
                pe.wait_ge(places, t + 1)
                ph, bvw = hot(t)
                for k in range(TOPK):
                    last = mm(ps[:, 7, 0:2 * NB], ph[:, k], bvw[:, k], start=(t == 0 and k == 0),
                              stop=(t == NT - 1 and k == TOPK - 1))
                last.then_inc(hot_used, 1)

            pe.wait_ge(s_gate, 3)
            pe.wait_ge(s_up, 3)
            pe.wait_ge(table_copied, 1)
            for a in range(2):
                for n in range(2):
                    mm(ps[64 * n:64 * n + 64, 4 + a, 0:2 * NB], ident[:, 64 * a:64 * a + 64], table,
                       start=True, stop=True)
            mm(ps[0:1, 0, 0:NB], const[:, C_MAP + 1:C_MAP + 2], table[:, 0:NB], start=True, stop=True)
            for u in range(U):
                last = mm(ps[0:1, 0, NB + u * (NB // U):NB + (u + 1) * (NB // U)], freg[:, 224 + u:225 + u],
                          ident[:, 0:NB // U], start=True, stop=True)
            last.then_inc(table_spread, 1)

            def turn_x(n, s, k):
                pe.wait_ge(xg_in[s], 16 * (k + 1))
                for c in range(KC):
                    last = nc.tensor.transpose(ps[:, 4 + c // 4, (c % 4) * P:(c % 4 + 1) * P],
                                               xg[s].rearrange("p (j c) -> p j c", c=KC)[:, :, c], ident)
                last.then_inc(xt_done, 1)

            def pe_block(g, u):
                b = g * U + u
                first = isinstance(g, int) and b == 0
                code = pe.value_load(steer[0:1, at(u * (NB // U) + g, 1)], min_val=0, max_val=2 * (NE // U) - 1)
                if not first:
                    before = pe.value_load(steer[0:1, code_before(g, u)], min_val=0, max_val=2 * (NE // U) - 1)
                pe.wait_ge(w_in[u], 32 + 32 * (code >> 1))
                pe.wait_ge(xt_act, b + 1)
                pe.wait_ge(xt_dve, b + 1)
                need(pe, mid_ready, b - 1)
                gu = gate_up(wbuf(u))

                def gate_up_half(a):
                    for k in range(KC):
                        for f in range(2):
                            last = mm(halves(u % 2)[64 * f:64 * f + 64, a], xgT[:, u % 2, k, 64 * a:64 * a + 64],
                                      gu[:, :, k, P * f:P * f + P], start=(k == 0), stop=(k == KC - 1))
                    return last

                with pe.If((code & 1) > 0):
                    gate_up_half(1)
                if not first:
                    mid_turn(b, u)
                gate_up_half(0).then_inc(gu_done, 1)
                turn_x(b + 1, (u + 1) % U, g + (u + 1) // U)
                if not first:
                    down_turn(b, u, before)

            def code_before(g, u):
                return at((u - 1) % U * (NB // U) + (g if u else g - 1), 1)

            def mid_turn(b, u):
                pe.wait_ge(mid_ready, b)
                need(pe, mt_out, b - 1)
                for a in range(2):
                    last = nc.tensor.transpose(ps[:, 6, a * P:(a + 1) * P], hmid[:, (u - 1) % 2, a * P:(a + 1) * P], ident)
                last.then_inc(mt_done, 1)

            def down_turn(b, u, code):
                pe.wait_ge(d_in[(u - 1) % U], 16 + 16 * (code >> 1))
                pe.wait_ge(mt_out, b)
                need(pe, y_act, b - 1)
                need(pe, y_dve, b - 1)
                dn = down(wbuf((u - 1) % U))

                def down_half(a):
                    m = hmT[:, (u - 1) % 2].rearrange("p a (c n) -> p a c n", c=2)
                    for c in range(2):
                        for n in range(2):
                            last = mm(ps[64 * n:64 * n + 64, 2 + a], m[:, a, c], dn[:, c, n * 512:(n + 1) * 512],
                                      start=(c == 0), stop=(c == 1))
                    return last

                with pe.If((code & 1) > 0):
                    down_half(1)
                down_half(0).then_inc(dn_done, 1)

            def pe_ending(g):
                code = pe.value_load(steer[0:1, code_before(g, 0)], min_val=0, max_val=2 * (NE // U) - 1)
                mid_turn(g * U, 0)
                down_turn(g * U, 0, code)

            pe.wait_ge(slots_ready, 1)
            turn_x(0, 0, 0)
            pe.wait_ge(s_mid, NT)
            pe.wait_ge(steer_ready, 1)
            for u in range(U):
                pe_block(0, u)
            pe.wait_ge(steer_ready, 1)
            turns = pe.value_load(steer[0:1, NB:NB + 1], min_val=0, max_val=TURNS - 1) + 1
            with pe.Fori(0, SPANS) as q:
                with pe.If(q * SPAN + 1 < turns):
                    with pe.Fori(1, SPAN + 1) as i:
                        g = (q * SPAN + i).with_bounds(min_val=1, max_val=TURNS - 1)
                        with pe.If(g < turns):
                            for u in range(U):
                                pe_block(g, u)
            pe_ending(turns)
            pe.wait_ge(y_act, turns * U)
            pe.wait_ge(y_dve, turns * U)
            for t in range(NT):
                shared_down(t)

        @block.vector
        def _(dve):
            steps = [0]

            def link(ins):
                steps[0] += 1
                ins.then_inc(dve_step, 1)
                dve.wait_ge(dve_step, steps[0])

            dve.memset(wbd, 0.0).then_inc(wbd_zero, 1)
            dve.memset(silc, 0.0).then_inc(wbd_zero, 1)
            link(dve.memset(ones[:], 1.0))
            for t in range(NCT + NT):
                src = xctx[:, t] if t < NCT else xres[:, t - NCT]
                dve.wait_ge(x_in[t], 16)
                dve.wait_ge(rms_ready, t + 1)
                dve.tensor_scalar(xn[:, t], src, nrm[:, 2, t:t + 1], None, ALU.mult).then_inc(xn_ready, 1)
            for c in range(KC):
                dve.wait_ge(tlat_done, c + 1)
                dve.tensor_copy(hT[:, c, NCTX:], ps[:, c % 2]).then_inc(hlat_raw, 1)

            def modulation_out(m):
                dve.wait_ge(mod_done, m + 1)
                rows, cols = grow[:, 0, 0:256], grow[:, 0, 256:512]
                link(dve.tensor_copy(rows.rearrange("p (c j) -> p c j", c=KC),
                                     ps[:, 6 + m % 2, 0:256].rearrange("p (j c) -> p c j", c=KC)))
                link(dve.transpose(cols, rows))
                dve.tensor_tensor(modc[:, m], cols.rearrange("p (c s) -> p c s", c=KC)[:, :, 0:2],
                                  bmod[:, m].unsqueeze(2).broadcast_to([P, KC, 2]), ALU.add).then_inc(mod_ready, 1)
                dve.wait_ge(mod_ready, m + 1 if m < 2 else m + 2)

            dve.wait_ge(small_in, 16 * NSMALL)
            modulation_out(0)
            modulation_out(1)
            dve.wait_ge(mod_ready, 2)
            dve.scalar_tensor_tensor(scl1[:], modc[:, 1], 1.0, gain[:, 0].unsqueeze(2).broadcast_to([P, KC, 2]),
                                     ALU.add, ALU.mult).then_inc(mod_ready, 1)
            dve.wait_ge(mod_ready, 3)
            for c in range(KC):
                dve.wait_ge(hlat_raw, c + 1)
                dve.tensor_scalar(hT[:, c, NCTX:], hT[:, c, NCTX:], scl1[:, c, 0:1], modc[:, 0, c, 0:1],
                                  ALU.mult, ALU.add).then_inc(hlat_ready, 1)
            dve.wait_ge(late_in, 16 * NLATE)
            for i in range(2):
                last = dve.tensor_tensor_reduce(out=junk[:, i * HD:(i + 1) * HD], in0=lamv[:, 2 * i], in1=lamv[:, 2 * i + 1],
                                                scale=1.0, scalar=0.0, op0=ALU.mult, op1=ALU.add,
                                                accum_out=lam[:, i:i + 1])
            last.then_inc(lam_sum, 1)
            dve.wait_ge(bd_done, 1)
            dve.tensor_copy(bd.rearrange("p j s n -> p (j s n)"), ps[:, 7]).then_inc(bd_ready, 1)
            dve.wait_ge(lam_exp, 1)
            dve.scalar_tensor_tensor(lam[:, 4:5], lam[:, 3:4], -LAM0, lam[:, 2:3], ALU.add, ALU.subtract)
            dve.tensor_scalar(gsub[:, 1:2], gsub[:, 0:1], 1.0 - LAM0, None, ALU.mult).then_inc(setup, 1)
            for step in plan_proj["dve"]:
                step(dve)
            for t in range(1, NT, 2):
                dve.wait_ge(g_done, t + 1)
                dve.tensor_copy(fg[:, t].rearrange("p j s n -> p (j s n)"), ps[:, t]).then_inc(g_ready, 1)
            for m in range(2, 4):
                modulation_out(m)

            N_LINK = 2

            def alink(ins, n, k):
                ins.then_inc(dve_step, 1)
                dve.wait_ge(dve_step, att0 + k + 1 + n * N_LINK)

            att0 = steps[0]

            def at_evac(n, qt):
                dve.wait_ge(at_done, n + 1)
                dve.tensor_copy(aT[:, qt % 2, 512:768], ps[:, 5, 0:256]).then_inc(at_out[1], 1)

            def dve_unit(h, u):
                n = h * NT + u
                first = isinstance(h, int) and h == 0
                st = stat[:, u]
                for m in range(2):
                    dve.wait_ge(s_done[m], n + 1)
                    dve.tensor_reduce(st[:, m:m + 1], psf[:, 1024 * m:1024 * m + NTOK], AX, ALU.max, negate=True)\
                       .then_inc(nmax[m], 1)
                    if m == 0 and (not first or u >= 2):
                        at_evac(n - 2, (u - 2) % 4)
                dve.wait_ge(exped[0], n + 1)
                dve.wait_ge(exped[1], n + 1)
                alink(dve.reciprocal(st[:, 4:6], st[:, 2:4]), n, 0)
                alink(dve.scalar_tensor_tensor(st[:, 6:7], st[:, 2:3], lam[:, 4:5], st[:, 5:6], ALU.mult, ALU.mult), n, 1)
                dve.scalar_tensor_tensor(prob[:, u % 2, 0], prob[:, u % 2, 1], st[:, 6:7], prob[:, u % 2, 0],
                                         ALU.mult, ALU.add).then_inc(combined, 1)

            dve.wait_ge(setup, 1)
            for u in range(NT):
                dve_unit(0, u)
            with dve.Fori(1, HEADS) as h:
                for u in range(NT):
                    dve_unit(h, u)
            steps[0] += N_LINK * UNITS
            at_evac(UNITS - 2, 2)
            at_evac(UNITS - 1, 3)
            for m in range(4, 6):
                modulation_out(m)
            dve.wait_ge(mod_ready, 7)
            dve.tensor_tensor(rowc[:, 0], modc[:, 2, :, 0], gain[:, 1], ALU.mult)
            dve.scalar_tensor_tensor(rowc[:, 1], modc[:, 4, :, 0], 1.0, gain[:, 2], ALU.add, ALU.mult)
            dve.tensor_copy(rowc[:, 2], modc[:, 3, :, 0])
            dve.tensor_tensor(rowc[:, 3], modc[:, 5, :, 0], gain[:, 3], ALU.mult).then_inc(rowc_ready, 1)

            for i in range(1, 8, 2):
                dve.wait_ge(row_done, i + 1)
                row_dst = (grow[:, 0], srow[:, 0], srow[:, 1], grow[:, 1])[i // 2]
                dve.tensor_copy(row_dst.rearrange("p (j c) -> p c j", c=KC)[:, 4:8],
                                ps[:, 5].rearrange("p (c j) -> p c j", c=4)).then_inc(row_out[1], 1)
            for half in range(2):
                dve.wait_ge(row_out[half], 4)

            def h2t_evac(t):
                dve.wait_ge(h2t_done, t + 1)
                dve.tensor_copy(hT2[:, 4:8, t * P:(t + 1) * P], ps[:, 5].rearrange("p (c n) -> p c n", c=4))\
                   .then_inc(h2t_dve, 1)

            for t in range(NT):
                b = 2 * (t % 2)
                dve.wait_ge(y_rms, t + 1)
                if t:
                    dve.wait_ge(x1_ready, t)
                dve.scalar_tensor_tensor(tmp1, psf[:, b * 512:b * 512 + D], nrm[:, 2, 6 + t:7 + t], grow[:, 0],
                                         ALU.mult, ALU.mult).then_inc(y_scaled, 1)
                dve.wait_ge(y_scaled, t + 1)
                dve.tensor_tensor(xres[:, t], xres[:, t], tmp1, ALU.add).then_inc(x1_ready, 1)
                dve.wait_ge(x1_rms, t + 1)
                if t >= 2:
                    dve.wait_ge(h2_stored[t % 2], 16 * (t // 2))
                    dve.wait_ge(h2t_done, t - 1)
                dve.scalar_tensor_tensor(h2[:, t % 2], xres[:, t], nrm[:, 2, 10 + t:11 + t], srow[:, 0],
                                         ALU.mult, ALU.mult).then_inc(h_scaled, 1)
                if t >= 2:
                    h2t_evac(t - 2)
            h2t_evac(NT - 2)
            h2t_evac(NT - 1)

            sc = rt[:, 0:256]
            mask = rt[:, 256:512]
            sel, selm, selr, wn, sslot = (rt[:, 512 + 256 * i:768 + 256 * i] for i in range(5))
            t4 = lambda v: v.rearrange("p (t e) -> p t e", t=NT)
            t48 = lambda v: v.rearrange("p (t g e) -> p t g e", t=NT, g=NGRP)
            scratch = qreg[:, D:4 * D]
            m8 = scratch[:, 2048:2304].rearrange("p (t g k) -> p t g k", t=NT, g=NGRP)
            cmp1, cmp2 = scratch[:, 2304:2560], scratch[:, 2560:2816]
            v8, idx = scratch[:, 2816:2848], scratch[:, 2848:2880].bitcast(U32)
            ovf = freg[:, 0:512]
            nb, bend, base = (ovf[:, 64 * i:64 * i + 64] for i in range(3))
            small = ovf[:, 192:256]
            ints = freg[:, 256:384].bitcast(I32)
            intl = freg[:, 384:416].bitcast(I32)
            cmp3 = freg[:, 416:480]
            for s in h2_stored:
                dve.wait_ge(s, 16 * NT // 2)
            dve.wait_ge(h2t_done, NT)
            dve.wait_ge(scores_turned, 1)
            turned = ps[:, 7, 256:512].rearrange("p (j h e) -> p h j e", j=2, h=2)
            dve.tensor_tensor(sel.rearrange("p (h j e) -> p h j e", h=2, j=2), turned,
                              rbias[:].unsqueeze(1).unsqueeze(1).broadcast_to([P, 2, 2, NE]), ALU.add)
            link(dve.tensor_copy(sc.rearrange("p (h j e) -> p h j e", h=2, j=2), turned))
            for t in range(NT):
                for g in range(NGRP):
                    last = dve.max(out=m8[:, t, g], in_=sel[:, t * NE + g * GE:t * NE + (g + 1) * GE])
            link(last)
            g3 = gsum.rearrange("p (t g) -> p t g", t=NT)
            link(dve.tensor_tensor(g3, m8[:, :, :, 0], m8[:, :, :, 1], ALU.add))
            other = g3.unsqueeze(2).broadcast_to([P, NT, NGRP, NGRP])
            own = g3.unsqueeze(3).broadcast_to([P, NT, NGRP, NGRP])
            dve.tensor_tensor(t48(cmp1), other, own, ALU.is_gt)
            link(dve.tensor_tensor(t48(cmp2), other, own, ALU.is_equal))
            earlier = const[:, C_LT:C_LT + 64].unsqueeze(1).broadcast_to([P, NT, 64])
            link(dve.tensor_tensor(t4(cmp2), t4(cmp2), earlier, ALU.mult))
            link(dve.tensor_tensor(cmp1, cmp1, cmp2, ALU.add))
            link(dve.tensor_reduce(rank, cmp1.rearrange("p (g k) -> p g k", k=NGRP), AX, ALU.add))
            link(dve.tensor_scalar(rank, rank, float(TOPG), -1e30, ALU.is_ge, ALU.mult))
            link(dve.tensor_tensor(selm.rearrange("p (g e) -> p g e", e=GE), sel.rearrange("p (g e) -> p g e", e=GE),
                                   rank.unsqueeze(2).broadcast_to([P, NT * NGRP, GE]), ALU.add))
            for t in range(NT):
                last = dve.max(out=v8[:, 8 * t:8 * t + 8], in_=selm[:, t * NE:(t + 1) * NE])
            link(last)
            for t in range(NT):
                dve.max_index(idx[:, 8 * t:8 * t + 8], v8[:, 8 * t:8 * t + 8], selm[:, t * NE:(t + 1) * NE])
            for t in range(NT):
                last = dve.match_replace(selr[:, t * NE:(t + 1) * NE], v8[:, 8 * t:8 * t + 8],
                                         selm[:, t * NE:(t + 1) * NE], -3e38)
            link(last)
            dve.tensor_tensor(mask, selm, selr, ALU.not_equal).then_inc(mask_ready, 1)
            dve.tensor_copy(idxf, idx)
            dve.wait_ge(mask_ready, 1)
            link(dve.tensor_tensor(selr, sc, mask, ALU.mult))
            link(dve.tensor_reduce(small[:, 0:4], t4(selr), AX, ALU.add))
            link(dve.tensor_scalar(small[:, 4:8], small[:, 0:4], 1e-20, None, ALU.add))
            link(dve.reciprocal(small[:, 8:12], small[:, 4:8]))
            link(dve.tensor_scalar(small[:, 12:16], small[:, 8:12], ROUTED_SCALE, None, ALU.mult))
            link(dve.tensor_tensor(t4(wn), t4(selr), small[:, 12:16].unsqueeze(2).broadcast_to([P, NT, NE]), ALU.mult))

            pick = scratch[:, 0:NT * TOPK * NE].rearrange("p (i e) -> p i e", e=NE)

            def pick_chosen(table_, out):
                for i in range(NT * TOPK):
                    t = i // TOPK
                    last = dve.scalar_tensor_tensor(pick[:, i], iota[:, 0:NE], idxf[:, i:i + 1],
                                                    table_[:, t * NE:(t + 1) * NE], ALU.is_equal, ALU.mult,
                                                    accum_out=out[:, i:i + 1])
                link(last)

            pick_chosen(wn, wkf)
            dve.wait_ge(pos_done, 1)
            link(dve.tensor_scalar(nb, ps[:, 5, 0:NE], float(P), 1.0, ALU.is_gt, ALU.add))
            link(dve.scalar_tensor_tensor(nb, ps[:, 5, 0:NE], float(2 * P), nb, ALU.is_gt, ALU.add))
            link(dve.scalar_tensor_tensor(nb, ps[:, 5, 0:NE], float(3 * P), nb, ALU.is_gt, ALU.add))
            lane = lambda v, u: v.rearrange("p (j u) -> p u j", u=U)[:, u]
            for u in range(U):
                last = dve.tensor_tensor_scan(lane(bend, u), ones[:, 0:NE // U], lane(nb, u), 0.0, ALU.mult, ALU.add)
            link(last)
            link(dve.tensor_tensor(base, bend, nb, ALU.subtract))
            pos = ps[:, 4, 0:256]
            link(dve.scalar_tensor_tensor(t4(sslot), base.unsqueeze(1).broadcast_to([P, NT, NE]), 1024.0, t4(pos),
                                          ALU.mult, ALU.add))
            pick_chosen(sslot, skf)
            link(dve.tensor_copy(ints[:, 0:32], skf))
            dve.tensor_scalar(ints[:, 32:64], ints[:, 0:32], P - 1, None, ALU.bitwise_and)
            dve.tensor_scalar(intl, idx.bitcast(I32), U - 1, None, ALU.bitwise_and)
            dve.tensor_scalar(ints[:, 96:128], ints[:, 0:32], 8, 256 - U, ALU.logical_shift_right, ALU.bitwise_and)
            link(dve.tensor_scalar(ints[:, 64:96], ints[:, 0:32], 5, 7 * U, ALU.logical_shift_right, ALU.bitwise_and))
            link(dve.tensor_tensor(intl, intl, ints[:, 96:128], ALU.bitwise_or))
            dve.tensor_copy(pf, ints[:, 32:64])
            dve.tensor_tensor(bf, intl, ints[:, 64:96], ALU.add).then_inc(place_ready, 1)
            dve.wait_ge(place_ready, 1)
            for t in range(NT):
                if t >= 2:
                    dve.wait_ge(hot_used, t - 1)
                elif t == 1:
                    dve.wait_ge(sgu_done, NT)
                _, bvw = hot(t)
                for k in range(TOPK):
                    i = t * TOPK + k
                    dve.tensor_scalar(bvw[:, k, 0:NB], iota[:, 0:NB], bf[:, i:i + 1], const[:, C_V + i:C_V + i + 1],
                                      ALU.is_equal, ALU.mult)
                    last = dve.tensor_scalar(bvw[:, k, NB:2 * NB], iota[:, 0:NB], bf[:, i:i + 1], wkf[:, i:i + 1],
                                             ALU.is_equal, ALU.mult)
                last.then_inc(hot_ready, 1)
            link(dve.tensor_scalar(cmp3, bend, const[:, C_ROW:C_ROW + 1], None, ALU.is_le))
            link(dve.tensor_reduce(small[:, 32:32 + U], cmp3.rearrange("p (j u) -> p u j", u=U), AX, ALU.add))
            link(dve.tensor_reduce(small[0:1, 43:44], bend[0:1, NE - U:NE], AX, ALU.max))
            dve.tensor_scalar(small[0:1, 40:41], small[0:1, 43:44], -1.0, None, ALU.add)
            dve.tensor_scalar(small[0:1, 41:42], small[0:1, 43:44], 32.0 * U // 2, None, ALU.mult)
            link(dve.tensor_scalar(small[0:1, 42:43], small[0:1, 43:44], 16.0, None, ALU.mult))
            link(dve.tensor_copy(steer[:, NB:NB + 3], small[0:1, 40:43]))
            slots_flat = slots.rearrange("p b k -> p (b k)")

            def take_tokens(b, u):
                dve.tensor_copy(take[:, u:u + 1], slots_flat[:, at(b * 5, 1)]).then_inc(take_ready, 1)

            dve.wait_ge(hot_used, NT)
            dve.tensor_copy(table, ps[:, 7, 0:2 * NB]).then_inc(table_copied, 1)
            dve.wait_ge(table_copied, 1)
            emp, rowf = freg[:, 512:512 + NB], freg[:, 704:704 + NB]
            emp2, rowf2 = (freg[:, 896 + 384 * i:896 + 384 * i + 2 * NB].rearrange("p (a n) -> p a n", a=2) for i in range(2))
            link(dve.tensor_scalar(emp, table[:, 0:NB], 0.0, SKIP, ALU.is_equal, ALU.mult))
            link(dve.scalar_tensor_tensor(rowf, table[:, 0:NB], -1.0, emp, ALU.add, ALU.add))
            rowi = freg[:, 1664:1664 + NB].bitcast(I32)
            link(dve.tensor_copy(rowi, rowf))
            link(dve.tensor_scalar(slots[:, :, 0], rowi, 3, None, ALU.logical_shift_right))
            for u in range(U - 1):
                take_tokens(u, u)
            dve.wait_ge(table_spread, 1)
            tv, tw = ps[:, 4:6, 0:NB], ps[:, 4:6, NB:2 * NB]
            e2 = freg[0:1, 1856:1856 + NB]
            link(dve.tensor_scalar(e2, ps[0:1, 0, NB:2 * NB], float(NE // U - 1), 2.0, ALU.min, ALU.mult))
            by_lane = lambda v: v.rearrange("p (u t) -> p u t", u=U)
            dve.scalar_tensor_tensor(by_lane(steer[:, 0:NB]), ps[0:1, 0, 0:NB].rearrange("p (t u) -> p u t", u=U), 0.0,
                                     by_lane(e2), ALU.is_gt, ALU.add).then_inc(steer_ready, 1)
            dve.tensor_copy(slots.bitcast(F32)[:, :, 3:5].rearrange("p b a -> p a b"), tw)
            link(dve.tensor_scalar(emp2, tv, 0.0, SKIP, ALU.is_equal, ALU.mult))
            link(dve.scalar_tensor_tensor(rowf2, tv, 2.0, emp2, ALU.mult, ALU.add))
            dve.tensor_scalar(slots[:, :, 1:3].rearrange("p b a -> p a b"), rowf2, const[:, C_MAP + 1:C_MAP + 2], -2.0,
                              ALU.add, ALU.add).then_inc(slots_ready, 1)
            dve.wait_ge(slots_ready, 1)

            def take_rows(g, u):
                need(dve, y_out[u % 2], g * (32 * U // 2) + 32 * ((u - 4) // 2 + 1))
                dve.tensor_copy(put[:, u], slots_flat[:, at((g * U + u) * 5 + 1, 4)]).then_inc(put_ready, 1)


            def x_evac(n, s):
                dve.wait_ge(xt_done, n + 1)
                dve.tensor_copy(xgT[:, s, 4:8], ps[:, 5].rearrange("p (c n) -> p c n", c=4)).then_inc(xt_dve, 1)

            def dve_block(g, u):
                b = g * U + u
                first = isinstance(g, int) and b == 0
                take_tokens(b + 3, (u + 3) % U)
                take_rows(g, u)
                dve.wait_ge(gate_ready, b + 1)
                two = lambda v: v.rearrange("p (a n) -> p a n", a=2)
                dve.tensor_tensor(two(hmid[:, u % 2]), halves(u % 2)[:, :, 1], two(gsil[:, u % 2]), ALU.mult)\
                    .then_inc(mid_ready, 1)
                x_evac(b + 1, (u + 1) % 2)
                if not first:
                    y_evac(g, u)

            def y_evac(g, u):
                dve.wait_ge(dn_done, g * U + u)
                need(dve, y_out[(u - 1) % 2], done_scatters(g, u))
                dve.wait_ge(put_ready, g * U + u)
                w = put[:, (u - 1) % U, 3:4].bitcast(F32)
                dve.tensor_scalar(yb[:, (u - 1) % 2, 512:1024], ps[:, 3], w, None, ALU.mult).then_inc(y_dve, 1)

            x_evac(0, 0)
            for u in range(U):
                dve_block(0, u)
            dve.wait_ge(steer_ready, 1)
            turns = dve.value_load(steer[0:1, NB:NB + 1], min_val=0, max_val=TURNS - 1) + 1
            with dve.Fori(0, SPANS) as q:
                with dve.If(q * SPAN + 1 < turns):
                    with dve.Fori(1, SPAN + 1) as i:
                        g = (q * SPAN + i).with_bounds(min_val=1, max_val=TURNS - 1)
                        with dve.If(g < turns):
                            for u in range(U):
                                dve_block(g, u)
            y_evac(turns, 0)

            def gate_half(t):
                dve.wait_ge(r_rms, t + 1)
                link(dve.scalar_tensor_tensor(dve_part(shy, t), dve_part(shy, t), nrm[:, 2, 14 + t:15 + t],
                                              dve_part(grow, 1), ALU.mult, ALU.mult))
                dve.tensor_tensor(dve_part(shy, t), dve_part(shy, t), dve_part(xres, t), ALU.add).then_inc(r_fin[1], 1)

            for c in range(2 * NT):
                dve.wait_ge(r_in[c], 16)
                if c >= 2:
                    dve.wait_ge(r_sum, c - 1)
                dve.tensor_reduce(rsum(c), ranks(c).rearrange("p k n -> p n k"), AX, ALU.add).then_inc(r_red, 1)
                if c % 2 == 0 and c:
                    gate_half(c // 2 - 1)
            gate_half(NT - 1)

        @block.gpsimd
        def _(pool):
            steps = [0]

            def link(ins):
                steps[0] += 1
                ins.then_inc(pool_step, 1)
                pool.wait_ge(pool_step, steps[0])

            link(pool.memset(mhalf[:], -0.5))

            def rms(i, ready):
                link(pool.tensor_scalar(nrm[:, 1, i:i + 1], nrm[:, 0, i:i + 1], 1.0 / D, EPS, ALU.mult, ALU.add))
                pool.tensor_tensor(nrm[:, 2, i:i + 1], nrm[:, 1, i:i + 1], mhalf[:], ALU.pow).then_inc(ready, 1)

            for t in range(NCT + NT):
                pool.wait_ge(squares, t + 1)
                rms(t, rms_ready)
            for step in plan_proj["pool"]:
                step(pool)

            def stage_q(n, h, qt):
                need(pool, s_done[1], n - 1)
                pool.tensor_tensor(qz[:, qt % 2], qT[:, at(h * NLAT + qt * P, P)].unsqueeze(1).broadcast_to([P, 2, P]),
                                   const[:, C_MAP:C_MAP + 2].unsqueeze(2).broadcast_to([P, 2, P]), ALU.mult)\
                    .then_inc(q_staged, 1)

            def o_rms_(n, qt):
                pool.wait_ge(o_square, n + 1)
                pool.sem_inc(pool_tick, 1)
                pool.tensor_scalar(stat[:, qt, 8:9], stat[:, qt, 7:8], 1.0 / VD, EPS, ALU.mult, ALU.add)\
                    .then_inc(pool_step, 1)
                pool.wait_ge(pool_step, n + (att0 + 1))
                pool.tensor_tensor(stat[:, qt, 9:10], stat[:, qt, 8:9], mhalf[:], ALU.pow).then_inc(o_rms, 1)
                pool.wait_ge(o_rms, n + 1)
                pool.tensor_tensor(onrm[:, qt % 2], osb[:, qt % 2], stat[:, qt, 9:10].broadcast_to([P, P]), ALU.mult)\
                    .then_inc(o_normed, 1)

            att0 = steps[0]
            pool.wait_ge(g_done, NT)
            pool.wait_ge(turn_out, sum(1 for x in plan_proj["pe"] if x))
            stage_q(0, 0, 0)

            def pool_unit(h, u, last=False):
                n = h * NT + u
                first = isinstance(h, int) and h == 0
                if not last:
                    stage_q(n + 1, h + (1 if u == NT - 1 else 0), (u + 1) % NT)
                if not first or u >= 3:
                    o_rms_(n - 3, (u - 3) % 4)

            for u in range(NT):
                pool_unit(0, u)
            with pool.Fori(1, HEADS - 1) as h:
                for u in range(NT):
                    pool_unit(h, u)
            for u in range(NT):
                pool_unit(HEADS - 1, u, last=(u == NT - 1))
            o_rms_(UNITS - 3, 1)
            o_rms_(UNITS - 2, 2)
            o_rms_(UNITS - 1, 3)
            steps[0] += UNITS
            for t in range(NT):
                pool.wait_ge(y_square, t + 1)
                rms(6 + t, y_rms)
                pool.wait_ge(x1_square, t + 1)
                rms(10 + t, x1_rms)
                pool.wait_ge(h_scaled, t + 1)
                pool.tensor_tensor(h2[:, t % 2], h2[:, t % 2], srow[:, 1], ALU.add).then_inc(h2_ready, 1)

            def shared_mid(t):
                pool.wait_ge(s_up, t + 1)
                pool.wait_ge(s_gate, t + 1)
                pool.tensor_tensor(smid[:, t], gsil[:, t % 2], sreg[:, 1024 + (t % 2) * DE:1024 + (t % 2) * DE + DE],
                                   ALU.mult).then_inc(s_mid, 1)

            def place_rows(t):
                if t >= 2:
                    pool.wait_ge(hot_used, t - 1)
                elif t == 1:
                    pool.wait_ge(sgu_done, NT)
                ph, _ = hot(t)
                for k in range(TOPK):
                    last = pool.tensor_scalar(ph[:, k], iota[:, 0:P], pf[:, t * TOPK + k:t * TOPK + k + 1], None, ALU.is_equal)
                last.then_inc(places, 1)

            shared_mid(0)
            shared_mid(1)
            pool.wait_ge(h2t_done, NT)
            pool.memset(hreg[:, 4096:6144], 0.0).then_inc(xg_zero, 1)
            pool.wait_ge(xg_zero, 1)
            shared_mid(2)
            pool.wait_ge(place_ready, 1)
            place_rows(0)
            place_rows(1)
            shared_mid(3)
            place_rows(2)
            place_rows(3)

            def code_of(g, lane):
                return pool.value_load(steer[0:1, at(lane * (NB // U) + g, 1)], min_val=0, max_val=2 * (NE // U) - 1)

            def gather(b, u, code):
                pool.wait_ge(take_ready, b + 1)
                pool.sem_inc(pool_tick, 1)
                rows = lambda n: pool.indirect_dma_start(
                    xg[u % U][0:n], None, h2_dram[:], bass.IndirectOffsetOnAxis(take[0:n, u % U:u % U + 1], 0),
                    bounds_check=NLAT - 1, oob_is_err=False).then_inc(xg_in[u % U], 16)
                if code is None:
                    rows(P)
                else:
                    with pool.If((code & 1) > 0):
                        rows(P)
                    with pool.If((code & 1) < 1):
                        rows(P // 2)

            def pool_block(g, u):
                b = g * U + u
                first = isinstance(g, int) and b == 0
                ahead = code_of(g + (u + 3) // U, (u + 3) % U)
                if not first:
                    before = code_of(g if u else g - 1, (u - 1) % U)
                need(pool, xt_done, b)
                gather(b + 3, u + 3, ahead)
                if not first:
                    scatter(b, u, before)

            def scatter(b, u, code):
                pool.wait_ge(put_ready, b)
                pool.wait_ge(y_act, b)
                pool.wait_ge(y_dve, b)
                pool.sem_inc(pool_tick, 1)
                rows = lambda a, n: pool.indirect_dma_start(
                    y_dram.rearrange("r (f n) -> (r f) n", f=2),
                    bass.IndirectOffsetOnAxis(put[0:n, (u - 1) % U, a:1 + a], 0),
                    yb[0:n, (u - 1) % 2, 512 * a:512 * a + 512], None,
                    bounds_check=2 * NLAT * TOPK - 1, oob_is_err=False).then_inc(y_out[(u - 1) % 2], 16)
                rows(0, P)
                with pool.If((code & 1) > 0):
                    rows(1, P)
                with pool.If((code & 1) < 1):
                    rows(1, 2)

            for s in h2_stored:
                pool.wait_ge(s, 16 * NT // 2)
            for u in range(U - 1):
                gather(u, u, None)
            pool.wait_ge(steer_ready, 1)
            for u in range(U):
                pool_block(0, u)
            pool.wait_ge(steer_ready, 1)
            turns = pool.value_load(steer[0:1, NB:NB + 1], min_val=0, max_val=TURNS - 1) + 1
            with pool.Fori(0, SPANS) as q:
                with pool.If(q * SPAN + 1 < turns):
                    with pool.Fori(1, SPAN + 1) as i:
                        g = (q * SPAN + i).with_bounds(min_val=1, max_val=TURNS - 1)
                        with pool.If(g < turns):
                            for u in range(U):
                                pool_block(g, u)
            scatter(turns * U, 0, code_of(turns - 1, U - 1))
            counts = [pool.value_load(steer[0:1, NB + 1 + i:NB + 2 + i], min_val=0, max_val=16 * U * TURNS)
                      for i in range(2)]
            for x in y_out:
                pool.wait_ge(x, counts[0])
            for u in range(U):
                pool.wait_ge(xg_in[u], counts[1] + (16 if u < U - 1 else 0))
            pool.sem_inc(moe_done, 1)
            for t in range(NT):
                pool.wait_ge(sy_out, t + 1)
                for h in range(2):
                    pool.wait_ge(r_red, 2 * t + h + 1)
                    pool.tensor_tensor(part(t, h), part(t, h), rsum(2 * t + h), ALU.add).then_inc(r_sum, 1)
                pool.wait_ge(r_square, t + 1)
                rms(14 + t, r_rms)
                pool.wait_ge(r_scaled, t + 1)
                pool.tensor_tensor(pool_part(shy, t), pool_part(shy, t), pool_part(grow, 1), ALU.mult).then_inc(r_gated, 1)
                pool.wait_ge(r_gated, t + 1)
                pool.tensor_tensor(pool_part(shy, t), pool_part(shy, t), pool_part(xres, t), ALU.add)\
                    .then_inc(r_fin[0], 1)


_OUT = ((1, NLAT, D), "float32")


def shape_tables():
    import numpy as np

    c = np.zeros((P, C_ALL), np.float32)
    p = np.arange(P)
    c[:, C_ID:C_ID + P] = np.eye(P)
    c[:, C_TRI:C_TRI + P] = p[:, None] < p[None, :]
    c[:, C_IOTA:C_IOTA + NB] = np.arange(NB)
    c[:, C_ROW] = p
    g = np.arange(NGRP)
    c[:, C_LT:C_LT + 64] = (g[None, :] < g[:, None]).reshape(1, 64)
    t, k = np.arange(NT), np.arange(TOPK)
    c[:, C_V:C_V + 32] = ((t[None, :, None] * P + p[:, None, None]) * TOPK + k[None, None, :] + 1).reshape(P, 32)
    c[0:64, C_MAP], c[64:128, C_MAP + 1] = 1.0, 1.0
    j = np.arange(64)
    ang = 2 * np.pi * (np.outer(j, j) % 64) / 64
    for h in range(2):
        s = slice(64 * h, 64 * h + 64)
        c[s, C_CC + 64 * h:C_CC + 64 * h + 64] = np.cos(ang) / 8
        c[s, C_SC + 64 * h:C_SC + 64 * h + 64] = -np.sin(ang) / 8
    n = np.arange(NLAT)
    ang = 2 * np.pi * (np.outer(n, n) % NLAT) / NLAT
    d = np.stack([np.cos(ang), np.sin(ang)]) / np.sqrt(NLAT)
    dft = d.reshape(2, NT, P, NLAT).transpose(2, 0, 1, 3).reshape(P, 2 * NT * NLAT).astype(np.float32)
    inv = (10000.0 ** (-np.arange(0, 32, 2, dtype=np.float32) / np.float32(32))).astype(np.float32)
    pos = np.stack([n // 64, n % 64], -1).astype(np.float32)
    ang = (pos[:, :, None] * inv).astype(np.float32)
    cos, sin = np.cos(ang), np.sin(ang)
    rope = np.stack([np.stack([cos, cos], 2).reshape(NLAT, HD), np.stack([-sin, sin], 2).reshape(NLAT, HD)], 1)
    return {"consts": c, "dft": dft, "rope": rope.astype(np.float32)}


def kernel(**inputs):
    import numpy as np
    import concourse.bacc as bacc
    from concourse.bass_utils import run_bass_kernel_spmd

    nc = bacc.Bacc("TRN2", target_bir_lowering=False, num_devices=1)
    arrays, args = {}, {}
    for name, a in {**inputs, **shape_tables()}.items():
        a = np.ascontiguousarray(a)
        arrays[f"in_{name}"] = a
        args[name] = nc.dram_tensor(f"in_{name}", a.shape, mybir.dt.from_np(a.dtype), kind="ExternalInput").ap()
    args["out"] = nc.dram_tensor("out_x", _OUT[0], F32, kind="ExternalOutput").ap()
    build(nc, args)
    r = run_bass_kernel_spmd(nc, [arrays], core_ids=[0])
    return r.results[0]["out_x"]
```
